# Optimizing a Trainium2 kernel written in Bass

```python
import math
import jax, jax.numpy as jnp
from jax import lax
import numpy as np

D_MODEL = 1024
BATCH = 1
SEQ = 256
DEPTH = 2

N_A = DEPTH // 2
N_B = DEPTH - N_A

H_A = 16
NOPE_A = 64
ROPE_A = 32
V_A = 64
Q_LORA = 768
KV_LORA = 256
WIDTH_A = H_A * V_A
QBLOCK = 128

H_B = 16
HD_B = 64
WIDTH_B = H_B * HD_B
MOBA_BLOCK = 256
MOBA_TOPK = 3
QCHUNK = 8

THETA = 10000.0
LN_EPS = 1e-5
RMS_EPS = 1e-6
ALPHA = (2 * DEPTH) ** 0.25
BETA = (8 * DEPTH) ** (-0.25)


def rope_tables(seq, dim):
    inv = THETA ** (-jnp.arange(0, dim, 2, dtype=jnp.float32) / dim)
    ang = jnp.arange(seq, dtype=jnp.float32)[:, None] * inv[None, :]
    ang = jnp.concatenate([ang, ang], axis=-1)
    return jnp.cos(ang), jnp.sin(ang)

def apply_rope(x, cos, sin):
    x1, x2 = jnp.split(x, 2, axis=-1)
    rot = jnp.concatenate([-x2, x1], axis=-1)
    return (x * cos + rot * sin).astype(x.dtype)

def layer_norm(x, g, b):
    xf = x.astype(jnp.float32)
    mu = jnp.mean(xf, axis=-1, keepdims=True)
    var = jnp.mean(jnp.square(xf - mu), axis=-1, keepdims=True)
    return ((xf - mu) * lax.rsqrt(var + LN_EPS) * g + b).astype(x.dtype)

def rms_norm(x, g):
    xf = x.astype(jnp.float32)
    return (xf * lax.rsqrt(jnp.mean(jnp.square(xf), axis=-1, keepdims=True) + RMS_EPS) * g).astype(x.dtype)

def mla_mixer(x, w_in, q_norm, kv_norm, w_uq, w_ukv, w_o, cos, sin):
    B, S, _ = x.shape
    h = x @ w_in
    c_q, c_kv, k_rope, gate = jnp.split(h, [Q_LORA, Q_LORA + KV_LORA, Q_LORA + KV_LORA + ROPE_A], axis=-1)
    q = (rms_norm(c_q, q_norm) @ w_uq).reshape(B, S, H_A, NOPE_A + ROPE_A)
    q_nope = q[..., :NOPE_A]
    q_rope = apply_rope(q[..., NOPE_A:], cos[None, :, None, :], sin[None, :, None, :])
    kv = (rms_norm(c_kv, kv_norm) @ w_ukv).reshape(B, S, H_A, NOPE_A + V_A)
    k_nope, v = kv[..., :NOPE_A], kv[..., NOPE_A:]
    k_rope = apply_rope(k_rope, cos[None], sin[None])
    scale = (NOPE_A + ROPE_A) ** -0.5
    outs = []
    for i in range(S // QBLOCK):
        q0, kend = i * QBLOCK, (i + 1) * QBLOCK
        s = (jnp.einsum('bqhd,bkhd->bhqk', q_nope[:, q0:kend], k_nope[:, :kend])
             + jnp.einsum('bqhr,bkr->bhqk', q_rope[:, q0:kend], k_rope[:, :kend])).astype(jnp.float32) * scale
        q_pos = q0 + jnp.arange(QBLOCK)
        mask = jnp.arange(kend)[None, :] <= q_pos[:, None]
        p = jax.nn.softmax(jnp.where(mask, s, -jnp.inf), axis=-1).astype(v.dtype)
        outs.append(jnp.einsum('bhqk,bkhd->bqhd', p, v[:, :kend]))
    o = jnp.concatenate(outs, axis=1).reshape(B, S, WIDTH_A)
    return (o * jax.nn.silu(gate)) @ w_o

def moba_shared_kv(x, w_kv, cos, sin):
    B, S, _ = x.shape
    kv = x @ w_kv
    k = kv[..., :WIDTH_B].reshape(B, S, H_B, HD_B)
    v = kv[..., WIDTH_B:].reshape(B, S, H_B, HD_B)
    k = apply_rope(k, cos[None, :, None, :], sin[None, :, None, :])
    nb = -(-S // MOBA_BLOCK)
    pad = nb * MOBA_BLOCK - S
    k = jnp.pad(k, ((0, 0), (0, pad), (0, 0), (0, 0)))
    v = jnp.pad(v, ((0, 0), (0, pad), (0, 0), (0, 0)))
    k_blocks = k.reshape(B, nb, MOBA_BLOCK, H_B, HD_B).transpose(0, 3, 1, 2, 4)
    v_blocks = v.reshape(B, nb, MOBA_BLOCK, H_B, HD_B).transpose(0, 3, 1, 2, 4)
    cnt = jnp.clip(S - jnp.arange(nb) * MOBA_BLOCK, 1, MOBA_BLOCK).astype(jnp.float32)
    k_mean = (jnp.sum(k_blocks.astype(jnp.float32), axis=3) / cnt[:, None]).astype(k.dtype)
    return k_blocks, v_blocks, k_mean

def moba_mixer(x, k_blocks, v_blocks, k_mean, w_in, w_o, cos, sin):
    B, S, _ = x.shape
    nb = k_blocks.shape[2]
    h = x @ w_in
    q, gate = h[..., :WIDTH_B], h[..., WIDTH_B:]
    q = apply_rope(q.reshape(B, S, H_B, HD_B), cos[None, :, None, :], sin[None, :, None, :])
    q = q.transpose(0, 2, 1, 3)
    gs = jnp.einsum('bhsd,bhnd->bhsn', q, k_mean).astype(jnp.float32)
    q_blk = jnp.arange(S) // MOBA_BLOCK
    past = jnp.arange(nb)[None, :] < q_blk[:, None]
    gs = jnp.where(past, gs, -jnp.inf)
    topk = min(MOBA_TOPK, nb)
    _, idx = lax.top_k(gs, topk)
    valid = idx < q_blk[:, None]
    n_chunks = S // QCHUNK
    q_c = q.reshape(B, H_B, n_chunks, QCHUNK, HD_B).transpose(2, 0, 1, 3, 4)
    idx_c = idx.reshape(B, H_B, n_chunks, QCHUNK, topk).transpose(2, 0, 1, 3, 4)
    valid_c = valid.reshape(B, H_B, n_chunks, QCHUNK, topk).transpose(2, 0, 1, 3, 4)
    starts = jnp.arange(n_chunks, dtype=jnp.int32) * QCHUNK
    b_ix = jnp.arange(B)[:, None, None, None]
    h_ix = jnp.arange(H_B)[None, :, None, None]
    scale = HD_B ** -0.5

    def attend(args):
        qq, ii, vv, start = args
        k_sel = k_blocks[b_ix, h_ix, ii]
        v_sel = v_blocks[b_ix, h_ix, ii]
        qb = start // MOBA_BLOCK
        k_own = lax.dynamic_index_in_dim(k_blocks, qb, axis=2, keepdims=False)
        v_own = lax.dynamic_index_in_dim(v_blocks, qb, axis=2, keepdims=False)
        s_sel = jnp.einsum('bhcd,bhctkd->bhctk', qq, k_sel).astype(jnp.float32) * scale
        s_sel = jnp.where(vv[..., None], s_sel, -jnp.inf).reshape(B, H_B, QCHUNK, topk * MOBA_BLOCK)
        s_own = jnp.einsum('bhcd,bhkd->bhck', qq, k_own).astype(jnp.float32) * scale
        k_pos = qb * MOBA_BLOCK + jnp.arange(MOBA_BLOCK)
        q_pos = start + jnp.arange(QCHUNK)
        s_own = jnp.where(k_pos[None, :] <= q_pos[:, None], s_own, -jnp.inf)
        p = jax.nn.softmax(jnp.concatenate([s_sel, s_own], axis=-1), axis=-1).astype(qq.dtype)
        p_sel = p[..., :topk * MOBA_BLOCK].reshape(B, H_B, QCHUNK, topk, MOBA_BLOCK)
        p_own = p[..., topk * MOBA_BLOCK:]
        return (jnp.einsum('bhctk,bhctkd->bhcd', p_sel, v_sel)
                + jnp.einsum('bhck,bhkd->bhcd', p_own, v_own))

    o = lax.map(attend, (q_c, idx_c, valid_c, starts))
    o = o.transpose(1, 0, 3, 2, 4).reshape(B, S, WIDTH_B)
    return (o * jax.nn.silu(gate)) @ w_o

def first_inputs(seed: int = 0) -> dict:
    key = jax.random.key(seed)
    ks = jax.random.split(key, 14)

    def nrm(k, shape, fan_in, scale=1.0):
        return jax.random.normal(k, shape, jnp.float32) * (scale * fan_in ** -0.5)

    x = jax.random.normal(ks[0], (BATCH, SEQ, D_MODEL), jnp.float32)
    mla_w_in = nrm(ks[1], (N_A, D_MODEL, Q_LORA + KV_LORA + ROPE_A + WIDTH_A), D_MODEL)
    mla_q_norm = 1.0 + 0.02 * jax.random.normal(ks[2], (N_A, Q_LORA), jnp.float32)
    mla_kv_norm = 1.0 + 0.02 * jax.random.normal(ks[3], (N_A, KV_LORA), jnp.float32)
    mla_w_uq = nrm(ks[4], (N_A, Q_LORA, H_A * (NOPE_A + ROPE_A)), Q_LORA)
    mla_w_ukv = nrm(ks[5], (N_A, KV_LORA, H_A * (NOPE_A + V_A)), KV_LORA)
    mla_w_o = nrm(ks[6], (N_A, WIDTH_A, D_MODEL), WIDTH_A, BETA)
    moba_w_kv = nrm(ks[7], (D_MODEL, 2 * WIDTH_B), D_MODEL)
    moba_w_in = nrm(ks[8], (N_B, D_MODEL, 2 * WIDTH_B), D_MODEL)
    moba_w_o = nrm(ks[9], (N_B, WIDTH_B, D_MODEL), WIDTH_B, BETA)
    ln_g = 1.0 + 0.02 * jax.random.normal(ks[10], (DEPTH, D_MODEL), jnp.float32)
    ln_b = 0.02 * jax.random.normal(ks[11], (DEPTH, D_MODEL), jnp.float32)
    return {"x": x, "mla_w_in": mla_w_in, "mla_q_norm": mla_q_norm, "mla_kv_norm": mla_kv_norm,
            "mla_w_uq": mla_w_uq, "mla_w_ukv": mla_w_ukv, "mla_w_o": mla_w_o,
            "moba_w_kv": moba_w_kv, "moba_w_in": moba_w_in, "moba_w_o": moba_w_o,
            "ln_g": ln_g, "ln_b": ln_b}

def first_block(x, mla_w_in, mla_q_norm, mla_kv_norm, mla_w_uq, mla_w_ukv, mla_w_o,
              moba_w_kv, moba_w_in, moba_w_o, ln_g, ln_b):
    S = x.shape[1]
    cos_a, sin_a = rope_tables(S, ROPE_A)
    cos_b, sin_b = rope_tables(S, HD_B)
    shared = None
    for layer in range(DEPTH):
        if layer < N_A:
            y = mla_mixer(x, mla_w_in[layer], mla_q_norm[layer], mla_kv_norm[layer],
                          mla_w_uq[layer], mla_w_ukv[layer], mla_w_o[layer], cos_a, sin_a)
        else:
            if shared is None:
                shared = moba_shared_kv(x, moba_w_kv, cos_b, sin_b)
            j = layer - N_A
            y = moba_mixer(x, shared[0], shared[1], shared[2], moba_w_in[j], moba_w_o[j], cos_b, sin_b)
        x = layer_norm(ALPHA * x + y, ln_g[layer], ln_b[layer])
    return x


DEPTH_2 = 1

EPS = 1e-6
GRID_W = 64
D_MIX = D_MODEL

GLA_HEADS = 4
GLA_DK = 64
GLA_DV = 128
GLA_KEY_WIDTH = GLA_HEADS * GLA_DK
GLA_WIDTH = GLA_HEADS * GLA_DV
GLA_GATE_RANK = 16
GLA_GATE_NORM = 16.0
GLA_CHUNK = 64

ATT_HEADS = 8
ATT_KV_HEADS = 2
ATT_HEAD_DIM = 64
ATT_WIDTH = ATT_HEADS * ATT_HEAD_DIM
ATT_KV_WIDTH = ATT_KV_HEADS * ATT_HEAD_DIM
Q_BLOCK = 128
ROPE_THETA = 10000.0

N_GROUPS = 8
EXPERTS_PER_GROUP = 8
N_EXPERTS = N_GROUPS * EXPERTS_PER_GROUP
TOP_K = 2
D_EXPERT = 512
MOE_BLOCK = 128

IN_SIZES = (GLA_KEY_WIDTH, GLA_KEY_WIDTH, GLA_WIDTH, GLA_WIDTH,
            GLA_GATE_RANK, GLA_GATE_RANK,
            ATT_WIDTH, ATT_KV_WIDTH, ATT_KV_WIDTH)
D_IN = 2336


def rms_norm_2(x, gain):
    x32 = x.astype(jnp.float32)
    y = x32 * lax.rsqrt(jnp.mean(x32 * x32, axis=-1, keepdims=True) + EPS)
    return y.astype(x.dtype) * gain

def gla_chunked(q, k, v, log_a):
    B, H, T, dk = q.shape
    dv = v.shape[-1]
    C = GLA_CHUNK
    N = T // C
    f32 = jnp.float32
    qf = q.astype(f32).reshape(B, H, N, C, dk)
    kf = k.astype(f32).reshape(B, H, N, C, dk)
    vf = v.astype(f32).reshape(B, H, N, C, dv)
    b = jnp.cumsum(log_a.astype(f32).reshape(B, H, N, C, dk), axis=3)
    b_ref = b[:, :, :, C // 2 - 1:C // 2, :]
    b_last = b[:, :, :, -1:, :]
    scores = jnp.einsum('bhncd,bhnsd->bhncs', qf * jnp.exp(b - b_ref), kf * jnp.exp(b_ref - b))
    mask = jnp.tril(jnp.ones((C, C), dtype=bool))
    scores = jnp.where(mask, scores, 0.0)
    o_intra = jnp.einsum('bhncs,bhnse->bhnce', scores, vf)
    chunk_kv = jnp.einsum('bhncd,bhnce->bhnde', kf * jnp.exp(b_last - b), vf)
    chunk_decay = jnp.exp(b_last[:, :, :, 0, :])

    def step(state, inp):
        decay, kv = inp
        return decay[..., None] * state + kv, state

    init = jnp.zeros((B, H, dk, dv), f32)
    _, states = lax.scan(step, init, (jnp.moveaxis(chunk_decay, 2, 0), jnp.moveaxis(chunk_kv, 2, 0)))
    states = jnp.moveaxis(states, 0, 2)
    o_inter = jnp.einsum('bhncd,bhnde->bhnce', qf * jnp.exp(b), states)
    return (o_intra + o_inter).reshape(B, H, T, dv).astype(v.dtype)

def gla_group(q, k, v, g, z_fwd, z_bwd, up_f, up_f_bias, up_b, up_b_bias, out_gain):
    B, T, _ = q.shape

    def heads(t, d):
        return t.reshape(B, T, GLA_HEADS, d).transpose(0, 2, 1, 3)

    qh = heads(q, GLA_DK) * (GLA_DK ** -0.5)
    kh = heads(k, GLA_DK)
    vh = heads(v, GLA_DV)
    la_f = heads(jax.nn.log_sigmoid((z_fwd @ up_f + up_f_bias).astype(jnp.float32)) / GLA_GATE_NORM, GLA_DK)
    la_b = heads(jax.nn.log_sigmoid((z_bwd @ up_b + up_b_bias).astype(jnp.float32)) / GLA_GATE_NORM, GLA_DK)
    o_f = gla_chunked(qh, kh, vh, la_f)
    flip = lambda t: jnp.flip(t, axis=2)
    o_b = flip(gla_chunked(flip(qh), flip(kh), flip(vh), flip(la_b)))
    o = rms_norm_2(o_f + o_b, out_gain)
    o = o.transpose(0, 2, 1, 3).reshape(B, T, GLA_WIDTH)
    return o * jax.nn.silu(g)

def axial_rope_tables(T):
    rows = T // GRID_W
    row = jnp.repeat(jnp.arange(rows), GRID_W).astype(jnp.float32)
    col = jnp.tile(jnp.arange(GRID_W), rows).astype(jnp.float32)
    axis_dim = ATT_HEAD_DIM // 2
    inv_freq = ROPE_THETA ** (-jnp.arange(0, axis_dim, 2, dtype=jnp.float32) / axis_dim)
    ang = jnp.concatenate([row[:, None] * inv_freq, col[:, None] * inv_freq], axis=-1)
    return jnp.cos(ang), jnp.sin(ang)

def apply_axial_rope(x, cos, sin):
    xr = x.astype(jnp.float32).reshape(*x.shape[:-1], -1, 2)
    x0, x1 = xr[..., 0], xr[..., 1]
    out = jnp.stack([x0 * cos - x1 * sin, x0 * sin + x1 * cos], axis=-1)
    return out.reshape(x.shape).astype(x.dtype)

def gqa_group(q, k, v, q_gain, k_gain, out_gain):
    B, T, _ = q.shape
    dh = ATT_HEAD_DIM
    G = ATT_HEADS // ATT_KV_HEADS
    qh = rms_norm_2(q.reshape(B, T, ATT_HEADS, dh).transpose(0, 2, 1, 3), q_gain)
    kh = rms_norm_2(k.reshape(B, T, ATT_KV_HEADS, dh).transpose(0, 2, 1, 3), k_gain)
    vh = v.reshape(B, T, ATT_KV_HEADS, dh).transpose(0, 2, 1, 3)
    cos, sin = axial_rope_tables(T)
    qh = apply_axial_rope(qh, cos, sin) * (dh ** -0.5)
    kh = apply_axial_rope(kh, cos, sin)
    nb = T // Q_BLOCK
    q_blocks = qh.reshape(B, ATT_KV_HEADS, G, nb, Q_BLOCK, dh).transpose(3, 0, 1, 2, 4, 5)

    def attend(qb):
        s = jnp.einsum('bkgqd,bksd->bkgqs', qb, kh).astype(jnp.float32)
        p = jax.nn.softmax(s, axis=-1).astype(vh.dtype)
        return jnp.einsum('bkgqs,bksd->bkgqd', p, vh)

    o = lax.map(attend, q_blocks)
    o = o.transpose(1, 0, 4, 2, 3, 5).reshape(B, T, ATT_WIDTH)
    return rms_norm_2(o, out_gain)

def hier_moe(x, w_group, b_group, w_expert, b_expert, w_gate, w_up, w_down):
    B, T, D = x.shape
    xt = x.reshape(-1, D)
    N = xt.shape[0]
    g_logits = (xt @ w_group + b_group).astype(jnp.float32)
    g_prob = jax.nn.softmax(g_logits, axis=-1)
    g_idx = jnp.argmax(g_logits, axis=-1)
    g_w = jnp.take_along_axis(g_prob, g_idx[:, None], axis=-1)
    e_logits = (xt @ w_expert + b_expert).astype(jnp.float32).reshape(N, N_GROUPS, EXPERTS_PER_GROUP)
    e_logits = jnp.take_along_axis(e_logits, g_idx[:, None, None], axis=1)[:, 0]
    top_val, top_idx = lax.top_k(e_logits, TOP_K)
    gate = g_w * jax.nn.softmax(top_val, axis=-1)
    expert_id = g_idx[:, None] * EXPERTS_PER_GROUP + top_idx

    M = N * TOP_K
    flat_e = expert_id.reshape(M).astype(jnp.int32)
    flat_tok = jnp.repeat(jnp.arange(N, dtype=jnp.int32), TOP_K)
    flat_gate = gate.reshape(M).astype(x.dtype)
    order = jnp.argsort(flat_e)
    se = flat_e[order]
    counts = jnp.bincount(flat_e, length=N_EXPERTS)
    starts = jnp.cumsum(counts) - counts
    padded = (counts + MOE_BLOCK - 1) // MOE_BLOCK * MOE_BLOCK
    pad_ends = jnp.cumsum(padded)
    pad_starts = pad_ends - padded
    dest = pad_starts[se] + (jnp.arange(M, dtype=jnp.int32) - starts[se])
    P = M + N_EXPERTS * MOE_BLOCK
    slot_tok = jnp.zeros((P,), jnp.int32).at[dest].set(flat_tok[order])
    slot_gate = jnp.zeros((P,), x.dtype).at[dest].set(flat_gate[order])
    nblk = P // MOE_BLOCK
    blk_start = jnp.arange(nblk, dtype=jnp.int32) * MOE_BLOCK
    blk_expert = jnp.minimum(jnp.searchsorted(pad_ends, blk_start, side='right'), N_EXPERTS - 1)
    xs = xt[slot_tok].reshape(nblk, MOE_BLOCK, D)

    def run_block(args):
        xb, e = args
        h = jax.nn.silu(xb @ w_gate[e]) * (xb @ w_up[e])
        return h @ w_down[e]

    ys = lax.map(run_block, (xs, blk_expert)).reshape(P, D)
    y = jnp.zeros((N, D), x.dtype).at[slot_tok].add(ys * slot_gate[:, None])
    return y.reshape(B, T, D)

def second_inputs(seed: int = 0) -> dict:
    key = jax.random.key(seed)
    ks = jax.random.split(key, 24)
    f32 = jnp.float32
    L = DEPTH_2

    def nrm(k, shape, scale):
        return jax.random.normal(k, shape, f32) * scale

    def gain(k, shape):
        return 1.0 + 0.02 * jax.random.normal(k, shape, f32)

    return {
        "x": nrm(ks[0], (BATCH, SEQ, D_MODEL), 1.0),
        "norm1_gain": gain(ks[1], (L, D_MODEL)),
        "w_in": nrm(ks[2], (L, D_MODEL, D_IN), D_MODEL ** -0.5),
        "gla_up_fwd": nrm(ks[3], (L, GLA_GATE_RANK, GLA_KEY_WIDTH), GLA_GATE_RANK ** -0.5),
        "gla_up_fwd_bias": nrm(ks[4], (L, GLA_KEY_WIDTH), 0.1),
        "gla_up_bwd": nrm(ks[5], (L, GLA_GATE_RANK, GLA_KEY_WIDTH), GLA_GATE_RANK ** -0.5),
        "gla_up_bwd_bias": nrm(ks[6], (L, GLA_KEY_WIDTH), 0.1),
        "gla_out_gain": gain(ks[7], (L, GLA_DV)),
        "q_norm_gain": gain(ks[8], (L, ATT_HEAD_DIM)),
        "k_norm_gain": gain(ks[9], (L, ATT_HEAD_DIM)),
        "att_out_gain": gain(ks[10], (L, ATT_WIDTH)),
        "w_out": nrm(ks[11], (L, D_MIX, D_MODEL), D_MIX ** -0.5),
        "norm2_gain": gain(ks[12], (L, D_MODEL)),
        "w_group": nrm(ks[13], (L, D_MODEL, N_GROUPS), D_MODEL ** -0.5),
        "b_group": nrm(ks[14], (L, N_GROUPS), 0.01),
        "w_expert": nrm(ks[15], (L, D_MODEL, N_EXPERTS), D_MODEL ** -0.5),
        "b_expert": nrm(ks[16], (L, N_EXPERTS), 0.01),
        "w_gate": nrm(ks[17], (L, N_EXPERTS, D_MODEL, D_EXPERT), D_MODEL ** -0.5),
        "w_up": nrm(ks[18], (L, N_EXPERTS, D_MODEL, D_EXPERT), D_MODEL ** -0.5),
        "w_down": nrm(ks[19], (L, N_EXPERTS, D_EXPERT, D_MODEL), D_EXPERT ** -0.5),
        "final_gain": gain(ks[20], (D_MODEL,)),
    }

def second_block(x, norm1_gain, w_in, gla_up_fwd, gla_up_fwd_bias, gla_up_bwd, gla_up_bwd_bias,
              gla_out_gain, q_norm_gain, k_norm_gain, att_out_gain, w_out, norm2_gain,
              w_group, b_group, w_expert, b_expert, w_gate, w_up, w_down, final_gain):
    split_points = np.cumsum(IN_SIZES)[:-1].tolist()
    h = x
    for l in range(DEPTH_2):
        u = rms_norm_2(h, norm1_gain[l])
        proj = u @ w_in[l]
        gq, gk, gv, gg, zf, zb, aq, ak, av = jnp.split(proj, split_points, axis=-1)
        o_gla = gla_group(gq, gk, gv, gg, zf, zb, gla_up_fwd[l], gla_up_fwd_bias[l],
                          gla_up_bwd[l], gla_up_bwd_bias[l], gla_out_gain[l])
        o_att = gqa_group(aq, ak, av, q_norm_gain[l], k_norm_gain[l], att_out_gain[l])
        mixed = jnp.concatenate([o_gla, o_att], axis=-1)
        h = h + mixed @ w_out[l]
        h = h + hier_moe(rms_norm_2(h, norm2_gain[l]), w_group[l], b_group[l], w_expert[l],
                         b_expert[l], w_gate[l], w_up[l], w_down[l])
    return rms_norm_2(h, final_gain)


def setup_inputs(seed=0):
    out = dict(first_inputs(seed))
    for name, value in second_inputs(seed + 1).items():
        if name != "x":
            out[name + "_2"] = value
    return out


def reference(
    x, mla_w_in, mla_q_norm, mla_kv_norm, mla_w_uq, mla_w_ukv, mla_w_o, moba_w_kv, moba_w_in,
    moba_w_o, ln_g, ln_b, norm1_gain_2, w_in_2, gla_up_fwd_2, gla_up_fwd_bias_2, gla_up_bwd_2,
    gla_up_bwd_bias_2, gla_out_gain_2, q_norm_gain_2, k_norm_gain_2, att_out_gain_2, w_out_2,
    norm2_gain_2, w_group_2, b_group_2, w_expert_2, b_expert_2, w_gate_2, w_up_2, w_down_2,
    final_gain_2,
):
    x = first_block(
        x, mla_w_in, mla_q_norm, mla_kv_norm, mla_w_uq, mla_w_ukv, mla_w_o, moba_w_kv,
        moba_w_in, moba_w_o, ln_g, ln_b,
    )
    return second_block(
        x, norm1_gain_2, w_in_2, gla_up_fwd_2, gla_up_fwd_bias_2, gla_up_bwd_2,
        gla_up_bwd_bias_2, gla_out_gain_2, q_norm_gain_2, k_norm_gain_2, att_out_gain_2,
        w_out_2, norm2_gain_2, w_group_2, b_group_2, w_expert_2, b_expert_2, w_gate_2, w_up_2,
        w_down_2, final_gain_2,
    )


_drawn_inputs = setup_inputs


def setup_inputs(seed=0):
    import zlib

    import numpy as np

    out = dict(_drawn_inputs(seed))
    spreads = {}
    factors = {'mla_q_norm': 8.0,
     'mla_kv_norm': 8.0,
     'gla_up_fwd_bias_2': 3.324,
     'gla_up_bwd_bias_2': 2.951,
     'gla_out_gain_2': 6.815,
     'q_norm_gain_2': 3.028,
     'k_norm_gain_2': 4.171,
     'att_out_gain_2': 3.177,
     'norm2_gain_2': 2.891,
     'b_group_2': 6.954,
     'b_expert_2': 8.0,
     'final_gain_2': 2.834}
    for name, (base, spread) in spreads.items():
        noise = np.random.default_rng([zlib.crc32(name.encode()), seed]).standard_normal(out[name].shape)
        drawn = base * np.exp(spread * noise) if base else spread * noise
        out[name] = __import__('jax').numpy.asarray(drawn.astype(out[name].dtype))
    for name, factor in factors.items():
        out[name] = (out[name] * factor).astype(out[name].dtype)
    return out
```

```python
from contextlib import ExitStack

import numpy as np

import concourse.bass as bass
from concourse import mybir

ALU = mybir.AluOpType
ACT = mybir.ActivationFunctionType
AX = mybir.AxisListType
F32 = mybir.dt.float32
BF16 = mybir.dt.bfloat16
I32 = mybir.dt.int32

P = 128
D = 1024
SEQ = 256
TILES = SEQ // P
KD = D // P

H = 16
NOPE, ROPE, VD = 64, 32, 64
QKD = NOPE + ROPE
Q_LORA, KV_LORA = 768, 256
HD = 64
SCALE_A = QKD ** -0.5
SCALE_B = HD ** -0.5
ALPHA = 4 ** 0.25
LN_EPS = 1e-5
RMS_EPS = 1e-6

GH, GDK, GDV = 4, 64, 128
GW = GH * GDK
CHUNK = 64
NCHUNK = SEQ // CHUNK
QH, KVH = 8, 2

NG, EPG = 8, 8
NE = NG * EPG
FE = 512
SLOTS = 32
GROUP = 4
ROUNDS = NE // GROUP
PASSES = SEQ // SLOTS
BIG = 1e30

RING = 6
SLOT = 4096
LAG = 2

BLOCKS = (
    [("mla_w_in", 8, a, n) for a, n in ((0, 512), (512, 512), (1024, 416), (1440, 320), (1760, 320))]
    + [("mla_w_uq", 6, 384 * b, 384) for b in range(4)]
    + [("mla_w_ukv", 2, 0, 2048)]
    + [("mla_w_o", 8, 512 * b, 512) for b in range(2)]
    + [("moba_w_kv", 8, 512 * b, 512) for b in range(4)]
    + [("moba_w_in", 8, 512 * b, 512) for b in range(4)]
    + [("moba_w_o", 8, 512 * b, 512) for b in range(2)]
    + [("w_in_2", 8, a, n) for a, n in ((0, 512), (512, 512), (1024, 512), (1536, 416), (1952, 384))]
    + [("w_out_2", 8, 512 * b, 512) for b in range(2)]
)


JOBS = []
for _name, _n, _tile_outer in (("mla_w_in", 5, 0), ("mla_w_uq", 4, 0), ("mla_w_ukv", 4, 0), ("mla_w_o", 2, 1),
                               ("moba_w_kv", 4, 0), ("moba_w_in", 4, 0), ("moba_w_o", 2, 1),
                               ("w_in_2", 5, 0), ("w_out_2", 2, 1)):
    if _tile_outer:
        JOBS += [(_name, b, t) for t in range(TILES) for b in range(_n)]
    else:
        JOBS += [(_name, b, t) for b in range(_n) for t in range(TILES)]
JOB = {job: n for n, job in enumerate(JOBS)}


def block_of(job):
    name, b, _ = job
    first = min(i for i, x in enumerate(BLOCKS) if x[0] == name)
    return first if name == "mla_w_ukv" else first + b


LAST_JOB = [max(n for n, job in enumerate(JOBS) if block_of(job) == b) for b in range(len(BLOCKS))]

KV_ORDER = [(way, step) for step in range(SEQ // 64 - 1) for way in range(2)]

RSQRT = {}
_at = 0
for _n, (_name, _w) in enumerate((("mla", 4), ("ln0t0", 1), ("ln0t1", 1), ("ln1t0", 1), ("ln1t1", 1),
                                  ("norm1t0", 1), ("norm1t1", 1), ("qk", 20), ("gla", 8), ("att", 2),
                                  ("norm2t0", 1), ("norm2t1", 1), ("finalt0", 1), ("finalt1", 1))):
    RSQRT[_name] = (_n, _at, _w)
    _at += _w
RSQRT_COLS = _at

GAIN_Q, GAIN_N1, GAIN_MIX, GAIN_ROWS = 0, 8, 16, 24


def shape_constants():
    f = np.float32
    tok = np.arange(SEQ, dtype=f)

    def tiled(a):
        return a.reshape(TILES, P, -1).transpose(1, 0, 2).reshape(P, -1)

    def half_tables(dim):
        inv = f(10000.0) ** (-np.arange(0, dim, 2, dtype=f) / f(dim))
        ang = (tok[:, None] * inv[None, :]).astype(f)
        c, s = np.cos(ang), np.sin(ang)
        return tiled(np.concatenate([c, c], 1)), tiled(np.concatenate([-s, s], 1))

    cos_a, sin_a = half_tables(ROPE)
    cos_b, sin_b = half_tables(HD)
    inv = f(10000.0) ** (-np.arange(0, 32, 2, dtype=f) / f(32))
    row, col = np.floor(tok / 64).astype(f), (tok % 64).astype(f)
    ang = np.concatenate([row[:, None] * inv, col[:, None] * inv], 1).astype(f)
    c, s = np.cos(ang), np.sin(ang)
    cos_g = tiled(np.repeat(c, 2, 1))
    sin_g = tiled(np.stack([-s, s], 2).reshape(SEQ, 64))
    i = np.arange(P)
    src, dst = i[:, None], i[None, :]
    same = (src // CHUNK) == (dst // CHUNK)
    fwd, bwd = same & (src <= dst), same & (src >= dst)
    mid_f, mid_b = same & (src % CHUNK <= CHUNK // 2 - 1), same & (src % CHUNK >= CHUNK // 2)
    out = {
        "ident": np.eye(P),
        "ones": np.ones((P, P)),
        "tri": src <= dst,
        "cum_fwd": np.concatenate([fwd.astype(f) - mid_f, fwd], 1),
        "cum_bwd": np.concatenate([bwd.astype(f) - mid_b, bwd], 1),
        "rest_fwd": same & (src > dst),
        "rest_bwd": same & (src < dst),
        "causal": np.where(dst > src, -BIG, 0.0),
        "cos_a": cos_a, "sin_a": sin_a, "cos_b": cos_b, "sin_b": sin_b, "cos_g": cos_g, "sin_g": sin_g,
        "iota": np.tile(np.arange(SLOTS), (P, 1)),
        "desc": np.tile(np.arange(NE, 0, -1), (P, 1)),
    }
    return {k: np.ascontiguousarray(v, dtype=f) for k, v in out.items()}


def const_layout():
    at, out = 0, {}
    for k, v in shape_constants().items():
        out[k] = (at, v.shape[1])
        at += v.shape[1]
    return out, at


def build(nc, t):
    where, const_cols = const_layout()
    with ExitStack() as ctx:
        def sb(name, shape, dt=F32):
            return ctx.enter_context(nc.sbuf_tensor(name, shape, dt))

        def sem(name):
            return ctx.enter_context(nc.semaphore(name))

        bank = [ctx.enter_context(nc.psum_tensor(f"bank{i}", [P, 512], F32)) for i in range(8)]
        proj_bank = bank[0:2]
        tr_bank = bank[2:4]
        score_bank = [bank[4], bank[5], bank[0], bank[1]]
        out_bank = bank[6:8]

        ring = sb("ring", [P, RING, SLOT])
        consts = sb("consts", [P, const_cols])
        res = sb("res", [P, TILES, D])
        xt = sb("xt", [P, KD, SEQ])
        gate = sb("gate", [P, TILES, D])
        wide = sb("wide", [P, TILES, D])
        val = sb("val", [P, TILES, D])
        qk = sb("qk", [P, 8192])
        stage = sb("stage", [P, 4, 512])
        probs = sb("probs", [P, 4, 256])
        probs_t = sb("probs_t", [P, 2, 256])
        tmp = sb("tmp", [P, 2, 1024])
        small = sb("small", [P, 512])
        gain_rows = tmp[0:GAIN_ROWS, 0, 0:P]
        head_gain = tmp[:, 1, 0:2 * HD]
        gain_cols = sb("gain_cols", [P, GAIN_ROWS])
        ident_b = sb("ident_b", [P, P], BF16)
        causal_b = sb("causal_b", [P, P], BF16)
        var = sb("var", [P, RSQRT_COLS])
        rstd = sb("rstd", [P, RSQRT_COLS])
        power = sb("power", [P, 20])
        router_w = stage[:, 0:2, :].rearrange("p a n -> p (a n)")[:, 0:KD * (NG + NE)].rearrange(
            "p (c n) -> p c n", c=KD)
        router_b = sb("router_b", [P, NG + NE])
        rank = sb("rank", [P, TILES, NE])
        gates = sb("gates", [P, TILES, NE])
        largest = sb("largest", [P, 1], I32)

        def const(name):
            a, n = where[name]
            return consts[:, a:a + n]

        ident = const("ident")
        q_t, k_t = qk[:, 0:4096], qk[:, 4096:8192]
        q_a = q_t.rearrange("p (h s) -> p h s", h=H)
        k_a = k_t.rearrange("p (h s) -> p h s", h=H)
        q_b = q_t[:, 0:2048].rearrange("p (h s) -> p h s", h=H // 2)
        k_b = k_t[:, 0:2048].rearrange("p (h s) -> p h s", h=H // 2)
        ln_row = tmp
        q_g = qk[:, 0:1024].rearrange("p (h s) -> p h s", h=QH // 2)
        k_g = qk[:, 1024:1536].rearrange("p (h s) -> p h s", h=KVH)
        exp_q = qk[:, 1536:2560].rearrange("p (d a s) -> p d a s", d=2, a=2)
        exp_k = qk[:, 2560:3584].rearrange("p (d a s) -> p d a s", d=2, a=2)
        exp_b = qk[:, 3584:4608].rearrange("p (d a s) -> p d a s", d=2, a=2)
        q_in = qk[:, 4608:5632].rearrange("p (d a s) -> p d a s", d=2, a=2)
        k_out = qk[:, 5632:6656].rearrange("p (t d n) -> p t d n", t=2, d=2)
        gla_t = qk[:, 6656:7680].rearrange("p (c s) -> p c s", c=4)
        z_t = qk[:, 7680:7936]
        gla_qk = stage[:, 0:2, :]
        decay = stage[:, 2:4, :]
        state = xt.rearrange("p c s -> p (c s)").rearrange("p (n a e) -> p n a e", n=4, a=2)
        state_b = val[:, :, 512:1024].rearrange("p t (a e) -> p t a e", a=2)
        att_q = gate[:, :, 512:1024]
        att_kv = sb("att_kv", [P, TILES, 256])
        key2 = probs_t
        z_in = sb("z_in", [P, TILES, 32])
        up_w = probs[0:33, 2:4, :].rearrange("p a b -> p (a b)")
        rope_g = sb("rope_g", [P, 4, 128])
        masked = wide[:, :, 512:1024]
        norm2_row, final_row = gate[:, 0, :], gate[:, 1, :]
        picked = qk[:, 0:1024].rearrange("p (c s) -> p c s", c=KD)
        onehot = qk[:, 1024:1280].rearrange("p (t s) -> p t s", t=2)
        weighted = qk[:, 1280:1536].rearrange("p (t s) -> p t s", t=2)
        back = qk[:, 1536:1792]
        act_g = qk[:, 1792:1920]
        hidden = qk[:, 1920:2048]
        hidden_t = qk[:, 2048:2176]
        expert_out = qk[:, 2176:3200]
        top_diff = small[:, 172:174]
        g_exp = small[:, 200:216]
        ratio = small[:, 216:218]
        g_diff = tmp[:, 0, 48:64]
        routed = wide.rearrange("p t (c k) -> p t c k", c=KD)

        x_landed = sem("x_landed")
        consts_landed = sem("consts_landed")
        gains_landed = sem("gains_landed")
        ln_landed = sem("ln_landed")
        row_landed = sem("row_landed")
        small_landed = sem("small_landed")
        up_zeroed = sem("up_zeroed")
        up_landed = sem("up_landed")
        block_landed = [sem(f"block_landed{i}") for i in range(RING)]
        proj_in_psum = sem("proj_in_psum")
        proj_in_sbuf = sem("proj_in_sbuf")
        tr_in_psum = sem("tr_in_psum")
        tr_in_sbuf = sem("tr_in_sbuf")
        masks_cast = sem("masks_cast")
        power_set = sem("power_set")
        rsqrt_asked = sem("rsqrt_asked")
        rsqrt_done = sem("rsqrt_done")
        sumsq_done = sem("sumsq_done")
        latents_normed = sem("latents_normed")
        heads_roped = sem("heads_roped")
        key_rope_placed = sem("key_rope_placed")
        scores_in_psum = sem("scores_in_psum")
        max_done = sem("max_done")
        probs_done = sem("probs_done")
        out_in_psum = sem("out_in_psum")
        out_drained = sem("out_drained")
        mixed_ready = sem("mixed_ready")
        res_ready = sem("res_ready")
        ln_used = sem("ln_used")
        normed_ready = sem("normed_ready")
        gqa_ready = sem("gqa_ready")
        decay_in_psum = sem("decay_in_psum")
        decay_log = sem("decay_log")
        decay_ready = sem("decay_ready")
        cum_in_psum = sem("cum_in_psum")
        cum_exp = sem("cum_exp")
        gla_operands = sem("gla_operands")
        kv_in_psum = sem("kv_in_psum")
        state_ready = sem("state_ready")
        gla_scores = sem("gla_scores")
        gla_masked = sem("gla_masked")
        gla_intra = sem("gla_intra")
        gla_inter = sem("gla_inter")
        gla_copied = sem("gla_copied")
        gla_summed = sem("gla_summed")
        routed_ready = sem("routed_ready")
        logits_in_psum = sem("logits_in_psum")
        mask_ready = sem("mask_ready")
        gates_exp = sem("gates_exp")
        rank_moved = sem("rank_moved")
        ranks_in_psum = sem("ranks_in_psum")
        routing_ready = sem("routing_ready")
        gate_up_landed = [sem(f"gate_up_landed{i}") for i in range(2)]
        down_landed = [sem(f"down_landed{i}") for i in range(2)]
        onehot_ready = sem("onehot_ready")
        picked_in_psum = sem("picked_in_psum")
        picked_ready = sem("picked_ready")
        back_in_psum = sem("back_in_psum")
        back_ready = sem("back_ready")
        hidden_in_psum = sem("hidden_in_psum")
        silu_done = sem("silu_done")
        hidden_ready = sem("hidden_ready")
        hidden_t_in_psum = sem("hidden_t_in_psum")
        hidden_t_ready = sem("hidden_t_ready")
        down_in_psum = sem("down_in_psum")
        down_drained_act = sem("down_drained_act")
        down_drained_dve = sem("down_drained_dve")
        sum_in_psum = sem("sum_in_psum")
        sum_added = sem("sum_added")
        act_chain = sem("act_chain")
        dve_chain = sem("dve_chain")
        out_ready = sem("out_ready")
        out_stored = sem("out_stored")

        block = ctx.enter_context(nc.Block())

        TR = {}
        count = 0
        for name, n in (("gains", 1), ("x", 4), ("latents", 4), ("q_a", 8), ("k_a", 8), ("att_a", 32), ("o_a", 4),
                        ("x1", 4), ("k_b", 4), ("q_b", 4), ("att_b", 32), ("o_b", 4), ("u", 4),
                        ("gla", 2), ("z", 2), ("gqa_q", 2), ("gqa_k", 2), ("att_g", 16), ("mixed", 4), ("routed", 4)):
            TR[name] = count
            count += n

        UNITS_A = UNITS_B = H * TILES
        UNITS_G = QH * TILES
        UNIT0 = {"a": 0, "b": UNITS_A, "g": UNITS_A + UNITS_B}
        OUT0 = {"a": 0, "b": 4, "g": 8}

        def state_of(way, step):
            n = 3 * way + step
            return state[:, n] if n < 4 else state_b[:, n - 4]

        def keys_of(kind, tile):
            return SEQ if kind == "g" else P * (tile + 1)

        @block.sync
        def _(sp):
            sp.dma_start(res[:], t["x"].rearrange("b (t p) d -> p (b t) d", p=P)).then_inc(x_landed, 16)
            sp.dma_start(consts[:], t["consts"]).then_inc(consts_landed, 16)
            for b, (name, kc, first, n) in enumerate(BLOCKS):
                slot = b % RING
                if b >= RING:
                    sp.wait_ge(proj_in_psum, LAST_JOB[b - RING] + 1)
                w = t[name]
                src = (w if name == "moba_w_kv" else w[0])[:, first:first + n].rearrange("(c p) n -> p c n", p=P)
                dst = ring[:, slot, 0:kc * n].rearrange("p (c n) -> p c n", c=kc)
                sp.dma_start(dst, src).then_inc(block_landed[slot], 16)

            def load_expert(e, parity, waits):
                base = 3 * parity
                waits(0)
                for k, name in ((0, "w_gate_2"), (1, "w_up_2")):
                    src = t[name][0, bass.ds(e, 1)].rearrange("e (p c) f -> p (e c f)", c=KD)
                    sp.dma_start(ring[:, base + k, :], src).then_inc(gate_up_landed[parity], 16)
                waits(1)
                src = t["w_down_2"][0, bass.ds(e, 1)].rearrange("e (j p) n -> p (e j) n", p=P)
                sp.dma_start(ring[:, base + 2, :].rearrange("p (j n) -> p j n", j=4), src).then_inc(
                    down_landed[parity], 16)

            def front_done(parity):
                def waits(k):
                    slots = (3 * parity, 3 * parity + 1) if k == 0 else (3 * parity + 2,)
                    last = max(b for b in range(len(BLOCKS)) if b % RING in slots)
                    sp.wait_ge(proj_in_psum, LAST_JOB[last] + 1)
                return waits

            def expert_used(before):
                def waits(k):
                    sp.wait_ge(hidden_in_psum if k == 0 else down_in_psum, before)
                return waits

            for e in range(2):
                load_expert(e, e, front_done(e))
            with sp.Fori(0, ROUNDS - 1) as r:
                for i in range(GROUP):
                    load_expert(GROUP * r + (i + 2), i % 2, expert_used(GROUP * r + (i + 1)))
            for e in range(NE - 2, NE):
                load_expert(e, e % 2, expert_used(e - 1))

            sp.wait_ge(routing_ready, 1)
            most = sp.value_load(largest[0:1, 0:1], min_val=0, max_val=SEQ)
            with sp.If(most > SLOTS):
                with sp.Fori(1, PASSES) as p:
                    for e in range(2):
                        load_expert(e, e, expert_used(NE * p + (e - 1)))
                    with sp.Fori(0, ROUNDS - 1) as r:
                        for i in range(GROUP):
                            load_expert(GROUP * r + (i + 2), i % 2, expert_used(NE * p + GROUP * r + (i + 1)))
                    for e in range(NE - 2, NE):
                        load_expert(e, e % 2, expert_used(NE * p + (e - 1)))

            for tile in range(TILES):
                sp.wait_ge(out_ready, tile + 1)
                sp.dma_start(t["out"][0, tile * P:(tile + 1) * P, :], wide[:, tile, :]).then_inc(out_stored, 16)
            sp.wait_ge(out_stored, 16 * TILES)

        @block.gpsimd
        def _(pool):
            nc.gpsimd.memset(power[:], -0.5).then_inc(power_set, 1)
            pool.wait_ge(power_set, 1)
            for n, a, w in RSQRT.values():
                pool.wait_ge(rsqrt_asked, n + 1)
                nc.gpsimd.tensor_tensor(rstd[:, a:a + w], var[:, a:a + w], power[:, 0:w], ALU.pow).then_inc(
                    rsqrt_done, 1)

        @block.scalar
        def _(act):
            rows = ((GAIN_Q, t["mla_q_norm"], 6), (6, t["mla_kv_norm"], 2), (GAIN_N1, t["norm1_gain_2"], 8),
                    (GAIN_MIX, t["gla_out_gain_2"], 1), (GAIN_MIX + 1, t["gla_out_gain_2"], 1),
                    (GAIN_MIX + 2, t["gla_out_gain_2"], 1), (GAIN_MIX + 3, t["gla_out_gain_2"], 1),
                    (GAIN_MIX + 4, t["att_out_gain_2"], 4))
            for a, src, n in rows:
                act.dma_start(gain_rows[a:a + n, :], src[0].rearrange("(r p) -> r p", p=P)).then_inc(gains_landed, 16)

            def load_row(dst, src, signal):
                act.dma_start(dst, src.rearrange("(a n) -> a n", a=1).to_broadcast([P, src.shape[0]])).then_inc(
                    signal, 16)

            def load_ln(layer):
                load_row(ln_row[:, 0, :], t["ln_g"][layer], ln_landed)
                load_row(ln_row[:, 1, :], t["ln_b"][layer], ln_landed)

            load_row(router_b[:, 0:NG], t["b_group_2"][0], small_landed)
            load_row(router_b[:, NG:], t["b_expert_2"][0], small_landed)
            load_row(head_gain[:, 0:HD], t["q_norm_gain_2"][0], small_landed)
            load_row(head_gain[:, HD:], t["k_norm_gain_2"][0], small_landed)

            def start_job(job):
                act.wait_ge(proj_in_psum, JOB[job] + 1)
                return proj_bank[JOB[job] % 2]

            def squares(src, column):
                return nc.scalar.activation(tmp[:, 0, 0:src.shape[-1]], src, ACT.Square,
                                            accum_out=small[:, column:column + 1])

            chain = [0]

            def link(ins):
                chain[0] += 1
                ins.then_inc(act_chain, 1)
                act.wait_ge(act_chain, chain[0])

            for tile in range(TILES):
                src = start_job(("mla_w_in", 0, tile))
                link(squares(src[:, 0:512], 3 * tile))
                nc.scalar.copy(wide[:, tile, 0:512], src[:]).then_inc(proj_in_sbuf, 1)
            for tile in range(TILES):
                src = start_job(("mla_w_in", 1, tile))
                link(squares(src[:, 0:256], 3 * tile + 1))
                squares(src[:, 256:512], 3 * tile + 2).then_inc(sumsq_done, 1)
                act.wait_ge(sumsq_done, tile + 1)
                nc.scalar.copy(wide[:, tile, 512:1024], src[:]).then_inc(proj_in_sbuf, 1)
            for tile in range(TILES):
                src = start_job(("mla_w_in", 2, tile))
                nc.scalar.copy(z_in[:, tile, :], src[:, 0:ROPE])
                nc.scalar.activation(gate[:, tile, 0:384], src[:, 32:416], ACT.Silu).then_inc(proj_in_sbuf, 1)
            for b, a in ((3, 384), (4, 704)):
                for tile in range(TILES):
                    src = start_job(("mla_w_in", b, tile))
                    nc.scalar.activation(gate[:, tile, a:a + 320], src[:, 0:320], ACT.Silu).then_inc(proj_in_sbuf, 1)
            for n, job in enumerate([("mla_w_uq", b, tile) for b in range(4) for tile in range(TILES)]):
                if n >= 4:
                    act.wait_ge(tr_in_psum, TR["q_a"] + n - 3)
                src = start_job(job)
                nc.scalar.mul(stage[:, n % 4, 0:384], src[:, 0:384], SCALE_A).then_inc(proj_in_sbuf, 1)
            for n, job in enumerate([("mla_w_ukv", b, tile) for b in range(4) for tile in range(TILES)]):
                if n == 0:
                    act.wait_ge(key_rope_placed, 1)
                if n >= 4:
                    act.wait_ge(tr_in_psum, TR["k_a"] + n - 3)
                src = start_job(job)[:].rearrange("p (h d) -> p h d", h=4)
                b, tile = job[1], job[2]
                nc.scalar.copy(stage[:, n % 4, 0:4 * QKD].rearrange("p (h d) -> p h d", h=4)[:, :, 0:NOPE],
                               src[:, :, 0:NOPE])
                nc.scalar.copy(val[:, tile, 256 * b:256 * b + 256].rearrange("p (h d) -> p h d", h=4),
                               src[:, :, NOPE:]).then_inc(proj_in_sbuf, 1)

            row_sum = small[:, 256:256 + 80]
            neg_max = small[:, 336:336 + 80]

            def softmax_units(kind, units):
                for u in range(units):
                    n = UNIT0[kind] + u
                    keys = keys_of(kind, u % TILES)
                    act.wait_ge(max_done, n + 1)
                    if u >= 4:
                        act.wait_ge(tr_in_psum, TR["att_" + kind] + u - 3)
                    nc.scalar.activation(probs[:, u % 4, 0:keys], score_bank[u % 4][:, 0:keys], ACT.Exp,
                                         bias=neg_max[:, n:n + 1], accum_out=row_sum[:, n:n + 1]).then_inc(
                        probs_done, 1)

            softmax_units("a", UNITS_A)
            load_ln(0)

            def drain_output(name):
                for tile in range(TILES):
                    for b in range(2):
                        src = start_job((name, b, tile))
                        nc.scalar.copy(wide[:, tile, 512 * b:512 * b + 512], src[:]).then_inc(proj_in_sbuf, 1)

            drain_output("mla_w_o")

            def drain_heads(name, scale, transposed):
                act.wait_ge(tr_in_psum, transposed)
                for n, job in enumerate([(name, b, tile) for b in range(2) for tile in range(TILES)]):
                    src = start_job(job)
                    nc.scalar.mul(stage[:, n, :], src[:], scale).then_inc(proj_in_sbuf, 1)

            drain_heads("moba_w_kv", 1.0, TR["k_a"] + 8)
            for b in range(2):
                for tile in range(TILES):
                    src = start_job(("moba_w_kv", 2 + b, tile))
                    nc.scalar.copy(val[:, tile, 512 * b:512 * b + 512], src[:]).then_inc(proj_in_sbuf, 1)
            drain_heads("moba_w_in", SCALE_B, TR["k_b"] + 4)
            for b in range(2):
                for tile in range(TILES):
                    src = start_job(("moba_w_in", 2 + b, tile))
                    nc.scalar.activation(gate[:, tile, 512 * b:512 * b + 512], src[:], ACT.Silu).then_inc(
                        proj_in_sbuf, 1)
            softmax_units("b", UNITS_B)
            load_ln(1)
            drain_output("moba_w_o")
            act.wait_ge(up_zeroed, 1)
            for k, (w, b) in enumerate((("gla_up_fwd_2", "gla_up_fwd_bias_2"), ("gla_up_bwd_2", "gla_up_bwd_bias_2"))):
                act.dma_start(up_w[16 * k:16 * k + 16, GW * k:GW * k + GW], t[w][0]).then_inc(up_landed, 16)
                act.dma_start(up_w[32:33, GW * k:GW * k + GW], t[b]).then_inc(up_landed, 16)

            def stream_squares(first):
                for tile in range(TILES):
                    act.wait_ge(res_ready, first + tile + 1)
                    squares(res[:, tile, :], 16 + first + tile).then_inc(sumsq_done, 1)
                    act.wait_ge(sumsq_done, first + tile + 1)

            act.wait_ge(ln_used, 2)
            stream_squares(2)

            for tile in range(TILES):
                src = start_job(("w_in_2", 0, tile))
                nc.scalar.mul(gla_qk[:, tile, 0:GW], src[:, 0:GW], GDK ** -0.5)
                nc.scalar.copy(gla_qk[:, tile, GW:512], src[:, GW:512]).then_inc(proj_in_sbuf, 1)
            for tile in range(TILES):
                src = start_job(("w_in_2", 1, tile))
                nc.scalar.copy(val[:, tile, 0:512], src[:]).then_inc(proj_in_sbuf, 1)
            for tile in range(TILES):
                src = start_job(("w_in_2", 2, tile))
                nc.scalar.activation(gate[:, tile, 0:512], src[:], ACT.Silu).then_inc(proj_in_sbuf, 1)
            for tile in range(TILES):
                src = start_job(("w_in_2", 3, tile))
                nc.scalar.copy(z_in[:, tile, :], src[:, 0:32])
                nc.scalar.copy(att_q[:, tile, 0:384], src[:, 32:416]).then_inc(proj_in_sbuf, 1)
            for tile in range(TILES):
                src = start_job(("w_in_2", 4, tile))
                nc.scalar.copy(att_q[:, tile, 384:512], src[:, 0:128])
                nc.scalar.copy(att_kv[:, tile, :], src[:, 128:384]).then_inc(proj_in_sbuf, 1)

            for tile in range(TILES):
                act.wait_ge(decay_in_psum, 2)
                log = probs[:, 2 * tile:2 * tile + 2, :].rearrange("p a b -> p (a b)")
                link(nc.scalar.activation(log, out_bank[tile][:], ACT.Abs))
                link(nc.scalar.activation(log, log, ACT.Exp, scale=-1.0))
                nc.scalar.activation(log, log, ACT.Ln, bias=const("ones")[:, 0:1]).then_inc(decay_log, 1)
            for n, (tile, way) in enumerate([(i, j) for i in range(TILES) for j in range(2)]):
                act.wait_ge(cum_in_psum, n + 1)
                cum = score_bank[n % 2][:].rearrange("p (a m s) -> p a m s", a=2, m=2)
                at = slice(tile * P, tile * P + P)
                nc.scalar.activation(exp_q[:, way, :, at], cum[:, :, 0, :], ACT.Exp, scale=1 / 16)
                nc.scalar.activation(exp_k[:, way, :, at], cum[:, :, 0, :], ACT.Exp, scale=-1 / 16)
                nc.scalar.activation(exp_b[:, way, :, at], cum[:, :, 1, :], ACT.Exp, scale=1 / 16)
                nc.scalar.activation(k_out[:, tile, way, :], score_bank[2 + n % 2][:, 0:GW], ACT.Exp,
                                     scale=1 / 16).then_inc(cum_exp, 1)
            for tile in range(TILES):
                act.wait_ge(gla_intra, tile + 1)
                nc.scalar.copy(wide[:, tile, 0:512], score_bank[1][:]).then_inc(gla_copied, 1)

            softmax_units("g", UNITS_G)
            load_row(norm2_row, t["norm2_gain_2"][0], row_landed)
            load_row(final_row, t["final_gain_2"], row_landed)
            for src, a, n in ((t["w_group_2"], 0, NG), (t["w_expert_2"], NG, NE)):
                act.dma_start(router_w[:, :, a:a + n], src[0].rearrange("(p c) n -> p c n", c=KD)).then_inc(
                    row_landed, 16)
            drain_output("w_out_2")
            stream_squares(4)

            act.wait_ge(logits_in_psum, 1)
            nc.scalar.copy(small[:, 0:144], proj_bank[0][:, 0:144]).then_inc(proj_in_sbuf, 1)
            act.wait_ge(mask_ready, 1)
            nc.scalar.activation(g_exp, g_diff, ACT.Exp).then_inc(gates_exp, 1)
            act.wait_ge(mask_ready, 2)
            nc.scalar.activation(ratio, top_diff, ACT.Exp).then_inc(gates_exp, 1)

            def expert_rounds(rounds, base):
                with act.Fori(0, rounds) as r:
                    for half in range(2):
                        act.wait_ge(picked_in_psum, 2 * (base + r) + (half + 1))
                        nc.scalar.copy(picked[:, 4 * half:4 * half + 4, :],
                                       bank[half][:].rearrange("p (c s) -> p c s", c=4)).then_inc(picked_ready, 1)
                    for i in range(GROUP):
                        act.wait_ge(hidden_in_psum, GROUP * (base + r) + (i + 1))
                        nc.scalar.activation(act_g, bank[2][:, 0:P], ACT.Silu).then_inc(silu_done, 1)
                        act.wait_ge(down_in_psum, GROUP * (base + r) + (i + 1))
                        nc.scalar.copy(expert_out[SLOTS * i:SLOTS * i + SLOTS, 0:256], bank[4][0:32, 0:256])
                        nc.scalar.copy(expert_out[SLOTS * i:SLOTS * i + SLOTS, 256:512],
                                       bank[4][32:64, 0:256]).then_inc(down_drained_act, 1)

            expert_rounds(ROUNDS, 0)
            act.wait_ge(routing_ready, 1)
            most = act.value_load(largest[0:1, 0:1], min_val=0, max_val=SEQ)
            with act.If(most > SLOTS):
                with act.Fori(1, PASSES) as p:
                    expert_rounds(ROUNDS, ROUNDS * p)

            stream_squares(6)

        @block.vector
        def _(dve):
            chain = [0]

            def link(ins):
                chain[0] += 1
                ins.then_inc(dve_chain, 1)
                dve.wait_ge(dve_chain, chain[0])

            def rsqrt(name):
                n, a, w = RSQRT[name]
                dve.wait_ge(rsqrt_done, n + 1)
                return rstd[:, a:a + w]

            def ask(name, ins):
                ins.then_inc(rsqrt_asked, 1)

            def variances(name):
                n, a, w = RSQRT[name]
                return var[:, a:a + w]

            tr = [0]

            def drain(dst, gain=None, rows=P, width=512):
                n = tr[0]
                dve.wait_ge(tr_in_psum, n + 1)
                src = tr_bank[n % 2][0:rows, 0:width]
                src = src.rearrange("p (c s) -> p c s", s=P)
                if gain is None:
                    ins = nc.vector.tensor_copy(dst, src)
                else:
                    blocks = width // P
                    ins = nc.vector.tensor_tensor(dst, src, gain.rearrange("p (c a) -> p c a", a=1).to_broadcast(
                        [P, blocks, P]), ALU.mult)
                ins.then_inc(tr_in_sbuf, 1)
                tr[0] += 1

            def drain_xt(gains=None, tiles=range(TILES)):
                for tile in tiles:
                    for half in range(2):
                        g = None if gains is None else gain_cols[:, gains + 4 * half:gains + 4 * half + 4]
                        drain(xt[:, 4 * half:4 * half + 4, tile * P:tile * P + P], g)

            dve.wait_ge(consts_landed, 16)
            nc.vector.tensor_copy(ident_b[:], ident)
            nc.vector.tensor_copy(causal_b[:], const("causal")).then_inc(masks_cast, 1)
            dve.wait_ge(small_landed, 64)
            for k in range(2):
                g = head_gain[:, HD * k:HD * k + HD]
                pairs = g.rearrange("p (d two) -> p d two", two=2)
                scale = HD ** -0.5 if k == 0 else 1.0
                for tile in range(TILES):
                    at = slice(HD * tile, HD * tile + HD)
                    cos, sin = const("cos_g")[:, at], const("sin_g")[:, at].rearrange("p (d two) -> p d two", two=2)
                    nc.vector.scalar_tensor_tensor(rope_g[:, 2 * k, at], cos, scale, g, ALU.mult, ALU.mult)
                    for x in range(2):
                        dst = rope_g[:, 2 * k + 1, at].rearrange("p (d two) -> p d two", two=2)[:, :, x]
                        last = nc.vector.scalar_tensor_tensor(dst, sin[:, :, x], scale, pairs[:, :, 1 - x],
                                                              ALU.mult, ALU.mult)
            link(last)

            dve.wait_ge(tr_in_psum, 1)
            nc.vector.tensor_copy(gain_cols[:], tr_bank[0][:, 0:GAIN_ROWS]).then_inc(tr_in_sbuf, 1)
            tr[0] += 1
            dve.wait_ge(tr_in_sbuf, 1)
            drain_xt()

            dve.wait_ge(sumsq_done, 2)
            dve.wait_ge(proj_in_sbuf, JOB["mla_w_in", 1, 1] + 1)
            v = variances("mla").rearrange("p (t n) -> p t n", n=2)
            ss = small[:, 0:6].rearrange("p (t n) -> p t n", n=3)
            link(nc.vector.tensor_tensor(small[:, 6:8], ss[:, :, 0], ss[:, :, 1], ALU.add))
            link(nc.vector.tensor_scalar(v[:, :, 0], small[:, 6:8], 1 / Q_LORA, RMS_EPS, ALU.mult, ALU.add))
            ask("mla", nc.vector.tensor_scalar(v[:, :, 1], ss[:, :, 2], 1 / KV_LORA, RMS_EPS, ALU.mult, ALU.add))
            r = rsqrt("mla")
            for tile in range(TILES):
                nc.vector.tensor_scalar(wide[:, tile, 0:Q_LORA], wide[:, tile, 0:Q_LORA],
                                        r[:, 2 * tile:2 * tile + 1], None, ALU.mult)
                nc.vector.tensor_scalar(wide[:, tile, Q_LORA:D], wide[:, tile, Q_LORA:D],
                                        r[:, 2 * tile + 1:2 * tile + 2], None, ALU.mult).then_inc(latents_normed, 1)
            dve.wait_ge(proj_in_sbuf, JOB["mla_w_in", 2, 1] + 1)

            def rope_a(x, heads, tile, out):
                half = ROPE // 2
                cos = const("cos_a")[:, ROPE * tile:ROPE * tile + ROPE]
                sin = const("sin_a")[:, ROPE * tile:ROPE * tile + ROPE]

                def over_heads(a):
                    return a.rearrange("p (h d) -> p h d", h=1).to_broadcast([P, heads, a.shape[-1]])

                c = tmp[:, 0, 0:heads * ROPE].rearrange("p (h d) -> p h d", h=heads)
                s = tmp[:, 1, 0:heads * ROPE].rearrange("p (h d) -> p h d", h=heads)
                nc.vector.tensor_tensor(c, x, over_heads(cos), ALU.mult)
                nc.vector.tensor_tensor(s[:, :, 0:half], x[:, :, half:ROPE], over_heads(sin[:, 0:half]), ALU.mult)
                link(nc.vector.tensor_tensor(s[:, :, half:ROPE], x[:, :, 0:half], over_heads(sin[:, half:ROPE]),
                                             ALU.mult))
                return nc.vector.tensor_tensor(out, c, s, ALU.add)

            key_rope = small[:, 64:64 + TILES * ROPE].rearrange("p (t d) -> p t d", t=TILES)
            for tile in range(TILES):
                x = z_in[:, tile, :].rearrange("p (h d) -> p h d", h=1)
                link(rope_a(x, 1, tile, key_rope[:, tile:tile + 1, :]))
            drain_xt(GAIN_Q)

            def q_a_rope(n):
                b, tile = n // TILES, n % TILES
                dve.wait_ge(proj_in_sbuf, JOB["mla_w_uq", b, tile] + 1)
                x = stage[:, n % 4, 0:4 * QKD].rearrange("p (h d) -> p h d", h=4)[:, :, NOPE:QKD]
                rope_a(x, 4, tile, x).then_inc(heads_roped, 1)
                dve.wait_ge(heads_roped, n + 1)

            def heads_out(dst, n, per, rows):
                b, tile = n // TILES, n % TILES
                drain(dst[0:rows, per * b:per * b + per, tile * P:tile * P + P], rows=rows, width=per * P)

            for n in range(8 + LAG):
                if n < 8:
                    q_a_rope(n)
                if n >= LAG:
                    heads_out(q_a, n - LAG, 4, QKD)
            for i in range(4):
                last = nc.vector.tensor_copy(
                    stage[:, i, 0:4 * QKD].rearrange("p (h d) -> p h d", h=4)[:, :, NOPE:QKD],
                    key_rope[:, i % 2:i % 2 + 1, :].to_broadcast([P, 4, ROPE]))
            last.then_inc(key_rope_placed, 1)
            for n in range(8):
                heads_out(k_a, n, 4, QKD)

            row_sum = small[:, 256:256 + 80]
            neg_max = small[:, 336:336 + 80]
            inverse = small[:, 416:416 + 80]

            def attention(kind, units, depth, out_of):
                for u in range(units + depth + 1):
                    if u < units:
                        n = UNIT0[kind] + u
                        dve.wait_ge(scores_in_psum, n + 1)
                        nc.vector.tensor_reduce(neg_max[:, n:n + 1], score_bank[u % 4][:, 0:keys_of(kind, u % TILES)],
                                                AX.X, ALU.max, negate=True).then_inc(max_done, 1)
                    m = u - depth
                    if 0 <= m < units:
                        keys = keys_of(kind, m % TILES)
                        drain(probs_t[:, m % 2, 0:keys].rearrange("p (c s) -> p c s", s=P), width=keys)
                    m = u - depth - 1
                    if m >= 0 and (m // TILES) % 8 == 7:
                        group, tile = m // (8 * TILES), m % TILES
                        first = UNIT0[kind] + group * 8 * TILES + tile
                        sums = row_sum[:, first:first + 8 * TILES].rearrange("p (h t) -> p h t", t=TILES)[:, :, 0] \
                            if tile == 0 else row_sum[:, first - 1:first - 1 + 8 * TILES].rearrange(
                                "p (h t) -> p h t", t=TILES)[:, :, 1]
                        inv = inverse[:, 8 * tile:8 * tile + 8]
                        dve.wait_ge(probs_done, UNIT0[kind] + m + 1)
                        link(nc.vector.reciprocal(inv, sums))
                        dve.wait_ge(out_in_psum, OUT0[kind] + group * TILES + tile + 1)
                        dst = out_of(tile, group)
                        link_out = nc.vector.tensor_tensor(
                            dst.rearrange("p (h d) -> p h d", h=8),
                            out_bank[tile][:].rearrange("p (h d) -> p h d", h=8),
                            inv.rearrange("p (h a) -> p h a", a=1).to_broadcast([P, 8, HD]), ALU.mult)
                        link_out.then_inc(out_drained, 1)
                        dve.wait_ge(out_drained, OUT0[kind] + group * TILES + tile + 1)
                        if kind != "g":
                            g = gate[:, tile, 512 * group:512 * group + 512]
                            nc.vector.tensor_tensor(dst, dst, g, ALU.mult).then_inc(mixed_ready, 1)

            def half_of(tile, group):
                return wide[:, tile, 512 * group:512 * group + 512]

            attention("a", UNITS_A, 3, half_of)
            drain_xt()

            def post_norm(layer, name):
                stats = small[:, 128:140].rearrange("p (c s) -> p c s", c=2)
                for tile in range(TILES):
                    dve.wait_ge(proj_in_sbuf, JOB[name, 1, tile] + 1)
                    link(nc.vector.scalar_tensor_tensor(res[:, tile, :], res[:, tile, :], ALPHA, wide[:, tile, :],
                                                        ALU.mult, ALU.add))
                    nc.vector.bn_stats(stats[:, 0, :], res[:, tile, 0:512])
                    link(nc.vector.bn_stats(stats[:, 1, :], res[:, tile, 512:1024]))
                    link(nc.vector.bn_aggr(small[:, 140:142], small[:, 128:140]))
                    rs = f"ln{layer}t{tile}"
                    ask(rs, nc.vector.tensor_scalar(variances(rs), small[:, 141:142], LN_EPS, None, ALU.add))
                    r = rsqrt(rs)
                    link(nc.vector.tensor_scalar(res[:, tile, :], res[:, tile, :], small[:, 140:141], r,
                                                 ALU.subtract, ALU.mult))
                    if tile == 0:
                        dve.wait_ge(ln_landed, 32 * (layer + 1))
                    link(nc.vector.tensor_tensor(res[:, tile, :], res[:, tile, :], ln_row[:, 0, :], ALU.mult))
                    nc.vector.tensor_tensor(res[:, tile, :], res[:, tile, :], ln_row[:, 1, :], ALU.add).then_inc(
                        res_ready, 1)
                    dve.wait_ge(res_ready, 2 * layer + tile + 1)
                    if tile == 0 and layer == 0:
                        drain_xt(tiles=[0])
                nc.vector.memset(small[:, 142:143], 0.0).then_inc(ln_used, 1)
                if layer == 0:
                    dve.wait_ge(ln_used, 1)
                    drain_xt(tiles=[1])

            post_norm(0, "mla_w_o")

            def rope_b(x, tile, heads, cos, sin, swap, n):
                def over_heads(a):
                    return a.rearrange("p (h d) -> p h d", h=1).to_broadcast([P, heads, HD])

                def split(a):
                    a = a.rearrange("p (h d) -> p h d", h=heads)
                    if swap == "halves":
                        return a[:, :, 0:HD // 2], a[:, :, HD // 2:HD]
                    a = a.rearrange("p h (d two) -> p h d two", two=2)
                    return a[:, :, :, 0], a[:, :, :, 1]

                width = heads * HD
                c, s = tmp[:, 0, 0:width], tmp[:, 1, 0:width]
                x0, x1 = split(x)
                s0, s1 = split(s)
                nc.vector.tensor_tensor(c.rearrange("p (h d) -> p h d", h=heads),
                                        x.rearrange("p (h d) -> p h d", h=heads), over_heads(cos), ALU.mult)
                sin3 = over_heads(sin)
                if swap == "halves":
                    w0, w1 = sin3[:, :, 0:HD // 2], sin3[:, :, HD // 2:HD]
                else:
                    w = sin.rearrange("p (h d two) -> p h d two", h=1, two=2)
                    w0 = w[:, :, :, 0].to_broadcast([P, heads, HD // 2])
                    w1 = w[:, :, :, 1].to_broadcast([P, heads, HD // 2])
                nc.vector.tensor_tensor(s0, x1, w0, ALU.mult)
                link(nc.vector.tensor_tensor(s1, x0, w1, ALU.mult))
                return nc.vector.tensor_tensor(x, c, s, ALU.add)

            def heads_b(name, base, dst):
                for n in range(4):
                    b, tile = n // TILES, n % TILES
                    dve.wait_ge(proj_in_sbuf, JOB[name, b, tile] + 1)
                    rope_b(stage[:, n, :], tile, 8, const("cos_b")[:, HD * tile:HD * tile + HD],
                           const("sin_b")[:, HD * tile:HD * tile + HD], "halves", n).then_inc(heads_roped, 1)
                    dve.wait_ge(heads_roped, base + n + 1)
                for n in range(4):
                    heads_out(dst, n, 4, P)

            heads_b("moba_w_kv", 8, k_b)
            heads_b("moba_w_in", 12, q_b)
            attention("b", UNITS_B, 3, half_of)
            drain_xt()
            nc.vector.memset(up_w, 0.0).then_inc(up_zeroed, 1)
            post_norm(1, "moba_w_o")

            def rms_of_stream(name, first_ready):
                for tile in range(TILES):
                    rs = f"{name}t{tile}"
                    dve.wait_ge(sumsq_done, first_ready + tile + 1)
                    ask(rs, nc.vector.tensor_scalar(variances(rs), small[:, 16 + first_ready + tile:17 + first_ready + tile],
                                                    1 / D, RMS_EPS, ALU.mult, ALU.add))
                    yield tile, rsqrt(rs)

            for tile, r in rms_of_stream("norm1", 2):
                nc.vector.tensor_scalar(wide[:, tile, :], res[:, tile, :], r, None, ALU.mult).then_inc(normed_ready, 1)
                drain_xt(GAIN_N1, [tile])

            nc.vector.memset(masked, 0.0)
            for tile in range(TILES):
                drain(gla_t[:, :, tile * P:tile * P + P])
            nc.vector.memset(z_t[32:33, :], 1.0)
            for tile in range(TILES):
                drain(z_t[0:32, tile * P:tile * P + P].rearrange("p (c s) -> p c s", s=P), rows=32, width=P)
            for tile in range(TILES):
                dve.wait_ge(decay_log, tile + 1)
                nc.vector.scalar_tensor_tensor(decay[:, tile, :], out_bank[tile][:], 0.0,
                                               probs[:, 2 * tile:2 * tile + 2, :].rearrange("p a b -> p (a b)"),
                                               ALU.min, ALU.subtract).then_inc(decay_ready, 1)
            dve.wait_ge(proj_in_sbuf, JOB["w_in_2", 4, 1] + 1)
            v = variances("qk")
            for tile in range(TILES):
                q, k = att_q[:, tile, :], att_kv[:, tile, 0:128]
                nc.vector.tensor_tensor(tmp[:, tile, 0:512], q, q, ALU.mult)
                link(nc.vector.tensor_tensor(tmp[:, tile, 512:640], k, k, ALU.mult))
                link(nc.vector.tensor_reduce(v[:, 10 * tile:10 * tile + 10],
                                             tmp[:, tile, 0:640].rearrange("p (h d) -> p h d", h=10), AX.X, ALU.add))
            ask("qk", nc.vector.tensor_scalar(v, v, 1 / HD, RMS_EPS, ALU.mult, ALU.add))
            r = rsqrt("qk")
            for tile in range(TILES):
                at = slice(HD * tile, HD * tile + HD)
                for x, heads, first, k in ((att_q[:, tile, :], QH, 0, 0), (att_kv[:, tile, 0:128], KVH, QH, 2)):
                    x3 = x.rearrange("p (h d) -> p h d", h=heads)
                    link(nc.vector.tensor_tensor(x3, x3, r[:, 10 * tile + first:10 * tile + first + heads].rearrange(
                        "p (h a) -> p h a", a=1).to_broadcast([P, heads, HD]), ALU.mult))
                    link(rope_b(x, tile, heads, rope_g[:, k, at], rope_g[:, k + 1, at], "pairs", 0))
                for kv in range(KVH):
                    last = nc.vector.tensor_copy(
                        key2[:, tile, 128 * kv:128 * kv + 128].rearrange("p (c d) -> p c d", c=2),
                        att_kv[:, tile, HD * kv:HD * kv + HD].rearrange("p (c d) -> p c d", c=1).to_broadcast(
                            [P, 2, HD]))
                last.then_inc(gqa_ready, 1)
            for tile in range(TILES):
                drain(q_g[:, :, tile * P:tile * P + P])
            for tile in range(TILES):
                drain(k_g[:, :, tile * P:tile * P + P], width=2 * P)

            for n, (tile, way) in enumerate([(i, j) for i in range(TILES) for j in range(2)]):
                at = slice(tile * P, tile * P + P)
                dve.wait_ge(cum_exp, n + 1)
                nc.vector.tensor_tensor(q_in[:, way, :, at], exp_b[:, way, :, at], gla_t[:, 0:2, at], ALU.mult)
                nc.vector.tensor_tensor(exp_q[:, way, :, at], exp_q[:, way, :, at], gla_t[:, 0:2, at], ALU.mult)
                nc.vector.tensor_tensor(exp_k[:, way, :, at], exp_k[:, way, :, at], gla_t[:, 2:4, at], ALU.mult)
                nc.vector.tensor_tensor(k_out[:, tile, way, :], k_out[:, tile, way, :], gla_qk[:, tile, GW:512],
                                        ALU.mult).then_inc(gla_operands, 1)
            dve.wait_ge(gla_operands, 4)
            for n, (way, step) in enumerate(KV_ORDER):
                chunk = step if way == 0 else NCHUNK - 1 - step
                src = score_bank[2 + chunk % 2][:].rearrange("p (a e) -> p a e", a=2)
                dst = state_of(way, step)
                dve.wait_ge(kv_in_psum, n + 1)
                if step == 0:
                    nc.vector.tensor_copy(dst, src).then_inc(state_ready, 1)
                else:
                    last_token = CHUNK * chunk + (CHUNK - 1 if way == 0 else 0)
                    dve.wait_ge(state_ready, n - 1)
                    for pair in range(2):
                        last = nc.vector.scalar_tensor_tensor(
                            dst[:, pair, :], state_of(way, step - 1)[:, pair, :],
                            exp_b[:, way, pair, last_token:last_token + 1], src[:, pair, :], ALU.mult, ALU.add)
                    last.then_inc(state_ready, 1)
            for tile in range(TILES):
                for way in range(2):
                    mask = const("cum_fwd" if way == 0 else "cum_bwd")[:, P:2 * P].bitcast(I32)
                    for odd in range(2):
                        dve.wait_ge(gla_scores, 4 * tile + 2 * way + odd + 1)
                        if tile:
                            dve.wait_ge(gla_intra, tile)
                        dst = masked[:, way, :].rearrange("p (a o s) -> p a o s", a=2, o=2)[:, :, odd, :]
                        src = score_bank[2 + odd][:, 0:2 * P].rearrange("p (a s) -> p a s", a=2)
                        for pair in range(2):
                            last = nc.vector.copy_predicated(dst[:, pair, :], mask, src[:, pair, :])
                        last.then_inc(gla_masked, 1)
                dve.wait_ge(gla_copied, tile + 1)
                dve.wait_ge(gla_inter, tile + 1)
                for odd in range(2):
                    o = wide[:, tile, 0:512].rearrange("p (a o e) -> p a o e", a=2, o=2)[:, :, odd, :]
                    last = nc.vector.tensor_tensor(o, o, out_bank[odd][:, 0:256].rearrange("p (a e) -> p a e", a=2),
                                                   ALU.add)
                last.then_inc(gla_summed, 1)
            dve.wait_ge(gla_summed, 2)
            v = variances("gla")
            for tile in range(TILES):
                link(nc.vector.tensor_tensor(tmp[:, tile, 0:512], wide[:, tile, 0:512], wide[:, tile, 0:512], ALU.mult))
                link(nc.vector.tensor_reduce(v[:, 4 * tile:4 * tile + 4],
                                             tmp[:, tile, 0:512].rearrange("p (h d) -> p h d", h=4), AX.X, ALU.add))
            ask("gla", nc.vector.tensor_scalar(v, v, 1 / GDV, RMS_EPS, ALU.mult, ALU.add))
            r = rsqrt("gla")
            for tile in range(TILES):
                o = wide[:, tile, 0:512].rearrange("p (h d) -> p h d", h=4)
                link(nc.vector.tensor_tensor(o, o, r[:, 4 * tile:4 * tile + 4].rearrange(
                    "p (h a) -> p h a", a=1).to_broadcast([P, 4, GDV]), ALU.mult))
                link(nc.vector.tensor_tensor(wide[:, tile, 0:512], wide[:, tile, 0:512], gate[:, tile, 0:512],
                                             ALU.mult))

            attention("g", UNITS_G, 3, lambda tile, group: wide[:, tile, 512:1024])
            v = variances("att")
            for tile in range(TILES):
                link(nc.vector.tensor_tensor(tmp[:, tile, 0:512], wide[:, tile, 512:1024], wide[:, tile, 512:1024],
                                             ALU.mult))
                link(nc.vector.tensor_reduce(v[:, tile:tile + 1], tmp[:, tile, 0:512], AX.X, ALU.add))
            ask("att", nc.vector.tensor_scalar(v, v, 1 / 512, RMS_EPS, ALU.mult, ALU.add))
            r = rsqrt("att")
            for tile in range(TILES):
                nc.vector.tensor_scalar(wide[:, tile, 512:1024], wide[:, tile, 512:1024], r[:, tile:tile + 1], None,
                                        ALU.mult).then_inc(mixed_ready, 1)
            drain_xt(GAIN_MIX)
            for tile in range(TILES):
                dve.wait_ge(proj_in_sbuf, JOB["w_out_2", 1, tile] + 1)
                nc.vector.tensor_tensor(res[:, tile, :], res[:, tile, :], wide[:, tile, :], ALU.add).then_inc(
                    res_ready, 1)
            for tile, r in rms_of_stream("norm2", 4):
                if tile == 0:
                    dve.wait_ge(row_landed, 64)
                dst = routed[:, tile].rearrange("p c k -> p k c")
                nc.vector.scalar_tensor_tensor(dst, res[:, tile, :].rearrange("p (k c) -> p k c", c=KD), r,
                                               norm2_row.rearrange("p (k c) -> p k c", c=KD),
                                               ALU.mult, ALU.mult).then_inc(routed_ready, 1)
            drain_xt()

            dve.wait_ge(proj_in_sbuf, len(JOBS) + 1)
            logits = small[:, 0:144].rearrange("p (t n) -> p t n", t=TILES)

            def over_tiles(a):
                return a.rearrange("p (t n) -> p t n", t=1).to_broadcast([P, TILES, a.shape[-1]])

            def over(a, n):
                return a.rearrange("p (t n) -> p t n", n=1).to_broadcast([P, TILES, n])

            def view(a, n):
                return tmp[:, 0, a:a + TILES * n].rearrange("p (t n) -> p t n", t=TILES)

            link(nc.vector.tensor_tensor(logits, logits, over_tiles(router_b[:]), ALU.add))
            scal = small[:, 160:180]
            g_log, e_log = logits[:, :, 0:NG], logits[:, :, NG:]

            def first_max(x, n, top, is_top, work, best, out):
                link(nc.vector.tensor_reduce(top, x, AX.X, ALU.max))
                link(nc.vector.tensor_tensor(is_top, x, over(top, n), ALU.is_equal))
                link(nc.vector.tensor_tensor(work, is_top, over_tiles(const("desc")[:, NE - n:NE]), ALU.mult))
                link(nc.vector.tensor_reduce(best, work, AX.X, ALU.max))
                link(nc.vector.tensor_tensor(out, work, over(best, n), ALU.is_equal))

            g_top, g_best = scal[:, 0:2], scal[:, 2:4]
            g_is, g_work, g_hot = view(0, NG), view(16, NG), view(32, NG)
            first_max(g_log, NG, g_top, g_is, g_work, g_best, g_hot)
            nc.vector.tensor_tensor(view(48, NG), g_log, over(g_top, NG), ALU.subtract).then_inc(mask_ready, 1)
            g_low = view(64, NG)
            link(nc.vector.tensor_scalar(g_low, g_hot, -1.0, BIG, ALU.add, ALU.mult))
            for tile in range(TILES):
                e3 = e_log[:, tile, :].rearrange("p (g e) -> p g e", g=NG)
                last = nc.vector.tensor_tensor(e3, e3, g_low[:, tile, :].rearrange("p (g a) -> p g a", a=1).to_broadcast(
                    [P, NG, EPG]), ALU.add)
            link(last)
            e_is, e_work = view(128, NE), view(256, NE)
            hot1, hot2 = view(384, NE), view(512, NE)
            top1, top2, best1, best2 = (scal[:, 4 + 2 * i:6 + 2 * i] for i in range(4))
            first_max(e_log, NE, top1, e_is, e_work, best1, hot1)
            e2 = view(640, NE)
            link(nc.vector.scalar_tensor_tensor(e2, hot1, -2 * BIG, e_log, ALU.mult, ALU.add))
            first_max(e2, NE, top2, e_is, e_work, best2, hot2)
            nc.vector.tensor_tensor(top_diff, top2, top1, ALU.subtract).then_inc(mask_ready, 1)
            mask = view(768, NE)
            nc.vector.tensor_tensor(mask, hot1, hot2, ALU.add).then_inc(mask_ready, 1)
            dve.wait_ge(gates_exp, 2)
            g_sum = small[:, 180:182]
            link(nc.vector.tensor_reduce(g_sum, g_exp.rearrange("p (t n) -> p t n", t=TILES), AX.X, ALU.add))
            link(nc.vector.tensor_scalar(scal[:, 14:16], ratio, 1.0, None, ALU.add))
            link(nc.vector.tensor_tensor(scal[:, 16:18], scal[:, 14:16], g_sum, ALU.mult))
            link(nc.vector.reciprocal(scal[:, 16:18], scal[:, 16:18]))
            link(nc.vector.tensor_tensor(scal[:, 18:20], scal[:, 16:18], ratio, ALU.mult))
            nc.vector.tensor_tensor(hot1, hot1, over(scal[:, 16:18], NE), ALU.mult)
            link(nc.vector.tensor_tensor(hot2, hot2, over(scal[:, 18:20], NE), ALU.mult))
            link(nc.vector.tensor_tensor(gates[:], hot1, hot2, ALU.add))
            dve.wait_ge(ranks_in_psum, 1)
            dve.wait_ge(mask_ready, 3)
            link(nc.vector.tensor_tensor(rank[:], proj_bank[1][:, 0:2 * NE].rearrange("p (t n) -> p t n", t=TILES),
                                         mask, ALU.mult))
            link(nc.vector.tensor_scalar(rank[:], rank[:], -1.0, None, ALU.add))
            link(nc.vector.tensor_reduce(small[:, 182:183], proj_bank[1][:, 2 * NE:3 * NE], AX.X, ALU.max))
            nc.vector.tensor_copy(largest[:], small[:, 182:183]).then_inc(routing_ready, 1)

            def expert_rounds(rounds, base):
                with dve.Fori(0, rounds) as r:
                    n = base + r
                    for tile in range(TILES):
                        nc.vector.tensor_tensor(
                            onehot[:, tile, :].rearrange("p (e s) -> p e s", e=GROUP),
                            const("iota").rearrange("p (e s) -> p e s", e=1).to_broadcast([P, GROUP, SLOTS]),
                            rank[:, tile, bass.ds(GROUP * r, GROUP)].rearrange("p (e s) -> p e s", s=1).to_broadcast(
                                [P, GROUP, SLOTS]), ALU.is_equal).then_inc(onehot_ready, 1)
                    dve.wait_ge(onehot_ready, 3 * n + 2)
                    for tile in range(TILES):
                        last = nc.vector.tensor_tensor(
                            weighted[:, tile, :].rearrange("p (e s) -> p e s", e=GROUP),
                            onehot[:, tile, :].rearrange("p (e s) -> p e s", e=GROUP),
                            gates[:, tile, bass.ds(GROUP * r, GROUP)].rearrange("p (e s) -> p e s", s=1).to_broadcast(
                                [P, GROUP, SLOTS]), ALU.mult)
                    last.then_inc(onehot_ready, 1)
                    dve.wait_ge(back_in_psum, n + 1)
                    nc.vector.tensor_copy(back, bank[3][:, 0:256]).then_inc(back_ready, 1)
                    for i in range(GROUP):
                        x = GROUP * n + i
                        dve.wait_ge(silu_done, x + 1)
                        nc.vector.tensor_tensor(hidden, act_g, bank[2][:, P:2 * P], ALU.mult).then_inc(hidden_ready, 1)
                        dve.wait_ge(hidden_t_in_psum, x + 1)
                        nc.vector.tensor_copy(hidden_t, bank[3][:, 256:384]).then_inc(hidden_t_ready, 1)
                        dve.wait_ge(down_in_psum, x + 1)
                        nc.vector.tensor_copy(expert_out[SLOTS * i:SLOTS * i + SLOTS, 512:768], bank[4][64:96, 0:256])
                        nc.vector.tensor_copy(expert_out[SLOTS * i:SLOTS * i + SLOTS, 768:1024],
                                              bank[4][96:128, 0:256]).then_inc(down_drained_dve, 1)
                    for k in range(4):
                        tile, half = k // 2, k % 2
                        dve.wait_ge(sum_in_psum, 4 * n + (k + 1))
                        dst = res[:, tile, 512 * half:512 * half + 512]
                        nc.vector.tensor_tensor(dst, dst, bank[5 + k % 3][:], ALU.add).then_inc(sum_added, 1)

            expert_rounds(ROUNDS, 0)
            dve.wait_ge(sum_added, 4 * ROUNDS)
            most = dve.value_load(largest[0:1, 0:1], min_val=0, max_val=SEQ)
            with dve.If(most > SLOTS):
                with dve.Fori(1, PASSES) as p:
                    dve.wait_ge(onehot_ready, 3 * ROUNDS * p)
                    nc.vector.tensor_scalar(rank[:], rank[:], -float(SLOTS), None, ALU.add).then_inc(rank_moved, 1)
                    dve.wait_ge(rank_moved, p)
                    nc.vector.memset(small[:, 150:151], 0.0)
                    expert_rounds(ROUNDS, ROUNDS * p)
                dve.wait_ge(sum_added, 4 * ROUNDS * PASSES)

            for tile in range(TILES):
                nc.vector.memset(small[:, 150 + tile:151 + tile], 0.0).then_inc(res_ready, 1)
            for tile, r in rms_of_stream("final", 6):
                nc.vector.scalar_tensor_tensor(wide[:, tile, :], res[:, tile, :], r, final_row, ALU.mult,
                                               ALU.mult).then_inc(out_ready, 1)

        @block.tensor
        def _(pe):
            tr = [0]

            def transposes(blocks):
                n = tr[0]
                if n >= 2:
                    pe.wait_ge(tr_in_sbuf, n - 1)
                for i, x in enumerate(blocks):
                    rows, cols = x.shape[0], x.shape[-1]
                    last = nc.tensor.transpose(tr_bank[n % 2][0:cols, P * i:P * i + rows], x, ident[0:rows, 0:rows])
                last.then_inc(tr_in_psum, 1)
                tr[0] += 1

            def transpose_rows(src, tile, half):
                transposes([src[:, tile, P * c:P * c + P] for c in range(4 * half, 4 * half + 4)])

            landed = set()

            def project(job, chunks=None):
                n = JOB[job]
                name, part, tile = job
                b = block_of(job)
                _, kc, _, width = BLOCKS[b]
                w = ring[:, b % RING, 0:kc * width].rearrange("p (c n) -> p c n", c=kc)
                if name == "mla_w_ukv":
                    w = w[:, :, 512 * part:512 * part + 512]
                    width = 512
                if b not in landed:
                    landed.add(b)
                    pe.wait_ge(block_landed[b % RING], 16 * (b // RING + 1))
                if n >= 2:
                    pe.wait_ge(proj_in_sbuf, n - 1)
                first = 6 if name == "mla_w_ukv" else 0
                for c in range(kc):
                    last = nc.tensor.matmul(proj_bank[n % 2][:, 0:width], xt[:, first + c, tile * P:tile * P + P],
                                            w[:, c, :], start=(c == 0), stop=(c == kc - 1))
                last.then_inc(proj_in_psum, 1)

            def xt_ready():
                pe.wait_ge(tr_in_sbuf, tr[0])

            def attention(kind, units, depth, scores, values):
                for u in range(units + depth + 1):
                    if u < units:
                        n = UNIT0[kind] + u
                        h, tile = u // TILES, u % TILES
                        keys = keys_of(kind, tile)
                        if u >= 4:
                            pe.wait_ge(probs_done, n - 3)
                        lhs, rhs = scores(h, tile, keys)
                        causal = kind != "g"
                        last = nc.tensor.matmul(score_bank[u % 4][:, 0:keys], lhs, rhs, start=True, stop=not causal)
                        if causal:
                            last = nc.tensor.matmul(score_bank[u % 4][:, keys - P:keys], ident_b[:], causal_b[:],
                                                    start=False, stop=True)
                        last.then_inc(scores_in_psum, 1)
                    m = u - depth
                    if 0 <= m < units:
                        pe.wait_ge(probs_done, UNIT0[kind] + m + 1)
                        transposes([probs[:, m % 4, P * k:P * k + P] for k in range(keys_of(kind, m % TILES) // P)])
                    m = u - depth - 1
                    if m >= 0:
                        h, tile = m // TILES, m % TILES
                        group = h // 8
                        pe.wait_ge(tr_in_sbuf, TR["att_" + kind] + m + 1)
                        if h % 8 == 0 and group:
                            pe.wait_ge(out_drained, OUT0[kind] + tile + 1)
                        blocks = keys_of(kind, tile) // P
                        for k in range(blocks):
                            last = nc.tensor.matmul(out_bank[tile][:, HD * (h % 8):HD * (h % 8) + HD],
                                                    probs_t[:, m % 2, P * k:P * k + P], values(h, k),
                                                    start=(k == 0), stop=(k == blocks - 1))
                        if h % 8 == 7:
                            last.then_inc(out_in_psum, 1)

            pe.wait_ge(consts_landed, 16)
            pe.wait_ge(gains_landed, 128)
            transposes([gain_rows])
            pe.wait_ge(x_landed, 16)
            for tile in range(TILES):
                for half in range(2):
                    transpose_rows(res, tile, half)
            xt_ready()
            for b in range(5):
                for tile in range(TILES):
                    project(("mla_w_in", b, tile))
            for tile in range(TILES):
                pe.wait_ge(latents_normed, tile + 1)
                for half in range(2):
                    transpose_rows(wide, tile, half)
            xt_ready()

            def staged_heads(n, width):
                return [stage[:, n % 4, width * i:width * i + width] for i in range(4)]

            for n in range(8 + LAG):
                if n < 8:
                    project(("mla_w_uq", n // TILES, n % TILES))
                if n >= LAG:
                    pe.wait_ge(heads_roped, n - LAG + 1)
                    transposes(staged_heads(n - LAG, QKD))
            for n in range(8 + LAG):
                if n < 8:
                    project(("mla_w_ukv", n // TILES, n % TILES))
                if n >= LAG:
                    m = n - LAG
                    pe.wait_ge(proj_in_sbuf, JOB["mla_w_ukv", m // TILES, m % TILES] + 1)
                    transposes(staged_heads(m, QKD))
            xt_ready()
            pe.wait_ge(proj_in_sbuf, JOB["mla_w_ukv", 3, 1] + 1)
            pe.wait_ge(masks_cast, 1)

            def scores_a(h, tile, keys):
                return q_a[0:QKD, h, tile * P:tile * P + P], k_a[0:QKD, h, 0:keys]

            def values_ab(h, k):
                return val[:, k, HD * h:HD * h + HD]

            attention("a", UNITS_A, 3, scores_a, values_ab)

            def output_projection(name, mixed_before):
                for tile in range(TILES):
                    for half in range(2):
                        pe.wait_ge(mixed_ready, mixed_before + 2 * half + tile + 1)
                        transpose_rows(wide, tile, half)
                xt_ready()
                for tile in range(TILES):
                    for b in range(2):
                        project((name, b, tile))

            output_projection("mla_w_o", 0)

            def first_jobs(name, src, ready, before):
                for tile in range(TILES):
                    pe.wait_ge(ready, before + tile + 1)
                    for half in range(2):
                        transpose_rows(src, tile, half)
                    xt_ready()
                    project((name, 0, tile))

            first_jobs("moba_w_kv", res, res_ready, 0)

            def heads_back(n, roped):
                pe.wait_ge(heads_roped, roped + n + 1)
                transposes(staged_heads(n, P))

            for n in range(2, 8):
                project(("moba_w_kv", n // TILES, n % TILES))
                if 0 <= n - 3 < 4:
                    heads_back(n - 3, 8)
            for n in range(8):
                project(("moba_w_in", n // TILES, n % TILES))
                if 0 <= n - 3 < 4:
                    heads_back(n - 3, 12)
            xt_ready()
            pe.wait_ge(proj_in_sbuf, JOB["moba_w_in", 3, 1] + 1)

            def scores_b(h, tile, keys):
                at = slice(HD * (h % 2), HD * (h % 2) + HD)
                return q_b[at, h // 2, tile * P:tile * P + P], k_b[at, h // 2, 0:keys]

            attention("b", UNITS_B, 3, scores_b, values_ab)
            output_projection("moba_w_o", 4)

            first_jobs("w_in_2", wide, normed_ready, 0)
            for n in range(2, 10):
                project(("w_in_2", n // TILES, n % TILES))
                if n == 3:
                    for tile in range(TILES):
                        pe.wait_ge(proj_in_sbuf, JOB["w_in_2", 0, tile] + 1)
                        transposes([gla_qk[:, tile, P * c:P * c + P] for c in range(4)])
                if n == 8:
                    for tile in range(TILES):
                        pe.wait_ge(proj_in_sbuf, JOB["w_in_2", 3, tile] + 1)
                        transposes([z_in[:, tile, :]])
            xt_ready()
            pe.wait_ge(up_landed, 64)
            for tile in range(TILES):
                nc.tensor.matmul(out_bank[tile][:], z_t[0:33, tile * P:tile * P + P], up_w, start=True,
                                 stop=True).then_inc(decay_in_psum, 1)
            for n, (tile, way) in enumerate([(i, j) for i in range(TILES) for j in range(2)]):
                pe.wait_ge(decay_ready, tile + 1)
                if n == 0:
                    pe.wait_ge(proj_in_sbuf, JOB["w_in_2", 4, 1] + 1)
                if n >= 2:
                    pe.wait_ge(cum_exp, n - 1)
                name = "fwd" if way == 0 else "bwd"
                for pair in range(2):
                    nc.tensor.matmul(score_bank[n % 2][:, 256 * pair:256 * pair + 256],
                                     decay[:, tile, GW * way + P * pair:GW * way + P * pair + P],
                                     const("cum_" + name), start=True, stop=True)
                nc.tensor.matmul(score_bank[2 + n % 2][:, 0:GW], const("rest_" + name),
                                 decay[:, tile, GW * way:GW * way + GW], start=True, stop=True).then_inc(
                    cum_in_psum, 1)
            for tile in range(TILES):
                pe.wait_ge(gqa_ready, tile + 1)
                transposes([att_q[:, tile, P * c:P * c + P] for c in range(4)])
            for tile in range(TILES):
                transposes([key2[:, tile, P * c:P * c + P] for c in range(KVH)])
            pe.wait_ge(gla_operands, 4)
            for n, (way, step) in enumerate(KV_ORDER):
                chunk = step if way == 0 else NCHUNK - 1 - step
                tile, rows = chunk // 2, slice(CHUNK * (chunk % 2), CHUNK * (chunk % 2) + CHUNK)
                if n >= 2:
                    pe.wait_ge(state_ready, n)
                for pair in range(2):
                    last = nc.tensor.matmul(score_bank[2 + chunk % 2][:, 256 * pair:256 * pair + 256],
                                            k_out[rows, tile, way, P * pair:P * pair + P],
                                            val[rows, tile, 256 * pair:256 * pair + 256], start=True, stop=True)
                last.then_inc(kv_in_psum, 1)
            pe.wait_ge(state_ready, len(KV_ORDER))
            for tile in range(TILES):
                at = slice(tile * P, tile * P + P)
                for way in range(2):
                    for odd in range(2):
                        j = 4 * tile + 2 * way + odd
                        rows = slice(GDK * odd, GDK * odd + GDK)
                        if j >= 2:
                            pe.wait_ge(gla_masked, j - 1)
                        for pair in range(2):
                            last = nc.tensor.matmul(score_bank[2 + odd][:, P * pair:P * pair + P],
                                                    exp_k[rows, way, pair, at], exp_q[rows, way, pair, at],
                                                    start=True, stop=True)
                        last.then_inc(gla_scores, 1)
                if tile:
                    pe.wait_ge(gla_summed, tile)
                for h in range(GH):
                    pair, odd = h // 2, h % 2
                    rows = slice(GDK * odd, GDK * odd + GDK)
                    for j in range(2):
                        chunk = 2 * tile + j
                        ways = [(0, chunk - 1)] * (chunk > 0) + [(1, NCHUNK - 2 - chunk)] * (chunk < NCHUNK - 1)
                        for k, (way, step) in enumerate(ways):
                            last = nc.tensor.matmul(
                                out_bank[odd][CHUNK * j:CHUNK * j + CHUNK, GDV * pair:GDV * pair + GDV],
                                q_in[rows, way, pair, CHUNK * chunk:CHUNK * chunk + CHUNK],
                                state_of(way, step)[rows, pair, GDV * odd:GDV * odd + GDV],
                                start=(k == 0), stop=(k == len(ways) - 1))
                last.then_inc(gla_inter, 1)
                pe.wait_ge(gla_masked, 4 * tile + 4)
                if tile:
                    pe.wait_ge(gla_copied, tile)
                for h in range(GH):
                    for way in range(2):
                        last = nc.tensor.matmul(score_bank[1][:, GDV * h:GDV * h + GDV],
                                                masked[:, way, P * h:P * h + P],
                                                val[:, tile, GDV * h:GDV * h + GDV],
                                                start=(way == 0), stop=(way == 1))
                last.then_inc(gla_intra, 1)
            pe.wait_ge(gla_summed, 2)

            def scores_g(h, tile, keys):
                at = slice(HD * (h % 2), HD * (h % 2) + HD)
                return q_g[at, h // 2, tile * P:tile * P + P], k_g[at, h // (QH // KVH), 0:keys]

            attention("g", UNITS_G, 3, scores_g,
                      lambda h, k: att_kv[:, k, 128 + HD * (h // (QH // KVH)):128 + HD * (h // (QH // KVH)) + HD])
            for tile in range(TILES):
                pe.wait_ge(mixed_ready, 8 + tile + 1)
                for half in range(2):
                    transpose_rows(wide, tile, half)
            xt_ready()
            for tile in range(TILES):
                for b in range(2):
                    project(("w_out_2", b, tile))

            for tile in range(TILES):
                pe.wait_ge(routed_ready, tile + 1)
                for half in range(2):
                    transpose_rows(wide, tile, half)
            xt_ready()
            pe.wait_ge(row_landed, 64)
            for tile in range(TILES):
                for c in range(KD):
                    last = nc.tensor.matmul(proj_bank[0][:, 72 * tile:72 * tile + 72], xt[:, c, tile * P:tile * P + P],
                                            router_w[:, c, :], start=(c == 0), stop=(c == KD - 1))
            last.then_inc(logits_in_psum, 1)
            pe.wait_ge(mask_ready, 3)
            mask = tmp[:, 0, 768:768 + 2 * NE]
            for n, (first, second) in enumerate((("tri", None), ("ones", "tri"), ("ones", "ones"))):
                dst = proj_bank[1][:, NE * n:NE * n + NE]
                last = nc.tensor.matmul(dst, const(first), mask[:, 0:NE], start=True, stop=second is None)
                if second:
                    last = nc.tensor.matmul(dst, const(second), mask[:, NE:2 * NE], start=False, stop=True)
            last.then_inc(ranks_in_psum, 1)

            def expert_rounds(rounds, base):
                with pe.Fori(0, rounds) as r:
                    n = base + r
                    pe.wait_ge(onehot_ready, 3 * n + 2)
                    for c in range(KD):
                        for tile in range(TILES):
                            last = nc.tensor.matmul(bank[c // 4][:, P * (c % 4):P * (c % 4) + P],
                                                    routed[:, tile, c, :], onehot[:, tile, :], start=(tile == 0),
                                                    stop=(tile == TILES - 1))
                        if c % 4 == 3:
                            last.then_inc(picked_in_psum, 1)
                    pe.wait_ge(onehot_ready, 3 * n + 3)
                    for tile in range(TILES):
                        last = nc.tensor.transpose(bank[3][:, P * tile:P * tile + P], weighted[:, tile, :], ident)
                    last.then_inc(back_in_psum, 1)
                    pe.wait_ge(picked_ready, 2 * n + 2)
                    for i in range(GROUP):
                        x = GROUP * n + i
                        base_slot = 3 * (i % 2)
                        pe.wait_ge(gate_up_landed[i % 2], 64 * n + (32 * (i // 2) + 32))
                        both = ring[:, base_slot:base_slot + 2, :].rearrange("p m (c f) -> p m c f", c=KD)
                        for c in range(KD):
                            for j in range(4):
                                last = nc.tensor.matmul(bank[2][SLOTS * j:SLOTS * j + SLOTS, 0:256],
                                                        picked[:, c, SLOTS * i:SLOTS * i + SLOTS],
                                                        both[:, :, c, P * j:P * j + P], start=(c == 0),
                                                        stop=(c == KD - 1))
                        last.then_inc(hidden_in_psum, 1)
                        pe.wait_ge(hidden_ready, x + 1)
                        nc.tensor.transpose(bank[3][:, 256:384], hidden, ident).then_inc(hidden_t_in_psum, 1)
                        pe.wait_ge(hidden_t_ready, x + 1)
                        pe.wait_ge(down_landed[i % 2], 32 * n + (16 * (i // 2) + 16))
                        if i:
                            pe.wait_ge(down_drained_act, x)
                            pe.wait_ge(down_drained_dve, x)
                        down = ring[:, base_slot + 2, :].rearrange("p (k d) -> p k d", k=4)
                        for k in range(4):
                            for j in range(4):
                                last = nc.tensor.matmul(bank[4][SLOTS * j:SLOTS * j + SLOTS, 0:256],
                                                        hidden_t[:, SLOTS * k:SLOTS * k + SLOTS],
                                                        down[:, k, 256 * j:256 * j + 256], start=(k == 0),
                                                        stop=(k == 3))
                        last.then_inc(down_in_psum, 1)
                    pe.wait_ge(back_ready, n + 1)
                    pe.wait_ge(down_drained_act, GROUP * n + GROUP)
                    pe.wait_ge(down_drained_dve, GROUP * n + GROUP)
                    for k in range(4):
                        tile, half = k // 2, k % 2
                        if k == 3:
                            pe.wait_ge(sum_added, 4 * n + 1)
                        nc.tensor.matmul(bank[5 + k % 3][:], back[:, P * tile:P * tile + P],
                                         expert_out[:, 512 * half:512 * half + 512], start=True,
                                         stop=True).then_inc(sum_in_psum, 1)

            expert_rounds(ROUNDS, 0)
            most = pe.value_load(largest[0:1, 0:1], min_val=0, max_val=SEQ)
            with pe.If(most > SLOTS):
                with pe.Fori(1, PASSES) as p:
                    expert_rounds(ROUNDS, ROUNDS * p)


def kernel(**inputs):
    import concourse.bacc as bacc
    from concourse.bass_utils import run_bass_kernel_spmd as run

    nc = bacc.Bacc("TRN2", target_bir_lowering=False, num_devices=1)
    arrays = {name: np.ascontiguousarray(a) for name, a in inputs.items()}
    arrays["consts"] = np.concatenate(list(shape_constants().values()), axis=1)
    t = {name: nc.dram_tensor(f"in_{name}", a.shape, F32, kind="ExternalInput").ap() for name, a in arrays.items()}
    t["out"] = nc.dram_tensor("out_0", inputs["x"].shape, F32, kind="ExternalOutput").ap()
    build(nc, t)
    r = run(nc, [{f"in_{name}": a for name, a in arrays.items()}], core_ids=[0])
    return r.results[0]["out_0"]
```

```python
from contextlib import ExitStack

import numpy as np

import concourse.bass as bass
from concourse import mybir

ALU = mybir.AluOpType
ACT = mybir.ActivationFunctionType
AX = mybir.AxisListType
F32 = mybir.dt.float32
BF16 = mybir.dt.bfloat16
I32 = mybir.dt.int32

P = 128
D = 1024
SEQ = 256
TILES = SEQ // P
KD = D // P

H = 16
NOPE, ROPE, VD = 64, 32, 64
QKD = NOPE + ROPE
Q_LORA, KV_LORA = 768, 256
HD = 64
SCALE_A = QKD ** -0.5
SCALE_B = HD ** -0.5
ALPHA = 4 ** 0.25
LN_EPS = 1e-5
RMS_EPS = 1e-6

GH, GDK, GDV = 4, 64, 128
GW = GH * GDK
CHUNK = 64
NCHUNK = SEQ // CHUNK
QH, KVH = 8, 2

NG, EPG = 8, 8
NE = NG * EPG
FE = 512
SLOTS = 32
GROUP = 4
ROUNDS = NE // GROUP
PASSES = SEQ // SLOTS
BIG = 1e30

RING = 6
SLOT = 4096
LAG = 2

BLOCKS = (
    [("mla_w_in", 8, a, n) for a, n in ((0, 512), (512, 512), (1024, 416), (1440, 320), (1760, 320))]
    + [("mla_w_uq", 6, 384 * b, 384) for b in range(4)]
    + [("mla_w_ukv", 2, 0, 2048)]
    + [("mla_w_o", 8, 512 * b, 512) for b in range(2)]
    + [("moba_w_kv", 8, 512 * b, 512) for b in range(4)]
    + [("moba_w_in", 8, 512 * b, 512) for b in range(4)]
    + [("moba_w_o", 8, 512 * b, 512) for b in range(2)]
    + [("w_in_2", 8, a, n) for a, n in ((1536, 416), (1952, 384), (0, 512), (512, 512), (1024, 512))]
    + [("w_out_2", 8, 512 * b, 512) for b in range(2)]
)


JOBS = []
for _name, _n, _tile_outer in (("mla_w_in", 5, 0), ("mla_w_uq", 4, 0), ("mla_w_ukv", 4, 0), ("mla_w_o", 2, 1),
                               ("moba_w_kv", 4, 0), ("moba_w_in", 4, 0), ("moba_w_o", 2, 1),
                               ("w_in_2", 5, 0), ("w_out_2", 2, 1)):
    if _name == "w_in_2":
        JOBS += [(_name, b, t) for t in range(TILES) for b in range(2)]
        JOBS += [(_name, b, t) for b in range(2, _n) for t in range(TILES)]
    elif _tile_outer:
        JOBS += [(_name, b, t) for t in range(TILES) for b in range(_n)]
    else:
        JOBS += [(_name, b, t) for b in range(_n) for t in range(TILES)]
JOB = {job: n for n, job in enumerate(JOBS)}


def block_of(job):
    name, b, _ = job
    first = min(i for i, x in enumerate(BLOCKS) if x[0] == name)
    return first if name == "mla_w_ukv" else first + b


LAST_JOB = [max(n for n, job in enumerate(JOBS) if block_of(job) == b) for b in range(len(BLOCKS))]

KV_ORDER = [(way, step) for step in range(SEQ // 64 - 1) for way in range(2)]

RSQRT = {}
_at = 0
for _n, (_name, _w) in enumerate((("mla", 4), ("ln0t0", 1), ("ln0t1", 1), ("ln1t0", 1), ("norm1t0", 1), ("ln1t1", 1),
                                  ("norm1t1", 1),
                                  ("qk", 20), ("gla", 8), ("att0", 1), ("att1", 1),
                                  ("norm2t0", 1), ("norm2t1", 1), ("finalt0", 1), ("finalt1", 1))):
    RSQRT[_name] = (_n, _at, _w)
    _at += _w
RSQRT_COLS = _at

GAIN_Q, GAIN_N1, GAIN_MIX, GAIN_ROWS = 0, 8, 16, 24


def shape_constants():
    f = np.float32
    tok = np.arange(SEQ, dtype=f)

    def tiled(a):
        return a.reshape(TILES, P, -1).transpose(1, 0, 2).reshape(P, -1)

    def half_tables(dim):
        inv = f(10000.0) ** (-np.arange(0, dim, 2, dtype=f) / f(dim))
        ang = (tok[:, None] * inv[None, :]).astype(f)
        c, s = np.cos(ang), np.sin(ang)
        return tiled(np.concatenate([c, c], 1)), tiled(np.concatenate([-s, s], 1))

    cos_a, sin_a = half_tables(ROPE)
    cos_b, sin_b = half_tables(HD)
    inv = f(10000.0) ** (-np.arange(0, 32, 2, dtype=f) / f(32))
    row, col = np.floor(tok / 64).astype(f), (tok % 64).astype(f)
    ang = np.concatenate([row[:, None] * inv, col[:, None] * inv], 1).astype(f)
    c, s = np.cos(ang), np.sin(ang)
    cos_g = tiled(np.repeat(c, 2, 1))
    sin_g = tiled(np.stack([-s, s], 2).reshape(SEQ, 64))
    i = np.arange(P)
    src, dst = i[:, None], i[None, :]
    same = (src // CHUNK) == (dst // CHUNK)
    fwd, bwd = same & (src <= dst), same & (src >= dst)
    mid_f, mid_b = same & (src % CHUNK <= CHUNK // 2 - 1), same & (src % CHUNK >= CHUNK // 2)
    out = {
        "ident": np.eye(P),
        "ones": np.ones((P, P)),
        "tri": src <= dst,
        "cum_fwd": np.concatenate([fwd.astype(f) - mid_f, fwd], 1),
        "cum_bwd": np.concatenate([bwd.astype(f) - mid_b, bwd], 1),
        "rest_fwd": same & (src > dst),
        "rest_bwd": same & (src < dst),
        "causal": np.where(dst > src, -BIG, 0.0),
        "cos_a": cos_a, "sin_a": sin_a, "cos_b": cos_b, "sin_b": sin_b, "cos_g": cos_g, "sin_g": sin_g,
        "iota": np.tile(np.arange(SLOTS), (P, 1)),
        "desc": np.tile(np.arange(NE, 0, -1), (P, 1)),
    }
    return {k: np.ascontiguousarray(v, dtype=f) for k, v in out.items()}


def const_layout():
    at, out = 0, {}
    for k, v in shape_constants().items():
        out[k] = (at, v.shape[1])
        at += v.shape[1]
    return out, at


def build(nc, t):
    where, const_cols = const_layout()
    with ExitStack() as ctx:
        def sb(name, shape, dt=F32):
            return ctx.enter_context(nc.sbuf_tensor(name, shape, dt))

        def sem(name):
            return ctx.enter_context(nc.semaphore(name))

        bank = [ctx.enter_context(nc.psum_tensor(f"bank{i}", [P, 512], F32)) for i in range(8)]
        proj_bank = bank[0:2]
        tr_bank = bank[2:4]
        score_bank = [bank[4], bank[5], bank[0], bank[1]]
        out_bank = bank[6:8]

        ring = sb("ring", [P, RING, SLOT])
        consts = sb("consts", [P, const_cols])
        res = sb("res", [P, TILES, D])
        xt = sb("xt", [P, KD, SEQ])
        gate = sb("gate", [P, TILES, D])
        wide = sb("wide", [P, TILES, D])
        val = sb("val", [P, TILES, D])
        qk = sb("qk", [P, 8192])
        stage = sb("stage", [P, 4, 512])
        probs = sb("probs", [P, 4, 256])
        probs_t = sb("probs_t", [P, 2, 256])
        tmp = sb("tmp", [P, 2, 1024])
        small = sb("small", [P, 512])
        gain_rows = probs[0:GAIN_ROWS, 0, 0:P]
        head_gain = tmp[:, 1, 0:2 * HD]
        gain_cols = sb("gain_cols", [P, GAIN_ROWS])
        ident_b = sb("ident_b", [P, P], BF16)
        causal_b = sb("causal_b", [P, P], BF16)
        var = sb("var", [P, RSQRT_COLS])
        rstd = sb("rstd", [P, RSQRT_COLS])
        power = sb("power", [P, 20])
        router_w = stage[:, 0:2, :].rearrange("p a n -> p (a n)")[:, 0:KD * (NG + NE)].rearrange(
            "p (c n) -> p c n", c=KD)
        router_b = sb("router_b", [P, NG + NE])
        rank = sb("rank", [P, TILES, NE])
        gates = sb("gates", [P, TILES, NE])
        largest = sb("largest", [P, 1], I32)

        def const(name):
            a, n = where[name]
            return consts[:, a:a + n]

        ident = const("ident")
        q_t, k_t = qk[:, 0:4096], qk[:, 4096:8192]
        q_a = q_t.rearrange("p (h s) -> p h s", h=H)
        k_a = k_t.rearrange("p (h s) -> p h s", h=H)
        q_b = q_t[:, 0:2048].rearrange("p (h s) -> p h s", h=H // 2)
        k_b = k_t[:, 0:2048].rearrange("p (h s) -> p h s", h=H // 2)
        ln_row = tmp
        q_g = qk[:, 0:1024].rearrange("p (h s) -> p h s", h=QH // 2)
        k_g = qk[:, 1024:1536].rearrange("p (h s) -> p h s", h=KVH)
        exp_q = qk[:, 1536:2560].rearrange("p (d a s) -> p d a s", d=2, a=2)
        exp_k = qk[:, 2560:3584].rearrange("p (d a s) -> p d a s", d=2, a=2)
        exp_b = qk[:, 3584:4608].rearrange("p (d a s) -> p d a s", d=2, a=2)
        q_in = qk[:, 4608:5632].rearrange("p (d a s) -> p d a s", d=2, a=2)
        k_out = qk[:, 5632:6656].rearrange("p (t d n) -> p t d n", t=2, d=2)
        gla_t = qk[:, 6656:7680].rearrange("p (c s) -> p c s", c=4)
        z_t = qk[:, 7680:7936]
        gla_qk = stage[:, 0:2, :]
        decay = stage[:, 2:4, :]
        state = stage.rearrange("p n (a e) -> p n a e", a=2)
        state_b = val[:, :, 512:1024].rearrange("p t (a e) -> p t a e", a=2)
        att_q = gate[:, :, 512:1024]
        att_kv = sb("att_kv", [P, TILES, 256])
        key2 = probs_t
        z_in = sb("z_in", [P, TILES, 32])
        up_w = probs[0:33, 2:4, :].rearrange("p a b -> p (a b)")
        rope_g = sb("rope_g", [P, 4, 128])
        masked = wide[:, :, 512:1024]
        norm2_row, final_row = gate[:, 0, :], gate[:, 1, :]
        picked = qk[:, 0:1024].rearrange("p (c s) -> p c s", c=KD)
        onehot = qk[:, 1024:1280].rearrange("p (t s) -> p t s", t=2)
        weighted = qk[:, 1280:1536].rearrange("p (t s) -> p t s", t=2)
        back = qk[:, 1536:1792]
        act_g = qk[:, 1792:1920]
        hidden = qk[:, 1920:2048]
        hidden_t = qk[:, 2048:2176]
        expert_out = qk[:, 2176:3200]
        top_diff = small[:, 172:174]
        g_exp = small[:, 200:216]
        ratio = small[:, 216:218]
        g_diff = tmp[:, 0, 48:64]
        routed = wide.rearrange("p t (c k) -> p t c k", c=KD)

        x_landed = sem("x_landed")
        ident_landed = sem("ident_landed")
        consts_landed = sem("consts_landed")
        gains_landed = sem("gains_landed")
        ln_landed = sem("ln_landed")
        row_landed = sem("row_landed")
        small_landed = sem("small_landed")
        up_zeroed = sem("up_zeroed")
        up_landed = sem("up_landed")
        block_landed = [sem(f"block_landed{i}") for i in range(RING)]
        proj_in_psum = sem("proj_in_psum")
        proj_in_sbuf = sem("proj_in_sbuf")
        tr_in_psum = sem("tr_in_psum")
        tr_in_sbuf = sem("tr_in_sbuf")
        masks_cast = sem("masks_cast")
        power_set = sem("power_set")
        rsqrt_asked = sem("rsqrt_asked")
        rsqrt_done = sem("rsqrt_done")
        sumsq_done = sem("sumsq_done")
        latents_normed = sem("latents_normed")
        heads_roped = sem("heads_roped")
        key_rope_placed = sem("key_rope_placed")
        scores_in_psum = sem("scores_in_psum")
        max_done = sem("max_done")
        probs_done = sem("probs_done")
        out_in_psum = sem("out_in_psum")
        out_drained = sem("out_drained")
        mixed_ready = sem("mixed_ready")
        res_ready = sem("res_ready")
        ln_used = sem("ln_used")
        normed_ready = sem("normed_ready")
        gqa_ready = sem("gqa_ready")
        decay_in_psum = sem("decay_in_psum")
        decay_log = sem("decay_log")
        decay_ready = sem("decay_ready")
        cum_in_psum = sem("cum_in_psum")
        cum_exp = sem("cum_exp")
        gla_operands = sem("gla_operands")
        kv_in_psum = sem("kv_in_psum")
        state_ready = sem("state_ready")
        gla_scores = sem("gla_scores")
        gla_masked = sem("gla_masked")
        gla_intra = sem("gla_intra")
        gla_inter = sem("gla_inter")
        gla_copied = sem("gla_copied")
        gla_summed = sem("gla_summed")
        routed_ready = sem("routed_ready")
        logits_in_psum = sem("logits_in_psum")
        mask_ready = sem("mask_ready")
        gates_exp = sem("gates_exp")
        rank_moved = sem("rank_moved")
        ranks_in_psum = sem("ranks_in_psum")
        routing_ready = sem("routing_ready")
        gate_up_landed = [sem(f"gate_up_landed{i}") for i in range(2)]
        down_landed = [sem(f"down_landed{i}") for i in range(2)]
        onehot_ready = sem("onehot_ready")
        picked_in_psum = sem("picked_in_psum")
        picked_ready = sem("picked_ready")
        back_in_psum = sem("back_in_psum")
        back_ready = sem("back_ready")
        hidden_in_psum = sem("hidden_in_psum")
        silu_done = sem("silu_done")
        hidden_ready = sem("hidden_ready")
        hidden_t_in_psum = sem("hidden_t_in_psum")
        hidden_t_ready = sem("hidden_t_ready")
        down_in_psum = sem("down_in_psum")
        down_drained_act = sem("down_drained_act")
        down_drained_dve = sem("down_drained_dve")
        sum_in_psum = sem("sum_in_psum")
        sum_added = sem("sum_added")
        act_chain = sem("act_chain")
        dve_chain = sem("dve_chain")
        out_ready = sem("out_ready")
        out_stored = sem("out_stored")

        block = ctx.enter_context(nc.Block())

        TR = {}
        count = 0
        for name, n in (("x", 4), ("gains", 1), ("latents", 4), ("q_a", 8), ("k_a", 8), ("att_a", 32), ("o_a", 4),
                        ("x1", 4), ("k_b", 4), ("q_b", 4), ("att_b", 32), ("o_b", 4), ("u", 4),
                        ("z", 2), ("gla", 2), ("gqa_q", 2), ("gqa_k", 2), ("att_g", 16), ("mixed", 4), ("routed", 4)):
            TR[name] = count
            count += n

        UNITS_A = UNITS_B = H * TILES
        UNITS_G = QH * TILES
        UNIT0 = {"a": 0, "b": UNITS_A, "g": UNITS_A + UNITS_B}
        OUT0 = {"a": 0, "b": 4, "g": 8}

        def state_of(way, step):
            n = 3 * way + step
            return state[:, n] if n < 4 else state_b[:, n - 4]

        def unit_of(u):
            group, tile, h = u // (8 * TILES), u // 8 % TILES, u % 8
            return 8 * group + h, tile

        def keys_of(kind, tile):
            return SEQ if kind == "g" else P * (tile + 1)

        @block.sync
        def _(sp):
            sp.dma_start(consts[:, 0:P], t["consts"][:, 0:P]).then_inc(ident_landed, 16)
            sp.dma_start(res[:], t["x"].rearrange("b (t p) d -> p (b t) d", p=P)).then_inc(x_landed, 16)
            for b, (name, kc, first, n) in enumerate(BLOCKS):
                slot = b % RING
                if b >= RING:
                    sp.wait_ge(proj_in_psum, LAST_JOB[b - RING] + 1)
                w = t[name]
                src = (w if name == "moba_w_kv" else w[0])[:, first:first + n].rearrange("(c p) n -> p c n", p=P)
                dst = ring[:, slot, 0:kc * n].rearrange("p (c n) -> p c n", c=kc)
                sp.dma_start(dst, src).then_inc(block_landed[slot], 16)
                if b == 1:
                    sp.dma_start(consts[:, P:], t["consts"][:, P:]).then_inc(consts_landed, 16)

            def load_expert(e, parity, waits):
                base = 3 * parity
                waits(0)
                for k, name in ((0, "w_gate_2"), (1, "w_up_2")):
                    src = t[name][0, bass.ds(e, 1)].rearrange("e (p c) f -> p (e c f)", c=KD)
                    sp.dma_start(ring[:, base + k, :], src).then_inc(gate_up_landed[parity], 16)
                waits(1)
                src = t["w_down_2"][0, bass.ds(e, 1)].rearrange("e (j p) n -> p (e j) n", p=P)
                sp.dma_start(ring[:, base + 2, :].rearrange("p (j n) -> p j n", j=4), src).then_inc(
                    down_landed[parity], 16)

            def front_done(parity):
                def waits(k):
                    slots = (3 * parity, 3 * parity + 1) if k == 0 else (3 * parity + 2,)
                    last = max(b for b in range(len(BLOCKS)) if b % RING in slots)
                    sp.wait_ge(proj_in_psum, LAST_JOB[last] + 1)
                return waits

            def expert_used(before):
                def waits(k):
                    sp.wait_ge(hidden_in_psum if k == 0 else down_in_psum, before)
                return waits

            for e in range(2):
                load_expert(e, e, front_done(e))
            with sp.Fori(0, ROUNDS - 1) as r:
                for i in range(GROUP):
                    load_expert(GROUP * r + (i + 2), i % 2, expert_used(GROUP * r + (i + 1)))
            for e in range(NE - 2, NE):
                load_expert(e, e % 2, expert_used(e - 1))

            sp.wait_ge(routing_ready, 1)
            most = sp.value_load(largest[0:1, 0:1], min_val=0, max_val=SEQ)
            with sp.If(most > SLOTS):
                with sp.Fori(1, PASSES) as p:
                    for e in range(2):
                        load_expert(e, e, expert_used(NE * p + (e - 1)))
                    with sp.Fori(0, ROUNDS - 1) as r:
                        for i in range(GROUP):
                            load_expert(GROUP * r + (i + 2), i % 2, expert_used(NE * p + GROUP * r + (i + 1)))
                    for e in range(NE - 2, NE):
                        load_expert(e, e % 2, expert_used(NE * p + (e - 1)))

            for tile in range(TILES):
                sp.wait_ge(out_ready, tile + 1)
                sp.dma_start(t["out"][0, tile * P:(tile + 1) * P, :], wide[:, tile, :]).then_inc(out_stored, 16)
            sp.wait_ge(out_stored, 16 * TILES)

        @block.gpsimd
        def _(pool):
            nc.gpsimd.memset(power[:], -0.5).then_inc(power_set, 1)
            pool.wait_ge(power_set, 1)
            for n, a, w in RSQRT.values():
                pool.wait_ge(rsqrt_asked, n + 1)
                nc.gpsimd.tensor_tensor(rstd[:, a:a + w], var[:, a:a + w], power[:, 0:w], ALU.pow).then_inc(
                    rsqrt_done, 1)

        @block.scalar
        def _(act):
            rows = ((GAIN_Q, t["mla_q_norm"], 6), (6, t["mla_kv_norm"], 2), (GAIN_N1, t["norm1_gain_2"], 8),
                    (GAIN_MIX, t["gla_out_gain_2"], 1), (GAIN_MIX + 1, t["gla_out_gain_2"], 1),
                    (GAIN_MIX + 2, t["gla_out_gain_2"], 1), (GAIN_MIX + 3, t["gla_out_gain_2"], 1),
                    (GAIN_MIX + 4, t["att_out_gain_2"], 4))
            for a, src, n in rows:
                act.dma_start(gain_rows[a:a + n, :], src[0].rearrange("(r p) -> r p", p=P)).then_inc(gains_landed, 16)

            def load_row(dst, src, signal):
                act.dma_start(dst, src.rearrange("(a n) -> a n", a=1).to_broadcast([P, src.shape[0]])).then_inc(
                    signal, 16)

            def load_ln(layer):
                load_row(ln_row[:, 0, :], t["ln_g"][layer], ln_landed)
                load_row(ln_row[:, 1, :], t["ln_b"][layer], ln_landed)

            load_row(router_b[:, 0:NG], t["b_group_2"][0], small_landed)
            load_row(router_b[:, NG:], t["b_expert_2"][0], small_landed)
            load_row(head_gain[:, 0:HD], t["q_norm_gain_2"][0], small_landed)
            load_row(head_gain[:, HD:], t["k_norm_gain_2"][0], small_landed)

            def start_job(job):
                act.wait_ge(proj_in_psum, JOB[job] + 1)
                return proj_bank[JOB[job] % 2]

            def squares(src, column, spare=tmp[:, 0, :]):
                return nc.scalar.activation(spare[:, 0:src.shape[-1]], src, ACT.Square,
                                            accum_out=small[:, column:column + 1])

            chain = [0]

            def link(ins):
                chain[0] += 1
                ins.then_inc(act_chain, 1)
                act.wait_ge(act_chain, chain[0])

            for tile in range(TILES):
                src = start_job(("mla_w_in", 0, tile))
                link(squares(src[:, 0:512], 3 * tile))
                nc.scalar.copy(wide[:, tile, 0:512], src[:]).then_inc(proj_in_sbuf, 1)
            for tile in range(TILES):
                src = start_job(("mla_w_in", 1, tile))
                link(squares(src[:, 0:256], 3 * tile + 1))
                squares(src[:, 256:512], 3 * tile + 2).then_inc(sumsq_done, 1)
                act.wait_ge(sumsq_done, tile + 1)
                nc.scalar.copy(wide[:, tile, 512:1024], src[:]).then_inc(proj_in_sbuf, 1)
            for tile in range(TILES):
                src = start_job(("mla_w_in", 2, tile))
                nc.scalar.copy(z_in[:, tile, :], src[:, 0:ROPE])
                nc.scalar.activation(gate[:, tile, 0:384], src[:, 32:416], ACT.Silu).then_inc(proj_in_sbuf, 1)
            for b, a in ((3, 384), (4, 704)):
                for tile in range(TILES):
                    src = start_job(("mla_w_in", b, tile))
                    nc.scalar.activation(gate[:, tile, a:a + 320], src[:, 0:320], ACT.Silu).then_inc(proj_in_sbuf, 1)
            for n, job in enumerate([("mla_w_uq", b, tile) for b in range(4) for tile in range(TILES)]):
                if n >= 4:
                    act.wait_ge(tr_in_psum, TR["q_a"] + n - 3)
                src = start_job(job)
                nc.scalar.mul(stage[:, n % 4, 0:384], src[:, 0:384], SCALE_A).then_inc(proj_in_sbuf, 1)
            for n, job in enumerate([("mla_w_ukv", b, tile) for b in range(4) for tile in range(TILES)]):
                if n == 0:
                    act.wait_ge(key_rope_placed, 1)
                if n >= 4:
                    act.wait_ge(tr_in_psum, TR["k_a"] + n - 3)
                src = start_job(job)[:].rearrange("p (h d) -> p h d", h=4)
                b, tile = job[1], job[2]
                nc.scalar.copy(stage[:, n % 4, 0:4 * QKD].rearrange("p (h d) -> p h d", h=4)[:, :, 0:NOPE],
                               src[:, :, 0:NOPE])
                nc.scalar.copy(val[:, tile, 256 * b:256 * b + 256].rearrange("p (h d) -> p h d", h=4),
                               src[:, :, NOPE:]).then_inc(proj_in_sbuf, 1)

            row_sum = small[:, 256:256 + 80]
            neg_max = small[:, 336:336 + 80]

            def softmax_units(kind, units):
                for u in range(units):
                    n = UNIT0[kind] + u
                    keys = keys_of(kind, unit_of(u)[1])
                    act.wait_ge(max_done, n + 1)
                    if u >= 4:
                        act.wait_ge(tr_in_psum, TR["att_" + kind] + u - 3)
                    nc.scalar.activation(probs[:, u % 4, 0:keys], score_bank[u % 4][:, 0:keys], ACT.Exp,
                                         bias=neg_max[:, n:n + 1], accum_out=row_sum[:, n:n + 1]).then_inc(
                        probs_done, 1)

            softmax_units("a", UNITS_A)
            load_ln(0)

            def drain_output(name, after=lambda tile: None):
                for tile in range(TILES):
                    for b in range(2):
                        src = start_job((name, b, tile))
                        nc.scalar.copy(wide[:, tile, 512 * b:512 * b + 512], src[:]).then_inc(proj_in_sbuf, 1)
                    after(tile)

            def stream_squares(n, tile, spare=tmp[:, 0, :]):
                act.wait_ge(res_ready, n + tile + 1)
                squares(res[:, tile, :], 16 + n + tile, spare).then_inc(sumsq_done, 1)
                act.wait_ge(sumsq_done, n + tile + 1)

            drain_output("mla_w_o")

            def drain_heads(name, scale, transposed):
                act.wait_ge(tr_in_psum, transposed)
                for n, job in enumerate([(name, b, tile) for b in range(2) for tile in range(TILES)]):
                    src = start_job(job)
                    nc.scalar.mul(stage[:, n, :], src[:], scale).then_inc(proj_in_sbuf, 1)

            drain_heads("moba_w_kv", 1.0, TR["k_a"] + 8)
            for b in range(2):
                for tile in range(TILES):
                    src = start_job(("moba_w_kv", 2 + b, tile))
                    nc.scalar.copy(val[:, tile, 512 * b:512 * b + 512], src[:]).then_inc(proj_in_sbuf, 1)
            drain_heads("moba_w_in", SCALE_B, TR["k_b"] + 4)
            for b in range(2):
                for tile in range(TILES):
                    src = start_job(("moba_w_in", 2 + b, tile))
                    nc.scalar.activation(gate[:, tile, 512 * b:512 * b + 512], src[:], ACT.Silu).then_inc(
                        proj_in_sbuf, 1)
            softmax_units("b", UNITS_B)
            load_ln(1)
            act.wait_ge(up_zeroed, 1)
            for k, (w, b) in enumerate((("gla_up_fwd_2", "gla_up_fwd_bias_2"), ("gla_up_bwd_2", "gla_up_bwd_bias_2"))):
                act.dma_start(up_w[16 * k:16 * k + 16, GW * k:GW * k + GW], t[w][0]).then_inc(up_landed, 16)
                act.dma_start(up_w[32:33, GW * k:GW * k + GW], t[b]).then_inc(up_landed, 16)
            drain_output("moba_w_o", lambda tile: stream_squares(2, tile, gate[:, tile, :]))

            for tile in range(TILES):
                src = start_job(("w_in_2", 0, tile))
                nc.scalar.copy(z_in[:, tile, :], src[:, 0:32])
                nc.scalar.copy(att_q[:, tile, 0:384], src[:, 32:416]).then_inc(proj_in_sbuf, 1)
                src = start_job(("w_in_2", 1, tile))
                nc.scalar.copy(att_q[:, tile, 384:512], src[:, 0:128])
                nc.scalar.copy(att_kv[:, tile, :], src[:, 128:384]).then_inc(proj_in_sbuf, 1)
            for tile in range(TILES):
                act.wait_ge(decay_in_psum, 2)
                log = probs[:, 2 * tile:2 * tile + 2, :].rearrange("p a b -> p (a b)")
                link(nc.scalar.activation(log, out_bank[tile][:], ACT.Abs))
                link(nc.scalar.activation(log, log, ACT.Exp, scale=-1.0))
                nc.scalar.activation(log, log, ACT.Ln, bias=const("ones")[:, 0:1]).then_inc(decay_log, 1)
            for tile in range(TILES):
                src = start_job(("w_in_2", 2, tile))
                nc.scalar.mul(gla_qk[:, tile, 0:GW], src[:, 0:GW], GDK ** -0.5)
                nc.scalar.copy(gla_qk[:, tile, GW:512], src[:, GW:512]).then_inc(proj_in_sbuf, 1)
            for tile in range(TILES):
                at = slice(tile * P, tile * P + P)
                for way in range(2):
                    n = 2 * tile + way
                    act.wait_ge(cum_in_psum, n + 1)
                    cum = score_bank[n % 2][:].rearrange("p (a m s) -> p a m s", a=2, m=2)
                    nc.scalar.activation(exp_q[:, way, :, at], cum[:, :, 0, :], ACT.Exp, scale=1 / 16)
                    nc.scalar.activation(exp_k[:, way, :, at], cum[:, :, 0, :], ACT.Exp, scale=-1 / 16)
                    nc.scalar.activation(exp_b[:, way, :, at], cum[:, :, 1, :], ACT.Exp, scale=1 / 16)
                    nc.scalar.activation(k_out[:, tile, way, :], out_bank[n % 2][:, 0:GW], ACT.Exp,
                                         scale=1 / 16).then_inc(cum_exp, 1)
                src = start_job(("w_in_2", 3, tile))
                nc.scalar.copy(val[:, tile, 0:512], src[:]).then_inc(proj_in_sbuf, 1)
            for tile in range(TILES):
                src = start_job(("w_in_2", 4, tile))
                nc.scalar.activation(gate[:, tile, 0:512], src[:], ACT.Silu).then_inc(proj_in_sbuf, 1)
            for tile in range(TILES):
                act.wait_ge(gla_intra, tile + 1)
                nc.scalar.copy(wide[:, tile, 0:512], proj_bank[tile][:]).then_inc(gla_copied, 1)

            softmax_units("g", UNITS_G)
            load_row(norm2_row, t["norm2_gain_2"][0], row_landed)
            load_row(final_row, t["final_gain_2"], row_landed)
            for src, a, n in ((t["w_group_2"], 0, NG), (t["w_expert_2"], NG, NE)):
                act.dma_start(router_w[:, :, a:a + n], src[0].rearrange("(p c) n -> p c n", c=KD)).then_inc(
                    row_landed, 16)
            drain_output("w_out_2", lambda tile: stream_squares(4, tile))

            act.wait_ge(logits_in_psum, 1)
            nc.scalar.copy(small[:, 0:144], proj_bank[0][:, 0:144]).then_inc(proj_in_sbuf, 1)
            act.wait_ge(mask_ready, 1)
            nc.scalar.activation(g_exp, g_diff, ACT.Exp).then_inc(gates_exp, 1)
            act.wait_ge(mask_ready, 2)
            nc.scalar.activation(ratio, top_diff, ACT.Exp).then_inc(gates_exp, 1)

            def expert_rounds(rounds, base):
                with act.Fori(0, rounds) as r:
                    for half in range(2):
                        act.wait_ge(picked_in_psum, 2 * (base + r) + (half + 1))
                        nc.scalar.copy(picked[:, 4 * half:4 * half + 4, :],
                                       bank[half][:].rearrange("p (c s) -> p c s", c=4)).then_inc(picked_ready, 1)
                    for i in range(GROUP):
                        act.wait_ge(hidden_in_psum, GROUP * (base + r) + (i + 1))
                        nc.scalar.activation(act_g, bank[2][:, 0:P], ACT.Silu).then_inc(silu_done, 1)
                        act.wait_ge(down_in_psum, GROUP * (base + r) + (i + 1))
                        nc.scalar.copy(expert_out[SLOTS * i:SLOTS * i + SLOTS, 0:256], bank[4][0:32, 0:256])
                        nc.scalar.copy(expert_out[SLOTS * i:SLOTS * i + SLOTS, 256:512],
                                       bank[4][32:64, 0:256]).then_inc(down_drained_act, 1)

            expert_rounds(ROUNDS, 0)
            act.wait_ge(routing_ready, 1)
            most = act.value_load(largest[0:1, 0:1], min_val=0, max_val=SEQ)
            with act.If(most > SLOTS):
                with act.Fori(1, PASSES) as p:
                    expert_rounds(ROUNDS, ROUNDS * p)

            for tile in range(TILES):
                stream_squares(6, tile)

        @block.vector
        def _(dve):
            chain = [0]

            def link(ins):
                chain[0] += 1
                ins.then_inc(dve_chain, 1)
                dve.wait_ge(dve_chain, chain[0])

            def rsqrt(name):
                n, a, w = RSQRT[name]
                dve.wait_ge(rsqrt_done, n + 1)
                return rstd[:, a:a + w]

            def ask(name, ins):
                ins.then_inc(rsqrt_asked, 1)

            def variances(name):
                n, a, w = RSQRT[name]
                return var[:, a:a + w]

            tr = [0]

            def drain(dst, gain=None, rows=P, width=512):
                n = tr[0]
                dve.wait_ge(tr_in_psum, n + 1)
                src = tr_bank[n % 2][0:rows, 0:width]
                src = src.rearrange("p (c s) -> p c s", s=P)
                if gain is None:
                    ins = nc.vector.tensor_copy(dst, src)
                else:
                    blocks = width // P
                    ins = nc.vector.tensor_tensor(dst, src, gain.rearrange("p (c a) -> p c a", a=1).to_broadcast(
                        [P, blocks, P]), ALU.mult)
                ins.then_inc(tr_in_sbuf, 1)
                tr[0] += 1

            def drain_xt(gains=None, tiles=range(TILES)):
                for tile in tiles:
                    for half in range(2):
                        g = None if gains is None else gain_cols[:, gains + 4 * half:gains + 4 * half + 4]
                        drain(xt[:, 4 * half:4 * half + 4, tile * P:tile * P + P], g)

            drain_xt()
            dve.wait_ge(tr_in_psum, TR["gains"] + 1)
            nc.vector.tensor_copy(gain_cols[:], tr_bank[0][:, 0:GAIN_ROWS]).then_inc(tr_in_sbuf, 1)
            tr[0] += 1
            dve.wait_ge(consts_landed, 16)
            nc.vector.tensor_copy(ident_b[:], ident)
            nc.vector.tensor_copy(causal_b[:], const("causal")).then_inc(masks_cast, 1)
            dve.wait_ge(small_landed, 64)
            for k in range(2):
                g = head_gain[:, HD * k:HD * k + HD]
                pairs = g.rearrange("p (d two) -> p d two", two=2)
                scale = HD ** -0.5 if k == 0 else 1.0
                for tile in range(TILES):
                    at = slice(HD * tile, HD * tile + HD)
                    cos, sin = const("cos_g")[:, at], const("sin_g")[:, at].rearrange("p (d two) -> p d two", two=2)
                    nc.vector.scalar_tensor_tensor(rope_g[:, 2 * k, at], cos, scale, g, ALU.mult, ALU.mult)
                    for x in range(2):
                        dst = rope_g[:, 2 * k + 1, at].rearrange("p (d two) -> p d two", two=2)[:, :, x]
                        last = nc.vector.scalar_tensor_tensor(dst, sin[:, :, x], scale, pairs[:, :, 1 - x],
                                                              ALU.mult, ALU.mult)
            link(last)

            dve.wait_ge(sumsq_done, 2)
            dve.wait_ge(proj_in_sbuf, JOB["mla_w_in", 1, 1] + 1)
            v = variances("mla").rearrange("p (t n) -> p t n", n=2)
            ss = small[:, 0:6].rearrange("p (t n) -> p t n", n=3)
            link(nc.vector.tensor_tensor(small[:, 6:8], ss[:, :, 0], ss[:, :, 1], ALU.add))
            link(nc.vector.tensor_scalar(v[:, :, 0], small[:, 6:8], 1 / Q_LORA, RMS_EPS, ALU.mult, ALU.add))
            ask("mla", nc.vector.tensor_scalar(v[:, :, 1], ss[:, :, 2], 1 / KV_LORA, RMS_EPS, ALU.mult, ALU.add))
            r = rsqrt("mla")
            for tile in range(TILES):
                nc.vector.tensor_scalar(wide[:, tile, 0:Q_LORA], wide[:, tile, 0:Q_LORA],
                                        r[:, 2 * tile:2 * tile + 1], None, ALU.mult)
                nc.vector.tensor_scalar(wide[:, tile, Q_LORA:D], wide[:, tile, Q_LORA:D],
                                        r[:, 2 * tile + 1:2 * tile + 2], None, ALU.mult).then_inc(latents_normed, 1)
            dve.wait_ge(proj_in_sbuf, JOB["mla_w_in", 2, 1] + 1)

            def rope_a(x, heads, tile, out):
                half = ROPE // 2
                cos = const("cos_a")[:, ROPE * tile:ROPE * tile + ROPE]
                sin = const("sin_a")[:, ROPE * tile:ROPE * tile + ROPE]

                def over_heads(a):
                    return a.rearrange("p (h d) -> p h d", h=1).to_broadcast([P, heads, a.shape[-1]])

                c = tmp[:, 0, 0:heads * ROPE].rearrange("p (h d) -> p h d", h=heads)
                s = tmp[:, 1, 0:heads * ROPE].rearrange("p (h d) -> p h d", h=heads)
                nc.vector.tensor_tensor(c, x, over_heads(cos), ALU.mult)
                nc.vector.tensor_tensor(s[:, :, 0:half], x[:, :, half:ROPE], over_heads(sin[:, 0:half]), ALU.mult)
                link(nc.vector.tensor_tensor(s[:, :, half:ROPE], x[:, :, 0:half], over_heads(sin[:, half:ROPE]),
                                             ALU.mult))
                return nc.vector.tensor_tensor(out, c, s, ALU.add)

            key_rope = small[:, 64:64 + TILES * ROPE].rearrange("p (t d) -> p t d", t=TILES)
            for tile in range(TILES):
                x = z_in[:, tile, :].rearrange("p (h d) -> p h d", h=1)
                link(rope_a(x, 1, tile, key_rope[:, tile:tile + 1, :]))
            dve.wait_ge(tr_in_sbuf, TR["gains"] + 1)
            drain_xt(GAIN_Q)

            def q_a_rope(n):
                b, tile = n // TILES, n % TILES
                dve.wait_ge(proj_in_sbuf, JOB["mla_w_uq", b, tile] + 1)
                x = stage[:, n % 4, 0:4 * QKD].rearrange("p (h d) -> p h d", h=4)[:, :, NOPE:QKD]
                rope_a(x, 4, tile, x).then_inc(heads_roped, 1)
                dve.wait_ge(heads_roped, n + 1)

            def heads_out(dst, n, per, rows):
                b, tile = n // TILES, n % TILES
                drain(dst[0:rows, per * b:per * b + per, tile * P:tile * P + P], rows=rows, width=per * P)

            for n in range(8 + LAG):
                if n < 8:
                    q_a_rope(n)
                if n >= LAG:
                    heads_out(q_a, n - LAG, 4, QKD)
            for i in range(4):
                last = nc.vector.tensor_copy(
                    stage[:, i, 0:4 * QKD].rearrange("p (h d) -> p h d", h=4)[:, :, NOPE:QKD],
                    key_rope[:, i % 2:i % 2 + 1, :].to_broadcast([P, 4, ROPE]))
            last.then_inc(key_rope_placed, 1)
            for n in range(8):
                heads_out(k_a, n, 4, QKD)

            row_sum = small[:, 256:256 + 80]
            neg_max = small[:, 336:336 + 80]
            inverse = small[:, 416:416 + 80]

            def attention(kind, units, depth, out_of, tail, beside=()):
                for u in range(units + depth + 1):
                    if u < units:
                        n = UNIT0[kind] + u
                        dve.wait_ge(scores_in_psum, n + 1)
                        nc.vector.tensor_reduce(neg_max[:, n:n + 1], score_bank[u % 4][:, 0:keys_of(kind, unit_of(u)[1])],
                                                AX.X, ALU.max, negate=True).then_inc(max_done, 1)
                    if u in beside:
                        beside[u]()
                    m = u - depth
                    if 0 <= m < units:
                        keys = keys_of(kind, unit_of(m)[1])
                        drain(probs_t[:, m % 2, 0:keys].rearrange("p (c s) -> p c s", s=P), width=keys)
                    if m == units - 1:
                        tail()
                    m = u - depth - 1
                    if m >= 0 and m % 8 == 7:
                        group, tile = m // (8 * TILES), unit_of(m)[1]
                        sums = row_sum[:, UNIT0[kind] + m - 7:UNIT0[kind] + m + 1]
                        inv = inverse[:, 8 * tile:8 * tile + 8]
                        dve.wait_ge(probs_done, UNIT0[kind] + m + 1)
                        link(nc.vector.reciprocal(inv, sums))
                        dve.wait_ge(out_in_psum, OUT0[kind] + group * TILES + tile + 1)
                        dst = out_of(tile, group)
                        link_out = nc.vector.tensor_tensor(
                            dst.rearrange("p (h d) -> p h d", h=8),
                            out_bank[tile][:].rearrange("p (h d) -> p h d", h=8),
                            inv.rearrange("p (h a) -> p h a", a=1).to_broadcast([P, 8, HD]), ALU.mult)
                        link_out.then_inc(out_drained, 1)
                        dve.wait_ge(out_drained, OUT0[kind] + group * TILES + tile + 1)
                        if kind != "g":
                            g = gate[:, tile, 512 * group:512 * group + 512]
                            nc.vector.tensor_tensor(dst, dst, g, ALU.mult).then_inc(mixed_ready, 1)

            def half_of(tile, group):
                return wide[:, tile, 512 * group:512 * group + 512]

            attention("a", UNITS_A, 3, half_of, lambda: drain_xt(tiles=[0]))
            drain_xt(tiles=[1])

            def rms_of_stream(name, first_ready, tile):
                rs, column = f"{name}t{tile}", 16 + first_ready + tile
                dve.wait_ge(sumsq_done, first_ready + tile + 1)
                ask(rs, nc.vector.tensor_scalar(variances(rs), small[:, column:column + 1], 1 / D, RMS_EPS,
                                                ALU.mult, ALU.add))
                return rsqrt(rs)

            def post_norm(layer, name):
                stats = small[:, 128:140].rearrange("p (c s) -> p c s", c=2)
                for tile in range(TILES):
                    for b in range(2):
                        half = slice(512 * b, 512 * b + 512)
                        dve.wait_ge(proj_in_sbuf, JOB[name, b, tile] + 1)
                        link(nc.vector.scalar_tensor_tensor(res[:, tile, half], res[:, tile, half], ALPHA,
                                                            wide[:, tile, half], ALU.mult, ALU.add))
                        last = nc.vector.bn_stats(stats[:, b, :], res[:, tile, half])
                    link(last)
                    link(nc.vector.bn_aggr(small[:, 140:142], small[:, 128:140]))
                    rs = f"ln{layer}t{tile}"
                    ask(rs, nc.vector.tensor_scalar(variances(rs), small[:, 141:142], LN_EPS, None, ALU.add))
                    r = rsqrt(rs)
                    link(nc.vector.tensor_scalar(res[:, tile, :], res[:, tile, :], small[:, 140:141], r,
                                                 ALU.subtract, ALU.mult))
                    if tile == 0:
                        dve.wait_ge(ln_landed, 32 * (layer + 1))
                    link(nc.vector.tensor_tensor(res[:, tile, :], res[:, tile, :], ln_row[:, 0, :], ALU.mult))
                    nc.vector.tensor_tensor(res[:, tile, :], res[:, tile, :], ln_row[:, 1, :], ALU.add).then_inc(
                        res_ready, 1)
                    dve.wait_ge(res_ready, 2 * layer + tile + 1)
                    if tile == 1:
                        nc.vector.memset(small[:, 142:143], 0.0).then_inc(ln_used, 1)
                        dve.wait_ge(ln_used, layer + 1)
                    if layer == 0:
                        drain_xt(tiles=[tile])
                    else:
                        r = rms_of_stream("norm1", 2, tile)
                        nc.vector.tensor_scalar(wide[:, tile, :], res[:, tile, :], r, None, ALU.mult).then_inc(
                            normed_ready, 1)
                        drain_xt(GAIN_N1, [tile])

            post_norm(0, "mla_w_o")

            def rope_b(x, tile, heads, cos, sin, swap, n):
                def over_heads(a):
                    return a.rearrange("p (h d) -> p h d", h=1).to_broadcast([P, heads, HD])

                def split(a):
                    a = a.rearrange("p (h d) -> p h d", h=heads)
                    if swap == "halves":
                        return a[:, :, 0:HD // 2], a[:, :, HD // 2:HD]
                    a = a.rearrange("p h (d two) -> p h d two", two=2)
                    return a[:, :, :, 0], a[:, :, :, 1]

                width = heads * HD
                c, s = tmp[:, 0, 0:width], tmp[:, 1, 0:width]
                x0, x1 = split(x)
                s0, s1 = split(s)
                nc.vector.tensor_tensor(c.rearrange("p (h d) -> p h d", h=heads),
                                        x.rearrange("p (h d) -> p h d", h=heads), over_heads(cos), ALU.mult)
                sin3 = over_heads(sin)
                if swap == "halves":
                    w0, w1 = sin3[:, :, 0:HD // 2], sin3[:, :, HD // 2:HD]
                else:
                    w = sin.rearrange("p (h d two) -> p h d two", h=1, two=2)
                    w0 = w[:, :, :, 0].to_broadcast([P, heads, HD // 2])
                    w1 = w[:, :, :, 1].to_broadcast([P, heads, HD // 2])
                nc.vector.tensor_tensor(s0, x1, w0, ALU.mult)
                link(nc.vector.tensor_tensor(s1, x0, w1, ALU.mult))
                return nc.vector.tensor_tensor(x, c, s, ALU.add)

            def heads_b(name, base, dst):
                for n in range(4):
                    b, tile = n // TILES, n % TILES
                    dve.wait_ge(proj_in_sbuf, JOB[name, b, tile] + 1)
                    rope_b(stage[:, n, :], tile, 8, const("cos_b")[:, HD * tile:HD * tile + HD],
                           const("sin_b")[:, HD * tile:HD * tile + HD], "halves", n).then_inc(heads_roped, 1)
                    dve.wait_ge(heads_roped, base + n + 1)
                for n in range(4):
                    heads_out(dst, n, 4, P)

            heads_b("moba_w_kv", 8, k_b)
            heads_b("moba_w_in", 12, q_b)
            attention("b", UNITS_B, 3, half_of, lambda: drain_xt(tiles=[0]))
            drain_xt(tiles=[1])
            nc.vector.memset(up_w, 0.0).then_inc(up_zeroed, 1)
            post_norm(1, "moba_w_o")

            nc.vector.memset(masked, 0.0)
            nc.vector.memset(z_t[32:33, :], 1.0)
            for tile in range(TILES):
                drain(z_t[0:32, tile * P:tile * P + P].rearrange("p (c s) -> p c s", s=P), rows=32, width=P)
            for tile in range(TILES):
                dve.wait_ge(decay_log, tile + 1)
                nc.vector.scalar_tensor_tensor(decay[:, tile, :], out_bank[tile][:], 0.0,
                                               probs[:, 2 * tile:2 * tile + 2, :].rearrange("p a b -> p (a b)"),
                                               ALU.min, ALU.subtract).then_inc(decay_ready, 1)
            dve.wait_ge(proj_in_sbuf, JOB["w_in_2", 1, 1] + 1)
            v = variances("qk")
            for tile in range(TILES):
                q, k = att_q[:, tile, :], att_kv[:, tile, 0:128]
                nc.vector.tensor_tensor(tmp[:, tile, 0:512], q, q, ALU.mult)
                link(nc.vector.tensor_tensor(tmp[:, tile, 512:640], k, k, ALU.mult))
                link(nc.vector.tensor_reduce(v[:, 10 * tile:10 * tile + 10],
                                             tmp[:, tile, 0:640].rearrange("p (h d) -> p h d", h=10), AX.X, ALU.add))
            ask("qk", nc.vector.tensor_scalar(v, v, 1 / HD, RMS_EPS, ALU.mult, ALU.add))
            r = rsqrt("qk")
            for tile in range(TILES):
                at = slice(HD * tile, HD * tile + HD)
                for x, heads, first, k in ((att_q[:, tile, :], QH, 0, 0), (att_kv[:, tile, 0:128], KVH, QH, 2)):
                    x3 = x.rearrange("p (h d) -> p h d", h=heads)
                    link(nc.vector.tensor_tensor(x3, x3, r[:, 10 * tile + first:10 * tile + first + heads].rearrange(
                        "p (h a) -> p h a", a=1).to_broadcast([P, heads, HD]), ALU.mult))
                    link(rope_b(x, tile, heads, rope_g[:, k, at], rope_g[:, k + 1, at], "pairs", 0))
                for kv in range(KVH):
                    last = nc.vector.tensor_copy(
                        key2[:, tile, 128 * kv:128 * kv + 128].rearrange("p (c d) -> p c d", c=2),
                        att_kv[:, tile, HD * kv:HD * kv + HD].rearrange("p (c d) -> p c d", c=1).to_broadcast(
                            [P, 2, HD]))
                last.then_inc(gqa_ready, 1)
            for tile in range(TILES):
                drain(gla_t[:, :, tile * P:tile * P + P])
            dve.wait_ge(tr_in_sbuf, TR["gla"] + 2)
            for n, (tile, way) in enumerate([(i, j) for i in range(TILES) for j in range(2)]):
                at = slice(tile * P, tile * P + P)
                dve.wait_ge(cum_exp, n + 1)
                nc.vector.tensor_tensor(q_in[:, way, :, at], exp_b[:, way, :, at], gla_t[:, 0:2, at], ALU.mult)
                nc.vector.tensor_tensor(exp_q[:, way, :, at], exp_q[:, way, :, at], gla_t[:, 0:2, at], ALU.mult)
                nc.vector.tensor_tensor(exp_k[:, way, :, at], exp_k[:, way, :, at], gla_t[:, 2:4, at], ALU.mult)
                nc.vector.tensor_tensor(k_out[:, tile, way, :], k_out[:, tile, way, :], gla_qk[:, tile, GW:512],
                                        ALU.mult).then_inc(gla_operands, 1)
            for tile in range(TILES):
                drain(q_g[:, :, tile * P:tile * P + P])
            for tile in range(TILES):
                drain(k_g[:, :, tile * P:tile * P + P], width=2 * P)
            dve.wait_ge(gla_operands, 4)
            for n, (way, step) in enumerate(KV_ORDER):
                chunk = step if way == 0 else NCHUNK - 1 - step
                src = score_bank[chunk % 2][:].rearrange("p (a e) -> p a e", a=2)
                dst = state_of(way, step)
                dve.wait_ge(kv_in_psum, n + 1)
                if step == 0:
                    nc.vector.tensor_copy(dst, src).then_inc(state_ready, 1)
                else:
                    last_token = CHUNK * chunk + (CHUNK - 1 if way == 0 else 0)
                    dve.wait_ge(state_ready, n - 1)
                    for pair in range(2):
                        last = nc.vector.scalar_tensor_tensor(
                            dst[:, pair, :], state_of(way, step - 1)[:, pair, :],
                            exp_b[:, way, pair, last_token:last_token + 1], src[:, pair, :], ALU.mult, ALU.add)
                    last.then_inc(state_ready, 1)
            for tile in range(TILES):
                for way in range(2):
                    mask = const("cum_fwd" if way == 0 else "cum_bwd")[:, P:2 * P].bitcast(I32)
                    for odd in range(2):
                        dve.wait_ge(gla_scores, 4 * tile + 2 * way + odd + 1)
                        if tile:
                            dve.wait_ge(gla_intra, tile)
                        dst = masked[:, way, :].rearrange("p (a o s) -> p a o s", a=2, o=2)[:, :, odd, :]
                        src = score_bank[odd][:, 0:2 * P].rearrange("p (a s) -> p a s", a=2)
                        for pair in range(2):
                            last = nc.vector.copy_predicated(dst[:, pair, :], mask, src[:, pair, :])
                        last.then_inc(gla_masked, 1)
                dve.wait_ge(gla_copied, tile + 1)
                dve.wait_ge(gla_inter, tile + 1)
                for odd in range(2):
                    o = wide[:, tile, 0:512].rearrange("p (a o e) -> p a o e", a=2, o=2)[:, :, odd, :]
                    last = nc.vector.tensor_tensor(o, o, out_bank[odd][:, 0:256].rearrange("p (a e) -> p a e", a=2),
                                                   ALU.add)
                last.then_inc(gla_summed, 1)
            dve.wait_ge(gla_summed, 2)

            def gla_variances():
                v = variances("gla")
                for tile in range(TILES):
                    o = wide[:, tile, 0:512]
                    link(nc.vector.tensor_tensor(tmp[:, tile, 0:512], o, o, ALU.mult))
                    link(nc.vector.tensor_reduce(v[:, 4 * tile:4 * tile + 4],
                                                 tmp[:, tile, 0:512].rearrange("p (h d) -> p h d", h=4), AX.X, ALU.add))
                ask("gla", nc.vector.tensor_scalar(v, v, 1 / GDV, RMS_EPS, ALU.mult, ALU.add))

            def gla_scaled(tile):
                r = rsqrt("gla")
                o = wide[:, tile, 0:512].rearrange("p (h d) -> p h d", h=4)
                link(nc.vector.tensor_tensor(o, o, r[:, 4 * tile:4 * tile + 4].rearrange(
                    "p (h a) -> p h a", a=1).to_broadcast([P, 4, GDV]), ALU.mult))
                link(nc.vector.tensor_tensor(wide[:, tile, 0:512], wide[:, tile, 0:512], gate[:, tile, 0:512],
                                             ALU.mult))

            def att_variance(tile):
                v = variances(f"att{tile}")
                link(nc.vector.tensor_tensor(tmp[:, tile, 0:512], wide[:, tile, 512:1024], wide[:, tile, 512:1024],
                                             ALU.mult))
                link(nc.vector.tensor_reduce(v, tmp[:, tile, 0:512], AX.X, ALU.add))
                ask(f"att{tile}", nc.vector.tensor_scalar(v, v, 1 / 512, RMS_EPS, ALU.mult, ALU.add))

            def att_scaled(tile):
                nc.vector.tensor_scalar(wide[:, tile, 512:1024], wide[:, tile, 512:1024], rsqrt(f"att{tile}"), None,
                                        ALU.mult).then_inc(mixed_ready, 1)

            attention("g", UNITS_G, 3, lambda tile, group: wide[:, tile, 512:1024],
                      lambda: drain_xt(GAIN_MIX, [0]),
                      {5: gla_variances, 8: lambda: gla_scaled(0), 11: lambda: gla_scaled(1),
                       13: lambda: att_variance(0), 15: lambda: att_scaled(0)})
            att_variance(1)
            att_scaled(1)
            drain_xt(GAIN_MIX, [1])
            for tile in range(TILES):
                for b in range(2):
                    half = slice(512 * b, 512 * b + 512)
                    dve.wait_ge(proj_in_sbuf, JOB["w_out_2", b, tile] + 1)
                    last = nc.vector.tensor_tensor(res[:, tile, half], res[:, tile, half], wide[:, tile, half], ALU.add)
                last.then_inc(res_ready, 1)
                r = rms_of_stream("norm2", 4, tile)
                if tile == 0:
                    dve.wait_ge(row_landed, 64)
                dst = routed[:, tile].rearrange("p c k -> p k c")
                nc.vector.scalar_tensor_tensor(dst, res[:, tile, :].rearrange("p (k c) -> p k c", c=KD), r,
                                               norm2_row.rearrange("p (k c) -> p k c", c=KD),
                                               ALU.mult, ALU.mult).then_inc(routed_ready, 1)
            drain_xt()

            dve.wait_ge(proj_in_sbuf, len(JOBS) + 1)
            logits = small[:, 0:144].rearrange("p (t n) -> p t n", t=TILES)

            def over_tiles(a):
                return a.rearrange("p (t n) -> p t n", t=1).to_broadcast([P, TILES, a.shape[-1]])

            def over(a, n):
                return a.rearrange("p (t n) -> p t n", n=1).to_broadcast([P, TILES, n])

            def view(a, n):
                return tmp[:, 0, a:a + TILES * n].rearrange("p (t n) -> p t n", t=TILES)

            link(nc.vector.tensor_tensor(logits, logits, over_tiles(router_b[:]), ALU.add))
            scal = small[:, 160:180]
            g_log, e_log = logits[:, :, 0:NG], logits[:, :, NG:]

            def first_max(x, n, top, is_top, work, best, out):
                link(nc.vector.tensor_reduce(top, x, AX.X, ALU.max))
                link(nc.vector.tensor_tensor(is_top, x, over(top, n), ALU.is_equal))
                link(nc.vector.tensor_tensor(work, is_top, over_tiles(const("desc")[:, NE - n:NE]), ALU.mult))
                link(nc.vector.tensor_reduce(best, work, AX.X, ALU.max))
                link(nc.vector.tensor_tensor(out, work, over(best, n), ALU.is_equal))

            g_top, g_best = scal[:, 0:2], scal[:, 2:4]
            g_is, g_work, g_hot = view(0, NG), view(16, NG), view(32, NG)
            first_max(g_log, NG, g_top, g_is, g_work, g_best, g_hot)
            nc.vector.tensor_tensor(view(48, NG), g_log, over(g_top, NG), ALU.subtract).then_inc(mask_ready, 1)
            g_low = view(64, NG)
            link(nc.vector.tensor_scalar(g_low, g_hot, -1.0, BIG, ALU.add, ALU.mult))
            for tile in range(TILES):
                e3 = e_log[:, tile, :].rearrange("p (g e) -> p g e", g=NG)
                last = nc.vector.tensor_tensor(e3, e3, g_low[:, tile, :].rearrange("p (g a) -> p g a", a=1).to_broadcast(
                    [P, NG, EPG]), ALU.add)
            link(last)
            e_is, e_work = view(128, NE), view(256, NE)
            hot1, hot2 = view(384, NE), view(512, NE)
            top1, top2, best1, best2 = (scal[:, 4 + 2 * i:6 + 2 * i] for i in range(4))
            first_max(e_log, NE, top1, e_is, e_work, best1, hot1)
            e2 = view(640, NE)
            link(nc.vector.scalar_tensor_tensor(e2, hot1, -2 * BIG, e_log, ALU.mult, ALU.add))
            first_max(e2, NE, top2, e_is, e_work, best2, hot2)
            nc.vector.tensor_tensor(top_diff, top2, top1, ALU.subtract).then_inc(mask_ready, 1)
            mask = view(768, NE)
            nc.vector.tensor_tensor(mask, hot1, hot2, ALU.add).then_inc(mask_ready, 1)
            dve.wait_ge(gates_exp, 2)
            g_sum = small[:, 180:182]
            link(nc.vector.tensor_reduce(g_sum, g_exp.rearrange("p (t n) -> p t n", t=TILES), AX.X, ALU.add))
            link(nc.vector.tensor_scalar(scal[:, 14:16], ratio, 1.0, None, ALU.add))
            link(nc.vector.tensor_tensor(scal[:, 16:18], scal[:, 14:16], g_sum, ALU.mult))
            link(nc.vector.reciprocal(scal[:, 16:18], scal[:, 16:18]))
            link(nc.vector.tensor_tensor(scal[:, 18:20], scal[:, 16:18], ratio, ALU.mult))
            nc.vector.tensor_tensor(hot1, hot1, over(scal[:, 16:18], NE), ALU.mult)
            link(nc.vector.tensor_tensor(hot2, hot2, over(scal[:, 18:20], NE), ALU.mult))
            link(nc.vector.tensor_tensor(gates[:], hot1, hot2, ALU.add))
            dve.wait_ge(ranks_in_psum, 1)
            dve.wait_ge(mask_ready, 3)
            link(nc.vector.tensor_tensor(rank[:], proj_bank[1][:, 0:2 * NE].rearrange("p (t n) -> p t n", t=TILES),
                                         mask, ALU.mult))
            link(nc.vector.tensor_scalar(rank[:], rank[:], -1.0, None, ALU.add))
            link(nc.vector.tensor_reduce(small[:, 182:183], proj_bank[1][:, 2 * NE:3 * NE], AX.X, ALU.max))
            nc.vector.tensor_copy(largest[:], small[:, 182:183]).then_inc(routing_ready, 1)

            def expert_rounds(rounds, base):
                with dve.Fori(0, rounds) as r:
                    n = base + r
                    for tile in range(TILES):
                        nc.vector.tensor_tensor(
                            onehot[:, tile, :].rearrange("p (e s) -> p e s", e=GROUP),
                            const("iota").rearrange("p (e s) -> p e s", e=1).to_broadcast([P, GROUP, SLOTS]),
                            rank[:, tile, bass.ds(GROUP * r, GROUP)].rearrange("p (e s) -> p e s", s=1).to_broadcast(
                                [P, GROUP, SLOTS]), ALU.is_equal).then_inc(onehot_ready, 1)
                    dve.wait_ge(onehot_ready, 3 * n + 2)
                    for tile in range(TILES):
                        last = nc.vector.tensor_tensor(
                            weighted[:, tile, :].rearrange("p (e s) -> p e s", e=GROUP),
                            onehot[:, tile, :].rearrange("p (e s) -> p e s", e=GROUP),
                            gates[:, tile, bass.ds(GROUP * r, GROUP)].rearrange("p (e s) -> p e s", s=1).to_broadcast(
                                [P, GROUP, SLOTS]), ALU.mult)
                    last.then_inc(onehot_ready, 1)
                    dve.wait_ge(back_in_psum, n + 1)
                    nc.vector.tensor_copy(back, bank[3][:, 0:256]).then_inc(back_ready, 1)
                    for i in range(GROUP):
                        x = GROUP * n + i
                        dve.wait_ge(silu_done, x + 1)
                        nc.vector.tensor_tensor(hidden, act_g, bank[2][:, P:2 * P], ALU.mult).then_inc(hidden_ready, 1)
                        dve.wait_ge(hidden_t_in_psum, x + 1)
                        nc.vector.tensor_copy(hidden_t, bank[3][:, 256:384]).then_inc(hidden_t_ready, 1)
                        dve.wait_ge(down_in_psum, x + 1)
                        nc.vector.tensor_copy(expert_out[SLOTS * i:SLOTS * i + SLOTS, 512:768], bank[4][64:96, 0:256])
                        nc.vector.tensor_copy(expert_out[SLOTS * i:SLOTS * i + SLOTS, 768:1024],
                                              bank[4][96:128, 0:256]).then_inc(down_drained_dve, 1)
                    for k in range(4):
                        tile, half = k // 2, k % 2
                        dve.wait_ge(sum_in_psum, 4 * n + (k + 1))
                        dst = res[:, tile, 512 * half:512 * half + 512]
                        nc.vector.tensor_tensor(dst, dst, bank[5 + k % 3][:], ALU.add).then_inc(sum_added, 1)

            expert_rounds(ROUNDS, 0)
            dve.wait_ge(sum_added, 4 * ROUNDS)
            most = dve.value_load(largest[0:1, 0:1], min_val=0, max_val=SEQ)
            with dve.If(most > SLOTS):
                with dve.Fori(1, PASSES) as p:
                    dve.wait_ge(onehot_ready, 3 * ROUNDS * p)
                    nc.vector.tensor_scalar(rank[:], rank[:], -float(SLOTS), None, ALU.add).then_inc(rank_moved, 1)
                    dve.wait_ge(rank_moved, p)
                    nc.vector.memset(small[:, 150:151], 0.0)
                    expert_rounds(ROUNDS, ROUNDS * p)
                dve.wait_ge(sum_added, 4 * ROUNDS * PASSES)

            for tile in range(TILES):
                nc.vector.memset(small[:, 150 + tile:151 + tile], 0.0).then_inc(res_ready, 1)
            for tile in range(TILES):
                r = rms_of_stream("final", 6, tile)
                nc.vector.scalar_tensor_tensor(wide[:, tile, :], res[:, tile, :], r, final_row, ALU.mult,
                                               ALU.mult).then_inc(out_ready, 1)

        @block.tensor
        def _(pe):
            tr = [0]

            def transposes(blocks):
                n = tr[0]
                if n >= 2:
                    pe.wait_ge(tr_in_sbuf, n - 1)
                for i, x in enumerate(blocks):
                    rows, cols = x.shape[0], x.shape[-1]
                    last = nc.tensor.transpose(tr_bank[n % 2][0:cols, P * i:P * i + rows], x, ident[0:rows, 0:rows])
                last.then_inc(tr_in_psum, 1)
                tr[0] += 1

            def transpose_rows(src, tile, half):
                transposes([src[:, tile, P * c:P * c + P] for c in range(4 * half, 4 * half + 4)])

            landed = set()

            def project(job, between=()):
                n = JOB[job]
                name, part, tile = job
                b = block_of(job)
                _, kc, _, width = BLOCKS[b]
                w = ring[:, b % RING, 0:kc * width].rearrange("p (c n) -> p c n", c=kc)
                if name == "mla_w_ukv":
                    w = w[:, :, 512 * part:512 * part + 512]
                    width = 512
                if b not in landed:
                    landed.add(b)
                    pe.wait_ge(block_landed[b % RING], 16 * (b // RING + 1))
                if n >= 2:
                    pe.wait_ge(proj_in_sbuf, n - 1)
                first = 6 if name == "mla_w_ukv" else 0
                for c in range(kc):
                    if c in between:
                        between[c]()
                    last = nc.tensor.matmul(proj_bank[n % 2][:, 0:width], xt[:, first + c, tile * P:tile * P + P],
                                            w[:, c, :], start=(c == 0), stop=(c == kc - 1))
                last.then_inc(proj_in_psum, 1)

            def xt_ready():
                pe.wait_ge(tr_in_sbuf, tr[0])

            def attention(kind, units, depth, scores, values, tail):
                for u in range(units + depth + 1):
                    if u < units:
                        n = UNIT0[kind] + u
                        h, tile = unit_of(u)
                        keys = keys_of(kind, tile)
                        if u >= 4:
                            pe.wait_ge(probs_done, n - 3)
                        lhs, rhs = scores(h, tile, keys)
                        causal = kind != "g"
                        last = nc.tensor.matmul(score_bank[u % 4][:, 0:keys], lhs, rhs, start=True, stop=not causal)
                        if causal:
                            last = nc.tensor.matmul(score_bank[u % 4][:, keys - P:keys], ident_b[:], causal_b[:],
                                                    start=False, stop=True)
                        last.then_inc(scores_in_psum, 1)
                    m = u - depth
                    if 0 <= m < units:
                        pe.wait_ge(probs_done, UNIT0[kind] + m + 1)
                        transposes([probs[:, m % 4, P * k:P * k + P] for k in range(keys_of(kind, unit_of(m)[1]) // P)])
                    if m == units - 1:
                        tail()
                    m = u - depth - 1
                    if m >= 0:
                        h, tile = unit_of(m)
                        group = h // 8
                        pe.wait_ge(tr_in_sbuf, TR["att_" + kind] + m + 1)
                        if h % 8 == 0 and group:
                            pe.wait_ge(out_drained, OUT0[kind] + tile + 1)
                        blocks = keys_of(kind, tile) // P
                        for k in range(blocks):
                            last = nc.tensor.matmul(out_bank[tile][:, HD * (h % 8):HD * (h % 8) + HD],
                                                    probs_t[:, m % 2, P * k:P * k + P], values(h, k),
                                                    start=(k == 0), stop=(k == blocks - 1))
                        if h % 8 == 7:
                            last.then_inc(out_in_psum, 1)

            def first_jobs(name, src, ready, blocks=1):
                for tile in range(TILES):
                    pe.wait_ge(*ready(tile))
                    for half in range(2):
                        transpose_rows(src, tile, half)
                    xt_ready()
                    for b in range(blocks):
                        project((name, b, tile))

            pe.wait_ge(ident_landed, 16)
            first_jobs("mla_w_in", res, lambda tile: (x_landed, 16))
            pe.wait_ge(gains_landed, 128)
            transposes([gain_rows])
            for b in range(1, 5):
                for tile in range(TILES):
                    project(("mla_w_in", b, tile))
            for tile in range(TILES):
                pe.wait_ge(latents_normed, tile + 1)
                for half in range(2):
                    transpose_rows(wide, tile, half)
            xt_ready()

            def staged_heads(n, width):
                return [stage[:, n % 4, width * i:width * i + width] for i in range(4)]

            for n in range(8 + LAG):
                if n < 8:
                    project(("mla_w_uq", n // TILES, n % TILES))
                if n >= LAG:
                    pe.wait_ge(heads_roped, n - LAG + 1)
                    transposes(staged_heads(n - LAG, QKD))
            for n in range(8 + LAG):
                if n < 8:
                    project(("mla_w_ukv", n // TILES, n % TILES))
                if n >= LAG:
                    m = n - LAG
                    pe.wait_ge(proj_in_sbuf, JOB["mla_w_ukv", m // TILES, m % TILES] + 1)
                    transposes(staged_heads(m, QKD))
            xt_ready()
            pe.wait_ge(proj_in_sbuf, JOB["mla_w_ukv", 3, 1] + 1)
            pe.wait_ge(masks_cast, 1)

            def scores_a(h, tile, keys):
                return q_a[0:QKD, h, tile * P:tile * P + P], k_a[0:QKD, h, 0:keys]

            def values_ab(h, k):
                return val[:, k, HD * h:HD * h + HD]

            def mixed_transposed(before, tile):
                for half in range(2):
                    pe.wait_ge(mixed_ready, before + 2 * half + tile + 1)
                    transpose_rows(wide, tile, half)

            def output_projection(name, transposed):
                xt_ready()
                project((name, 0, 0))
                transposed(1)
                project((name, 1, 0))
                xt_ready()
                for b in range(2):
                    project((name, b, 1))

            attention("a", UNITS_A, 3, scores_a, values_ab, lambda: mixed_transposed(0, 0))
            output_projection("mla_w_o", lambda tile: mixed_transposed(0, tile))

            first_jobs("moba_w_kv", res, lambda tile: (res_ready, tile + 1))

            def heads_back(n, roped):
                pe.wait_ge(heads_roped, roped + n + 1)
                transposes(staged_heads(n, P))

            for n in range(2, 8):
                project(("moba_w_kv", n // TILES, n % TILES))
                if 0 <= n - 3 < 4:
                    heads_back(n - 3, 8)
            for n in range(8):
                project(("moba_w_in", n // TILES, n % TILES))
                if 0 <= n - 3 < 4:
                    heads_back(n - 3, 12)
            xt_ready()
            pe.wait_ge(proj_in_sbuf, JOB["moba_w_in", 3, 1] + 1)

            def scores_b(h, tile, keys):
                at = slice(HD * (h % 2), HD * (h % 2) + HD)
                return q_b[at, h // 2, tile * P:tile * P + P], k_b[at, h // 2, 0:keys]

            attention("b", UNITS_B, 3, scores_b, values_ab, lambda: mixed_transposed(4, 0))
            output_projection("moba_w_o", lambda tile: mixed_transposed(4, tile))

            first_jobs("w_in_2", wide, lambda tile: (normed_ready, tile + 1), 2)
            for tile in range(TILES):
                pe.wait_ge(proj_in_sbuf, JOB["w_in_2", 0, tile] + 1)
                transposes([z_in[:, tile, :]])
            xt_ready()
            pe.wait_ge(up_landed, 64)
            for tile in range(TILES):
                nc.tensor.matmul(out_bank[tile][:], z_t[0:33, tile * P:tile * P + P], up_w, start=True,
                                 stop=True).then_inc(decay_in_psum, 1)
            project(("w_in_2", 2, 0))
            project(("w_in_2", 2, 1))

            def cumulate(n):
                tile, way = n // 2, n % 2
                if n < 2:
                    pe.wait_ge(decay_ready, n + 1)
                if n == 2:
                    pe.wait_ge(cum_exp, 2)
                name = "fwd" if way == 0 else "bwd"
                for pair in range(2):
                    nc.tensor.matmul(score_bank[n % 2][:, 256 * pair:256 * pair + 256],
                                     decay[:, tile, GW * way + P * pair:GW * way + P * pair + P],
                                     const("cum_" + name), start=True, stop=True)
                nc.tensor.matmul(out_bank[n % 2][:, 0:GW], const("rest_" + name),
                                 decay[:, tile, GW * way:GW * way + GW], start=True, stop=True).then_inc(
                    cum_in_psum, 1)

            cumulate(0)
            cumulate(1)
            for tile in range(TILES):
                pe.wait_ge(proj_in_sbuf, JOB["w_in_2", 2, tile] + 1)
                transposes([gla_qk[:, tile, P * c:P * c + P] for c in range(4)])
            project(("w_in_2", 3, 0))
            cumulate(2)
            cumulate(3)
            project(("w_in_2", 3, 1))
            for tile in range(TILES):
                pe.wait_ge(gqa_ready, tile + 1)
                transposes([att_q[:, tile, P * c:P * c + P] for c in range(4)])
            for tile in range(TILES):
                transposes([key2[:, tile, P * c:P * c + P] for c in range(KVH)])

            def chunk_sums(n):
                way, step = KV_ORDER[n]
                chunk = step if way == 0 else NCHUNK - 1 - step
                tile, rows = chunk // 2, slice(CHUNK * (chunk % 2), CHUNK * (chunk % 2) + CHUNK)
                if n == 0:
                    pe.wait_ge(gla_operands, 4)
                    pe.wait_ge(proj_in_sbuf, JOB["w_in_2", 3, 1] + 1)
                if n >= 2:
                    pe.wait_ge(state_ready, n)
                for pair in range(2):
                    last = nc.tensor.matmul(score_bank[chunk % 2][:, 256 * pair:256 * pair + 256],
                                            k_out[rows, tile, way, P * pair:P * pair + P],
                                            val[rows, tile, 256 * pair:256 * pair + 256], start=True, stop=True)
                last.then_inc(kv_in_psum, 1)

            def chunk_scores(j):
                tile, way, odd = j // 4, j // 2 % 2, j % 2
                at = slice(tile * P, tile * P + P)
                rows = slice(GDK * odd, GDK * odd + GDK)
                if j == 0:
                    pe.wait_ge(state_ready, len(KV_ORDER))
                if j >= 2:
                    pe.wait_ge(gla_masked, j - 1)
                for pair in range(2):
                    last = nc.tensor.matmul(score_bank[odd][:, P * pair:P * pair + P], exp_k[rows, way, pair, at],
                                            exp_q[rows, way, pair, at], start=True, stop=True)
                last.then_inc(gla_scores, 1)

            project(("w_in_2", 4, 0), {c: (lambda n=n: (chunk_sums(n), chunk_sums(n + 1)))
                                       for c, n in ((1, 0), (4, 2), (7, 4))})
            project(("w_in_2", 4, 1), {c: (lambda j=j: (chunk_scores(j), chunk_scores(j + 1)))
                                       for c, j in ((3, 0), (6, 2))})
            for tile in range(TILES):
                if tile:
                    for j in range(4, 8):
                        chunk_scores(j)
                if tile:
                    pe.wait_ge(gla_summed, tile)
                for h in range(GH):
                    pair, odd = h // 2, h % 2
                    rows = slice(GDK * odd, GDK * odd + GDK)
                    for j in range(2):
                        chunk = 2 * tile + j
                        ways = [(0, chunk - 1)] * (chunk > 0) + [(1, NCHUNK - 2 - chunk)] * (chunk < NCHUNK - 1)
                        for k, (way, step) in enumerate(ways):
                            last = nc.tensor.matmul(
                                out_bank[odd][CHUNK * j:CHUNK * j + CHUNK, GDV * pair:GDV * pair + GDV],
                                q_in[rows, way, pair, CHUNK * chunk:CHUNK * chunk + CHUNK],
                                state_of(way, step)[rows, pair, GDV * odd:GDV * odd + GDV],
                                start=(k == 0), stop=(k == len(ways) - 1))
                last.then_inc(gla_inter, 1)
                pe.wait_ge(gla_masked, 4 * tile + 4)
                pe.wait_ge(proj_in_sbuf, JOB["w_in_2", 4, tile] + 1)
                for h in range(GH):
                    for way in range(2):
                        last = nc.tensor.matmul(proj_bank[tile][:, GDV * h:GDV * h + GDV],
                                                masked[:, way, P * h:P * h + P],
                                                val[:, tile, GDV * h:GDV * h + GDV],
                                                start=(way == 0), stop=(way == 1))
                last.then_inc(gla_intra, 1)
            pe.wait_ge(gla_copied, 2)
            pe.wait_ge(gla_summed, 2)

            def scores_g(h, tile, keys):
                at = slice(HD * (h % 2), HD * (h % 2) + HD)
                return q_g[at, h // 2, tile * P:tile * P + P], k_g[at, h // (QH // KVH), 0:keys]

            def mixed_g_transposed(tile):
                pe.wait_ge(mixed_ready, 8 + tile + 1)
                for half in range(2):
                    transpose_rows(wide, tile, half)

            attention("g", UNITS_G, 3, scores_g,
                      lambda h, k: att_kv[:, k, 128 + HD * (h // (QH // KVH)):128 + HD * (h // (QH // KVH)) + HD],
                      lambda: mixed_g_transposed(0))
            output_projection("w_out_2", mixed_g_transposed)

            for tile in range(TILES):
                pe.wait_ge(routed_ready, tile + 1)
                for half in range(2):
                    transpose_rows(wide, tile, half)
            xt_ready()
            pe.wait_ge(row_landed, 64)
            for tile in range(TILES):
                for c in range(KD):
                    last = nc.tensor.matmul(proj_bank[0][:, 72 * tile:72 * tile + 72], xt[:, c, tile * P:tile * P + P],
                                            router_w[:, c, :], start=(c == 0), stop=(c == KD - 1))
            last.then_inc(logits_in_psum, 1)
            pe.wait_ge(mask_ready, 3)
            mask = tmp[:, 0, 768:768 + 2 * NE]
            for n, (first, second) in enumerate((("tri", None), ("ones", "tri"), ("ones", "ones"))):
                dst = proj_bank[1][:, NE * n:NE * n + NE]
                last = nc.tensor.matmul(dst, const(first), mask[:, 0:NE], start=True, stop=second is None)
                if second:
                    last = nc.tensor.matmul(dst, const(second), mask[:, NE:2 * NE], start=False, stop=True)
            last.then_inc(ranks_in_psum, 1)

            def expert_rounds(rounds, base):
                with pe.Fori(0, rounds) as r:
                    n = base + r
                    pe.wait_ge(onehot_ready, 3 * n + 2)
                    for c in range(KD):
                        for tile in range(TILES):
                            last = nc.tensor.matmul(bank[c // 4][:, P * (c % 4):P * (c % 4) + P],
                                                    routed[:, tile, c, :], onehot[:, tile, :], start=(tile == 0),
                                                    stop=(tile == TILES - 1))
                        if c % 4 == 3:
                            last.then_inc(picked_in_psum, 1)
                    pe.wait_ge(onehot_ready, 3 * n + 3)
                    for tile in range(TILES):
                        last = nc.tensor.transpose(bank[3][:, P * tile:P * tile + P], weighted[:, tile, :], ident)
                    last.then_inc(back_in_psum, 1)
                    pe.wait_ge(picked_ready, 2 * n + 2)
                    for i in range(GROUP):
                        x = GROUP * n + i
                        base_slot = 3 * (i % 2)
                        pe.wait_ge(gate_up_landed[i % 2], 64 * n + (32 * (i // 2) + 32))
                        both = ring[:, base_slot:base_slot + 2, :].rearrange("p m (c f) -> p m c f", c=KD)
                        for c in range(KD):
                            for j in range(4):
                                last = nc.tensor.matmul(bank[2][SLOTS * j:SLOTS * j + SLOTS, 0:256],
                                                        picked[:, c, SLOTS * i:SLOTS * i + SLOTS],
                                                        both[:, :, c, P * j:P * j + P], start=(c == 0),
                                                        stop=(c == KD - 1))
                        last.then_inc(hidden_in_psum, 1)
                        pe.wait_ge(hidden_ready, x + 1)
                        nc.tensor.transpose(bank[3][:, 256:384], hidden, ident).then_inc(hidden_t_in_psum, 1)
                        pe.wait_ge(hidden_t_ready, x + 1)
                        pe.wait_ge(down_landed[i % 2], 32 * n + (16 * (i // 2) + 16))
                        if i:
                            pe.wait_ge(down_drained_act, x)
                            pe.wait_ge(down_drained_dve, x)
                        down = ring[:, base_slot + 2, :].rearrange("p (k d) -> p k d", k=4)
                        for k in range(4):
                            for j in range(4):
                                last = nc.tensor.matmul(bank[4][SLOTS * j:SLOTS * j + SLOTS, 0:256],
                                                        hidden_t[:, SLOTS * k:SLOTS * k + SLOTS],
                                                        down[:, k, 256 * j:256 * j + 256], start=(k == 0),
                                                        stop=(k == 3))
                        last.then_inc(down_in_psum, 1)
                    pe.wait_ge(back_ready, n + 1)
                    pe.wait_ge(down_drained_act, GROUP * n + GROUP)
                    pe.wait_ge(down_drained_dve, GROUP * n + GROUP)
                    for k in range(4):
                        tile, half = k // 2, k % 2
                        if k == 3:
                            pe.wait_ge(sum_added, 4 * n + 1)
                        nc.tensor.matmul(bank[5 + k % 3][:], back[:, P * tile:P * tile + P],
                                         expert_out[:, 512 * half:512 * half + 512], start=True,
                                         stop=True).then_inc(sum_in_psum, 1)

            expert_rounds(ROUNDS, 0)
            most = pe.value_load(largest[0:1, 0:1], min_val=0, max_val=SEQ)
            with pe.If(most > SLOTS):
                with pe.Fori(1, PASSES) as p:
                    expert_rounds(ROUNDS, ROUNDS * p)


def kernel(**inputs):
    import concourse.bacc as bacc
    from concourse.bass_utils import run_bass_kernel_spmd as run

    nc = bacc.Bacc("TRN2", target_bir_lowering=False, num_devices=1)
    arrays = {name: np.ascontiguousarray(a) for name, a in inputs.items()}
    arrays["consts"] = np.concatenate(list(shape_constants().values()), axis=1)
    t = {name: nc.dram_tensor(f"in_{name}", a.shape, F32, kind="ExternalInput").ap() for name, a in arrays.items()}
    t["out"] = nc.dram_tensor("out_0", inputs["x"].shape, F32, kind="ExternalOutput").ap()
    build(nc, t)
    r = run(nc, [{f"in_{name}": a for name, a in arrays.items()}], core_ids=[0])
    return r.results[0]["out_0"]
```

```python
from contextlib import ExitStack

import numpy as np

import concourse.bass as bass
from concourse import mybir

ALU = mybir.AluOpType
ACT = mybir.ActivationFunctionType
AX = mybir.AxisListType
F32 = mybir.dt.float32
F32R = mybir.dt.float32r
BF16 = mybir.dt.bfloat16
I32 = mybir.dt.int32

P = 128
D = 1024
SEQ = 256
TILES = SEQ // P
KD = D // P

H = 16
NOPE, ROPE, VD = 64, 32, 64
QKD = NOPE + ROPE
Q_LORA, KV_LORA = 768, 256
HD = 64
SCALE_A = QKD ** -0.5
SCALE_B = HD ** -0.5
ALPHA = 4 ** 0.25
LN_EPS = 1e-5
RMS_EPS = 1e-6

GH, GDK, GDV = 4, 64, 128
GW = GH * GDK
CHUNK = 64
NCHUNK = SEQ // CHUNK
QH, KVH = 8, 2

NG, EPG = 8, 8
NE = NG * EPG
FE = 512
SLOTS = 32
GROUP = 4
ROUNDS = NE // GROUP
PASSES = SEQ // SLOTS
BIG = 1e30

RING = 6
SLOT = 4096
LAG = 2

BLOCKS = (
    [("mla_w_in", 8, a, n) for a, n in ((0, 512), (512, 512), (1024, 416), (1440, 320), (1760, 320))]
    + [("mla_w_uq", 6, 384 * b, 384) for b in range(4)]
    + [("mla_w_ukv", 2, 0, 2048)]
    + [("mla_w_o", 8, 512 * b, 512) for b in range(2)]
    + [("moba_w_kv", 8, 512 * b, 512) for b in range(4)]
    + [("moba_w_in", 8, 512 * b, 512) for b in range(4)]
    + [("moba_w_o", 8, 512 * b, 512) for b in range(2)]
    + [("w_in_2", 8, a, n) for a, n in ((1536, 416), (1952, 384), (0, 512), (512, 512), (1024, 512))]
    + [("w_out_2", 8, 512 * b, 512) for b in range(2)]
)


JOBS = []
for _name, _n, _tile_outer in (("mla_w_in", 5, 0), ("mla_w_uq", 4, 0), ("mla_w_ukv", 4, 0), ("mla_w_o", 2, 1),
                               ("moba_w_kv", 4, 0), ("moba_w_in", 4, 0), ("moba_w_o", 2, 1),
                               ("w_in_2", 5, 0), ("w_out_2", 2, 1)):
    if _name == "w_in_2":
        JOBS += [(_name, b, t) for t in range(TILES) for b in range(2)]
        JOBS += [(_name, b, t) for b in range(2, _n) for t in range(TILES)]
    elif _tile_outer:
        JOBS += [(_name, b, t) for t in range(TILES) for b in range(_n)]
    else:
        JOBS += [(_name, b, t) for b in range(_n) for t in range(TILES)]
JOB = {job: n for n, job in enumerate(JOBS)}


def block_of(job):
    name, b, _ = job
    first = min(i for i, x in enumerate(BLOCKS) if x[0] == name)
    return first if name == "mla_w_ukv" else first + b


LAST_JOB = [max(n for n, job in enumerate(JOBS) if block_of(job) == b) for b in range(len(BLOCKS))]

SPLIT = [n for n, block in enumerate(BLOCKS) if block[0] in ("mla_w_in", "moba_w_kv", "moba_w_in", "moba_w_o")]
OUT_B = next(b for b in SPLIT if BLOCKS[b][0] == "moba_w_o")
PAIR = {b: (b % 2 if BLOCKS[b][0] == "mla_w_in" else int(BLOCKS[b][0] == "moba_w_o" and BLOCKS[b][2] > 0))
        for b in SPLIT}

KV_ORDER = [(way, step) for step in range(SEQ // 64 - 1) for way in range(2)]

RSQRT = {}
_at = 0
for _n, (_name, _w) in enumerate((("mla", 4), ("ln0t0", 1), ("ln0t1", 1), ("ln1t0", 1), ("norm1t0", 1), ("ln1t1", 1),
                                  ("norm1t1", 1),
                                  ("qk", 20), ("gla", 8), ("att0", 1), ("att1", 1),
                                  ("norm2t0", 1), ("norm2t1", 1), ("finalt0", 1), ("finalt1", 1))):
    RSQRT[_name] = (_n, _at, _w)
    _at += _w
RSQRT_COLS = _at

GAIN_Q, GAIN_N1, GAIN_MIX, GAIN_ROWS = 0, 8, 16, 24


def shape_constants():
    f = np.float32
    tok = np.arange(SEQ, dtype=f)

    def tiled(a):
        return a.reshape(TILES, P, -1).transpose(1, 0, 2).reshape(P, -1)

    def half_tables(dim):
        inv = f(10000.0) ** (-np.arange(0, dim, 2, dtype=f) / f(dim))
        ang = (tok[:, None] * inv[None, :]).astype(f)
        c, s = np.cos(ang), np.sin(ang)
        return tiled(np.concatenate([c, c], 1)), tiled(np.concatenate([-s, s], 1))

    cos_a, sin_a = half_tables(ROPE)
    cos_b, sin_b = half_tables(HD)
    inv = f(10000.0) ** (-np.arange(0, 32, 2, dtype=f) / f(32))
    row, col = np.floor(tok / 64).astype(f), (tok % 64).astype(f)
    ang = np.concatenate([row[:, None] * inv, col[:, None] * inv], 1).astype(f)
    c, s = np.cos(ang), np.sin(ang)
    cos_g = tiled(np.repeat(c, 2, 1))
    sin_g = tiled(np.stack([-s, s], 2).reshape(SEQ, 64))
    i = np.arange(P)
    src, dst = i[:, None], i[None, :]
    same = (src // CHUNK) == (dst // CHUNK)
    fwd, bwd = same & (src <= dst), same & (src >= dst)
    mid_f, mid_b = same & (src % CHUNK <= CHUNK // 2 - 1), same & (src % CHUNK >= CHUNK // 2)
    out = {
        "ident": np.eye(P),
        "ones": np.ones((P, P)),
        "tri": src <= dst,
        "cum_fwd": np.concatenate([fwd.astype(f) - mid_f, fwd], 1),
        "cum_bwd": np.concatenate([bwd.astype(f) - mid_b, bwd], 1),
        "rest_fwd": same & (src > dst),
        "rest_bwd": same & (src < dst),
        "causal": np.where(dst > src, -BIG, 0.0),
        "cos_a": cos_a, "sin_a": sin_a, "cos_b": cos_b, "sin_b": sin_b, "cos_g": cos_g, "sin_g": sin_g,
        "iota": np.tile(np.arange(SLOTS), (P, 1)),
        "desc": np.tile(np.arange(NE, 0, -1), (P, 1)),
    }
    return {k: np.ascontiguousarray(v, dtype=f) for k, v in out.items()}


def const_layout():
    at, out = 0, {}
    for k, v in shape_constants().items():
        out[k] = (at, v.shape[1])
        at += v.shape[1]
    return out, at


def build(nc, t):
    where, const_cols = const_layout()
    with ExitStack() as ctx:
        def sb(name, shape, dt=F32):
            return ctx.enter_context(nc.sbuf_tensor(name, shape, dt))

        def sem(name):
            return ctx.enter_context(nc.semaphore(name))

        bank = [ctx.enter_context(nc.psum_tensor(f"bank{i}", [P, 512], F32)) for i in range(8)]
        proj_bank = bank[0:2]
        tr_bank = bank[2:4]
        score_bank = [bank[4], bank[5], bank[0], bank[1]]
        out_bank = bank[6:8]
        intra_bank = bank[4:6] + tr_bank

        def shared(name, shape, at):
            return nc.alloc_sbuf_tensor_at(name, shape, F32R, offset=at)

        def aligned():
            return -(-nc.sbuf_base // 32) * 32

        ring_at = aligned()
        ring = sb("ring", [P, RING, SLOT])
        ring_lo = shared("ring_lo", [P, RING, SLOT], ring_at)
        consts = sb("consts", [P, const_cols])
        res = sb("res", [P, TILES, D])
        xt_at = aligned()
        xt = sb("xt", [P, KD, SEQ])
        xt_hi = shared("xt_hi", [P, KD, SEQ], xt_at)
        xt_lo = sb("xt_lo", [P, KD, SEQ], F32R)
        expert_area = nc.alloc_sbuf_tensor_at("expert_area", [P, 2 * KD * SEQ], F32, offset=xt_at)
        gate = sb("gate", [P, TILES, D])
        wide = sb("wide", [P, TILES, D])
        val_at = aligned()
        val = sb("val", [P, TILES, D])
        stage = sb("stage", [P, 4, 512])
        early_down = nc.alloc_sbuf_tensor_at("early_down", [P, SLOT], F32, offset=val_at)
        qk_at = aligned()
        qk = sb("qk", [P, 8192])
        pieces = [[shared(f"pieces{pair}{n}", [P, SLOT // 2], qk_at + 4 * (4096 * n + 2048 * (1 - pair)))
                   for n in range(2)] for pair in range(2)]
        probs = sb("probs", [P, 4, 256])
        probs_t = sb("probs_t", [P, 2, 256])
        tmp = sb("tmp", [P, 2, 1024])
        small = sb("small", [P, 512])
        gain_rows = probs[0:GAIN_ROWS, 0, 0:P]
        head_gain = tmp[:, 1, 0:2 * HD]
        gain_cols = sb("gain_cols", [P, GAIN_ROWS])
        ident_b = sb("ident_b", [P, P], BF16)
        causal_b = sb("causal_b", [P, P], BF16)
        var = sb("var", [P, RSQRT_COLS])
        rstd = sb("rstd", [P, RSQRT_COLS])
        power = sb("power", [P, 20])
        router_w = sb("router_w", [P, KD, NG + NE])
        router_b = sb("router_b", [P, NG + NE])
        rank = sb("rank", [P, TILES, NE])
        gates = sb("gates", [P, TILES, NE])
        largest = sb("largest", [P, 1], I32)

        def const(name):
            a, n = where[name]
            return consts[:, a:a + n]

        ident = const("ident")
        q_t, k_t = qk[:, 0:4096], qk[:, 4096:8192]
        q_a = q_t.rearrange("p (h s) -> p h s", h=H)
        k_a = k_t.rearrange("p (h s) -> p h s", h=H)
        q_b = q_t[:, 0:2048].rearrange("p (h s) -> p h s", h=H // 2)
        k_b = k_t[:, 0:2048].rearrange("p (h s) -> p h s", h=H // 2)
        ln_row = tmp
        q_g = qk[:, 0:1024].rearrange("p (h s) -> p h s", h=QH // 2)
        k_g = qk[:, 1024:1536].rearrange("p (h s) -> p h s", h=KVH)
        exp_q = qk[:, 1536:2560].rearrange("p (d a s) -> p d a s", d=2, a=2)
        exp_k = qk[:, 2560:3584].rearrange("p (d a s) -> p d a s", d=2, a=2)
        exp_b = qk[:, 3584:4608].rearrange("p (d a s) -> p d a s", d=2, a=2)
        q_in = qk[:, 4608:5632].rearrange("p (d a s) -> p d a s", d=2, a=2)
        k_out = qk[:, 5632:6656].rearrange("p (t d n) -> p t d n", t=2, d=2)
        gla_t = qk[:, 6656:7680].rearrange("p (c s) -> p c s", c=4)
        z_t = qk[:, 7680:7936]
        gla_qk = stage[:, 0:2, :]
        decay = stage[:, 2:4, :]
        state = stage.rearrange("p n (a e) -> p n a e", a=2)
        state_b = val[:, :, 512:1024].rearrange("p t (a e) -> p t a e", a=2)
        att_q = gate[:, :, 512:1024]
        att_kv = sb("att_kv", [P, TILES, 256])
        key2 = probs_t
        z_in = sb("z_in", [P, TILES, 32])
        up_w = probs[0:33, 2:4, :].rearrange("p a b -> p (a b)")
        rope_g = sb("rope_g", [P, 4, 128])
        masked = wide[:, :, 512:1024]
        norm2_row, final_row = gate[:, 0, :], gate[:, 1, :]
        extra = qk.rearrange("p (m n) -> p m n", m=2)
        picked = expert_area[:, 0:1024].rearrange("p (c s) -> p c s", c=KD)
        onehot = expert_area[:, 1024:1280].rearrange("p (t s) -> p t s", t=2)
        weighted = expert_area[:, 1280:1536].rearrange("p (t s) -> p t s", t=2)
        back = expert_area[:, 1536:1792]
        act_g = expert_area[:, 1792:1920]
        hidden = expert_area[:, 1920:2048]
        hidden_t = expert_area[:, 2048:2176]
        expert_out = expert_area[:, 2176:3200]
        top_diff = small[:, 172:174]
        g_exp = small[:, 200:216]
        ratio = small[:, 216:218]
        g_diff = tmp[:, 0, 48:64]
        routed = wide.rearrange("p t (c k) -> p t c k", c=KD)

        x_landed = sem("x_landed")
        ident_landed = sem("ident_landed")
        consts_landed = sem("consts_landed")
        gains_landed = sem("gains_landed")
        ln_landed = sem("ln_landed")
        row_landed = sem("row_landed")
        small_landed = sem("small_landed")
        up_zeroed = sem("up_zeroed")
        up_landed = sem("up_landed")
        block_landed = [sem(f"block_landed{i}") for i in range(RING)]
        proj_in_psum = sem("proj_in_psum")
        proj_in_sbuf = sem("proj_in_sbuf")
        tr_in_psum = sem("tr_in_psum")
        tr_in_sbuf = sem("tr_in_sbuf")
        masks_cast = sem("masks_cast")
        power_set = sem("power_set")
        rsqrt_asked = sem("rsqrt_asked")
        rsqrt_done = sem("rsqrt_done")
        sumsq_done = sem("sumsq_done")
        latents_normed = sem("latents_normed")
        heads_roped = sem("heads_roped")
        key_rope_placed = sem("key_rope_placed")
        scores_in_psum = sem("scores_in_psum")
        max_done = sem("max_done")
        probs_done = sem("probs_done")
        out_in_psum = sem("out_in_psum")
        out_drained = sem("out_drained")
        mixed_ready = sem("mixed_ready")
        gla_squared = sem("gla_squared")
        att_squared = sem("att_squared")
        gla_normed = sem("gla_normed")
        gla_gated = sem("gla_gated")
        hi_ready = sem("hi_ready")
        split_ready = sem("split_ready")
        hi_used = sem("hi_used")
        res_ready = sem("res_ready")
        ln_used = sem("ln_used")
        normed_ready = sem("normed_ready")
        gqa_ready = sem("gqa_ready")
        decay_in_psum = sem("decay_in_psum")
        decay_log = sem("decay_log")
        decay_ready = sem("decay_ready")
        cum_in_psum = sem("cum_in_psum")
        cum_exp = sem("cum_exp")
        gla_operands = sem("gla_operands")
        kv_in_psum = sem("kv_in_psum")
        state_ready = sem("state_ready")
        gla_scores = sem("gla_scores")
        gla_masked = sem("gla_masked")
        gla_intra = sem("gla_intra")
        gla_inter = sem("gla_inter")
        gla_copied = sem("gla_copied")
        gla_summed = sem("gla_summed")
        routed_ready = sem("routed_ready")
        logits_in_psum = sem("logits_in_psum")
        mask_ready = sem("mask_ready")
        gates_exp = sem("gates_exp")
        rank_moved = sem("rank_moved")
        ranks_in_psum = sem("ranks_in_psum")
        routing_ready = sem("routing_ready")
        gate_up_landed = [sem(f"gate_up_landed{i}") for i in range(2)]
        down_landed = [sem(f"down_landed{i}") for i in range(2)]
        onehot_ready = sem("onehot_ready")
        picked_in_psum = sem("picked_in_psum")
        picked_ready = sem("picked_ready")
        back_in_psum = sem("back_in_psum")
        back_ready = sem("back_ready")
        hidden_in_psum = sem("hidden_in_psum")
        silu_done = sem("silu_done")
        hidden_ready = sem("hidden_ready")
        hidden_t_in_psum = sem("hidden_t_in_psum")
        hidden_t_ready = sem("hidden_t_ready")
        down_in_psum = sem("down_in_psum")
        down_drained_act = sem("down_drained_act")
        down_drained_dve = sem("down_drained_dve")
        sum_in_psum = sem("sum_in_psum")
        sum_added = sem("sum_added")
        act_chain = sem("act_chain")
        dve_chain = sem("dve_chain")
        out_ready = sem("out_ready")
        out_stored = sem("out_stored")

        block = ctx.enter_context(nc.Block())

        TR = {}
        count = 0
        for name, n in (("x", 4), ("gains", 1), ("latents", 4), ("q_a", 8), ("k_a", 8), ("att_a", 32), ("o_a", 4),
                        ("x1", 4), ("k_b", 4), ("q_b", 4), ("att_b", 32), ("o_b", 4), ("u", 4),
                        ("z", 2), ("gla", 2), ("gqa_q", 2), ("gqa_k", 2), ("att_g", 16), ("mixed", 4), ("routed", 4)):
            TR[name] = count
            count += n

        UNITS_A = UNITS_B = H * TILES
        UNITS_G = QH * TILES
        UNIT0 = {"a": 0, "b": UNITS_A, "g": UNITS_A + UNITS_B}
        OUT0 = {"a": 0, "b": 4, "g": 8}

        def state_of(way, step):
            n = 3 * way + step
            return state[:, n] if n < 4 else state_b[:, n - 4]

        def unit_of(u):
            group, tile, h = u // (8 * TILES), u // 8 % TILES, u % 8
            return 8 * group + h, tile

        def piece_of(b, piece):
            k, width = 2 * SPLIT.index(b) + piece, BLOCKS[b][3]
            at = slice(4 * width * piece, 4 * width * (piece + 1))
            return k, ring[:, b % RING, at], ring_lo[:, b % RING, at], pieces[PAIR[b]][piece][:, 0:4 * width]

        def after_block(b):
            n = SPLIT.index(b) + 1
            return SPLIT[n] if n < len(SPLIT) and SPLIT[n] == b + 1 else None

        def keys_of(kind, tile):
            return SEQ if kind == "g" else P * (tile + 1)

        @block.sync
        def _(sp):
            sp.dma_start(consts[:, 0:P], t["consts"][:, 0:P]).then_inc(ident_landed, 16)
            sp.dma_start(res[:], t["x"].rearrange("b (t p) d -> p (b t) d", p=P)).then_inc(x_landed, 16)
            for b, (name, kc, first, n) in enumerate(BLOCKS):
                slot = b % RING
                if b >= RING:
                    sp.wait_ge(proj_in_psum, LAST_JOB[b - RING] + 1)
                w = t[name]
                src = (w if name == "moba_w_kv" else w[0])[:, first:first + n].rearrange("(c p) n -> p c n", p=P)
                dst = ring[:, slot, 0:kc * n].rearrange("p (c n) -> p c n", c=kc)
                sp.dma_start(dst, src).then_inc(block_landed[slot], 16)
                if b == 1:
                    sp.dma_start(consts[:, P:], t["consts"][:, P:]).then_inc(consts_landed, 16)

            def load_expert(e, parity, gate_up_free, down_free, dst=None, down_dst=None):
                dst = ring[:, 3 - 3 * parity:5 - 3 * parity, :] if dst is None else dst
                gate_up_free()
                for k, name in enumerate(("w_gate_2", "w_up_2")):
                    src = t[name][0, bass.ds(e, 1)].rearrange("e (p c) f -> p (e c f)", c=KD)
                    sp.dma_start(dst[:, k, :], src).then_inc(gate_up_landed[parity], 16)
                down_free()
                src = t["w_down_2"][0, bass.ds(e, 1)].rearrange("e (j p) n -> p (e j) n", p=P)
                down_dst = ring[:, 2 + 3 * parity, :] if down_dst is None else down_dst
                sp.dma_start(down_dst.rearrange("p (j n) -> p j n", j=4), src).then_inc(down_landed[parity], 16)

            def front_done(*slots):
                last = max(b for b in range(len(BLOCKS)) if b % RING in slots)
                return lambda: sp.wait_ge(proj_in_psum, LAST_JOB[last] + 1)

            def hidden_taken(count):
                return lambda: sp.wait_ge(hidden_in_psum, count)

            def down_taken(count):
                return lambda: sp.wait_ge(down_in_psum, count)

            def heads_used():
                sp.wait_ge(scores_in_psum, UNIT0["g"] + UNITS_G)

            def front_used_and_landed():
                front_done(3, 4)()
                sp.wait_ge(gate_up_landed[0], 32)

            def load_further_experts(before):
                with sp.Fori(0, ROUNDS - 1) as r:
                    for i in range(GROUP):
                        taken = before + GROUP * r + (GROUP - 1 + i)
                        load_expert(GROUP * r + (GROUP + i), i % 2, hidden_taken(taken), down_taken(taken))

            load_expert(0, 0, front_done(0, 1), front_done(2), ring[:, 0:2, :])
            load_expert(1, 1, heads_used, front_done(5), extra)
            load_expert(2, 0, front_used_and_landed, lambda: sp.wait_ge(down_landed[0], 16), None, early_down[:])
            sp.wait_ge(gate_up_landed[1], 32)
            load_expert(3, 1, hidden_taken(1), down_taken(2))
            load_further_experts(0)

            sp.wait_ge(routing_ready, 1)
            most = sp.value_load(largest[0:1, 0:1], min_val=0, max_val=SEQ)
            with sp.If(most > SLOTS):
                with sp.Fori(1, PASSES) as p:
                    for e in range(GROUP):
                        load_expert(e, e % 2, hidden_taken(NE * p + (e - 1)), down_taken(NE * p + (e - 1)))
                    load_further_experts(NE * p)

            for tile in range(TILES):
                sp.wait_ge(out_ready, tile + 1)
                sp.dma_start(t["out"][0, tile * P:(tile + 1) * P, :], wide[:, tile, :]).then_inc(out_stored, 16)
            sp.wait_ge(out_stored, 16 * TILES)

        @block.gpsimd
        def _(pool):
            def scale_gla_heads(r, n):
                pool.wait_ge(rsqrt_done, n + 1)
                for tile in range(TILES):
                    o = wide[:, tile, 0:512]
                    o3 = o.rearrange("p (h d) -> p h d", h=4)
                    nc.gpsimd.tensor_tensor(o3, o3, r[:, 4 * tile:4 * tile + 4].rearrange(
                        "p (h a) -> p h a", a=1).to_broadcast([P, 4, GDV]), ALU.mult).then_inc(gla_normed, 1)
                    pool.wait_ge(gla_normed, tile + 1)
                    nc.gpsimd.tensor_tensor(o, o, gate[:, tile, 0:512], ALU.mult).then_inc(gla_gated, 1)

            def gate_outputs(kind):
                for n in range(4):
                    group, tile = n // TILES, n % TILES
                    half = slice(512 * group, 512 * group + 512)
                    pool.wait_ge(out_drained, OUT0[kind] + n + 1)
                    nc.gpsimd.tensor_tensor(wide[:, tile, half], wide[:, tile, half], gate[:, tile, half],
                                            ALU.mult).then_inc(mixed_ready, 1)

            nc.gpsimd.memset(power[:], -0.5).then_inc(power_set, 1)
            pool.wait_ge(power_set, 1)
            for name, (n, a, w) in RSQRT.items():
                if name in ("ln0t0", "ln1t0"):
                    gate_outputs("a" if name == "ln0t0" else "b")
                pool.wait_ge(rsqrt_asked, n + 1)
                nc.gpsimd.tensor_tensor(rstd[:, a:a + w], var[:, a:a + w], power[:, 0:w], ALU.pow).then_inc(
                    rsqrt_done, 1)
                if name == "gla":
                    scale_gla_heads(rstd[:, a:a + w], n)

        @block.scalar
        def _(act):
            rows = ((GAIN_Q, t["mla_q_norm"], 6), (6, t["mla_kv_norm"], 2), (GAIN_N1, t["norm1_gain_2"], 8),
                    (GAIN_MIX, t["gla_out_gain_2"], 1), (GAIN_MIX + 1, t["gla_out_gain_2"], 1),
                    (GAIN_MIX + 2, t["gla_out_gain_2"], 1), (GAIN_MIX + 3, t["gla_out_gain_2"], 1),
                    (GAIN_MIX + 4, t["att_out_gain_2"], 4))
            for a, src, n in rows:
                act.dma_start(gain_rows[a:a + n, :], src[0].rearrange("(r p) -> r p", p=P)).then_inc(gains_landed, 16)

            def load_row(dst, src, signal):
                act.dma_start(dst, src.rearrange("(a n) -> a n", a=1).to_broadcast([P, src.shape[0]])).then_inc(
                    signal, 16)

            def load_ln(layer):
                load_row(ln_row[:, 0, :], t["ln_g"][layer], ln_landed)
                load_row(ln_row[:, 1, :], t["ln_b"][layer], ln_landed)

            load_row(router_b[:, 0:NG], t["b_group_2"][0], small_landed)
            load_row(router_b[:, NG:], t["b_expert_2"][0], small_landed)
            load_row(head_gain[:, 0:HD], t["q_norm_gain_2"][0], small_landed)
            load_row(head_gain[:, HD:], t["k_norm_gain_2"][0], small_landed)

            def start_job(job):
                act.wait_ge(proj_in_psum, JOB[job] + 1)
                return proj_bank[JOB[job] % 2]

            def squares(src, column, spare=tmp[:, 0, :]):
                return nc.scalar.activation(spare[:, 0:src.shape[-1]], src, ACT.Square,
                                            accum_out=small[:, column:column + 1])

            chain = [0]

            def link(ins):
                chain[0] += 1
                ins.then_inc(act_chain, 1)
                act.wait_ge(act_chain, chain[0])

            def split_hi(b, piece):
                k, w, _, hi = piece_of(b, piece)
                if piece == 0:
                    act.wait_ge(block_landed[b % RING], 16 * (b // RING + 1))
                before = [x for x in SPLIT if x < b and PAIR[x] == PAIR[b]]
                if before and piece == 0:
                    act.wait_ge(hi_used, SPLIT.index(before[-1]) + 1)
                elif before:
                    act.wait_ge(proj_in_psum, LAST_JOB[before[-1]] + 1)
                nc.scalar.copy(hi, w).then_inc(hi_ready, 1)

            def drained(jobs):
                for job in jobs:
                    following = after_block(block_of(job))
                    if following is not None and (following != OUT_B or job[2] == 0):
                        split_hi(following, job[2])
                    yield job, start_job(job)

            for piece in range(2):
                split_hi(0, piece)
            for (_, _, tile), src in drained([("mla_w_in", 0, tile) for tile in range(TILES)]):
                link(squares(src[:, 0:512], 3 * tile))
                nc.scalar.copy(wide[:, tile, 0:512], src[:]).then_inc(proj_in_sbuf, 1)
            for (_, _, tile), src in drained([("mla_w_in", 1, tile) for tile in range(TILES)]):
                link(squares(src[:, 0:256], 3 * tile + 1))
                squares(src[:, 256:512], 3 * tile + 2).then_inc(sumsq_done, 1)
                act.wait_ge(sumsq_done, tile + 1)
                nc.scalar.copy(wide[:, tile, 512:1024], src[:]).then_inc(proj_in_sbuf, 1)
            for (_, _, tile), src in drained([("mla_w_in", 2, tile) for tile in range(TILES)]):
                nc.scalar.copy(z_in[:, tile, :], src[:, 0:ROPE])
                nc.scalar.activation(gate[:, tile, 0:384], src[:, 32:416], ACT.Silu).then_inc(proj_in_sbuf, 1)
            for (_, b, tile), src in drained([("mla_w_in", b, tile) for b in (3, 4) for tile in range(TILES)]):
                a = 384 + 320 * (b - 3)
                nc.scalar.activation(gate[:, tile, a:a + 320], src[:, 0:320], ACT.Silu).then_inc(proj_in_sbuf, 1)
            for n, job in enumerate([("mla_w_uq", b, tile) for b in range(4) for tile in range(TILES)]):
                if n >= 4:
                    act.wait_ge(tr_in_psum, TR["q_a"] + n - 3)
                src = start_job(job)
                nc.scalar.mul(stage[:, n % 4, 0:384], src[:, 0:384], SCALE_A).then_inc(proj_in_sbuf, 1)
            for n, job in enumerate([("mla_w_ukv", b, tile) for b in range(4) for tile in range(TILES)]):
                if n == 0:
                    act.wait_ge(key_rope_placed, 1)
                if n >= 4:
                    act.wait_ge(tr_in_psum, TR["k_a"] + n - 3)
                src = start_job(job)[:].rearrange("p (h d) -> p h d", h=4)
                b, tile = job[1], job[2]
                nc.scalar.copy(stage[:, n % 4, 0:4 * QKD].rearrange("p (h d) -> p h d", h=4)[:, :, 0:NOPE],
                               src[:, :, 0:NOPE])
                nc.scalar.copy(val[:, tile, 256 * b:256 * b + 256].rearrange("p (h d) -> p h d", h=4),
                               src[:, :, NOPE:]).then_inc(proj_in_sbuf, 1)

            row_sum = small[:, 256:256 + 80]
            neg_max = small[:, 336:336 + 80]

            def head_squares(u):
                v = var[:, RSQRT["gla"][1]:RSQRT["gla"][1] + 4 * TILES]
                if u == 4:
                    act.wait_ge(gla_summed, 2)
                for n in (2 * u - 8, 2 * u - 7) if 4 <= u < 8 else ():
                    nc.scalar.activation(tmp[:, 1, P * n:P * n + P], wide[:, n // 4, P * (n % 4):P * (n % 4) + P],
                                         ACT.Square, accum_out=v[:, n:n + 1]).then_inc(gla_squared, 1)
                tile = {14: 0, UNITS_G: 1}.get(u)
                if tile is not None:
                    column = RSQRT[f"att{tile}"][1]
                    act.wait_ge(out_drained, OUT0["g"] + tile + 1)
                    nc.scalar.activation(tmp[:, 0, 512 * tile:512 * tile + 512], wide[:, tile, 512:1024],
                                         ACT.Square, accum_out=var[:, column:column + 1]).then_inc(att_squared, 1)

            def softmax_units(kind, units):
                for u in range(units):
                    if kind == "g":
                        head_squares(u)
                    n = UNIT0[kind] + u
                    keys = keys_of(kind, unit_of(u)[1])
                    act.wait_ge(max_done, n + 1)
                    if u >= 4:
                        act.wait_ge(tr_in_psum, TR["att_" + kind] + u - 3)
                    nc.scalar.activation(probs[:, u % 4, 0:keys], score_bank[u % 4][:, 0:keys], ACT.Exp,
                                         bias=neg_max[:, n:n + 1], accum_out=row_sum[:, n:n + 1]).then_inc(
                        probs_done, 1)

            softmax_units("a", UNITS_A)
            load_ln(0)

            def drain_output(name, after=lambda tile: None):
                for tile in range(TILES):
                    for b in range(2):
                        src = start_job((name, b, tile))
                        nc.scalar.copy(wide[:, tile, 512 * b:512 * b + 512], src[:]).then_inc(proj_in_sbuf, 1)
                    after(tile)

            def stream_squares(n, tile, spare=tmp[:, 0, :]):
                act.wait_ge(res_ready, n + tile + 1)
                squares(res[:, tile, :], 16 + n + tile, spare).then_inc(sumsq_done, 1)
                act.wait_ge(sumsq_done, n + tile + 1)

            for piece in range(2):
                split_hi(block_of(("moba_w_kv", 0, 0)), piece)
            drain_output("mla_w_o")

            def drain_heads(name, scale, transposed):
                act.wait_ge(tr_in_psum, transposed)
                for n, (job, src) in enumerate(drained([(name, b, tile) for b in range(2) for tile in range(TILES)])):
                    nc.scalar.mul(stage[:, n, :], src[:], scale).then_inc(proj_in_sbuf, 1)

            drain_heads("moba_w_kv", 1.0, TR["k_a"] + 8)
            for (_, b, tile), src in drained([("moba_w_kv", b, tile) for b in (2, 3) for tile in range(TILES)]):
                nc.scalar.copy(val[:, tile, 512 * (b - 2):512 * (b - 1)], src[:]).then_inc(proj_in_sbuf, 1)
            drain_heads("moba_w_in", SCALE_B, TR["k_b"] + 4)
            for (_, b, tile), src in drained([("moba_w_in", b, tile) for b in (2, 3) for tile in range(TILES)]):
                nc.scalar.activation(gate[:, tile, 512 * (b - 2):512 * (b - 1)], src[:], ACT.Silu).then_inc(
                    proj_in_sbuf, 1)
            softmax_units("b", UNITS_B)
            split_hi(OUT_B, 1)
            for piece in range(2):
                split_hi(OUT_B + 1, piece)
            load_ln(1)
            act.wait_ge(up_zeroed, 1)
            for k, (w, b) in enumerate((("gla_up_fwd_2", "gla_up_fwd_bias_2"), ("gla_up_bwd_2", "gla_up_bwd_bias_2"))):
                act.dma_start(up_w[16 * k:16 * k + 16, GW * k:GW * k + GW], t[w][0]).then_inc(up_landed, 16)
                act.dma_start(up_w[32:33, GW * k:GW * k + GW], t[b]).then_inc(up_landed, 16)
            drain_output("moba_w_o", lambda tile: stream_squares(2, tile, gate[:, tile, :]))

            for tile in range(TILES):
                src = start_job(("w_in_2", 0, tile))
                nc.scalar.copy(z_in[:, tile, :], src[:, 0:32])
                nc.scalar.copy(att_q[:, tile, 0:384], src[:, 32:416]).then_inc(proj_in_sbuf, 1)
                src = start_job(("w_in_2", 1, tile))
                nc.scalar.copy(att_q[:, tile, 384:512], src[:, 0:128])
                nc.scalar.copy(att_kv[:, tile, :], src[:, 128:384]).then_inc(proj_in_sbuf, 1)
            for tile in range(TILES):
                act.wait_ge(decay_in_psum, 2)
                log = probs[:, 2 * tile:2 * tile + 2, :].rearrange("p a b -> p (a b)")
                link(nc.scalar.activation(log, out_bank[tile][:], ACT.Abs))
                link(nc.scalar.activation(log, log, ACT.Exp, scale=-1.0))
                nc.scalar.activation(log, log, ACT.Ln, bias=const("ones")[:, 0:1]).then_inc(decay_log, 1)
            for tile in range(TILES):
                src = start_job(("w_in_2", 2, tile))
                nc.scalar.mul(gla_qk[:, tile, 0:GW], src[:, 0:GW], GDK ** -0.5)
                nc.scalar.copy(gla_qk[:, tile, GW:512], src[:, GW:512]).then_inc(proj_in_sbuf, 1)
            for tile in range(TILES):
                at = slice(tile * P, tile * P + P)
                for way in range(2):
                    n = 2 * tile + way
                    act.wait_ge(cum_in_psum, n + 1)
                    cum = score_bank[n % 2][:].rearrange("p (a m s) -> p a m s", a=2, m=2)
                    nc.scalar.activation(exp_q[:, way, :, at], cum[:, :, 0, :], ACT.Exp, scale=1 / 16)
                    nc.scalar.activation(exp_k[:, way, :, at], cum[:, :, 0, :], ACT.Exp, scale=-1 / 16)
                    nc.scalar.activation(exp_b[:, way, :, at], cum[:, :, 1, :], ACT.Exp, scale=1 / 16)
                    nc.scalar.activation(k_out[:, tile, way, :], out_bank[n % 2][:, 0:GW], ACT.Exp,
                                         scale=1 / 16).then_inc(cum_exp, 1)
                src = start_job(("w_in_2", 3, tile))
                nc.scalar.copy(val[:, tile, 0:512], src[:]).then_inc(proj_in_sbuf, 1)
            for tile in range(TILES):
                src = start_job(("w_in_2", 4, tile))
                nc.scalar.activation(gate[:, tile, 0:512], src[:], ACT.Silu).then_inc(proj_in_sbuf, 1)
            for tile in range(TILES):
                act.wait_ge(gla_intra, tile + 1)
                nc.scalar.copy(wide[:, tile, 0:512], proj_bank[tile][:]).then_inc(gla_copied, 1)

            softmax_units("g", UNITS_G)
            head_squares(UNITS_G)
            act.wait_ge(gla_gated, 2)
            load_row(norm2_row, t["norm2_gain_2"][0], row_landed)
            load_row(final_row, t["final_gain_2"], row_landed)
            for src, a, n in ((t["w_group_2"], 0, NG), (t["w_expert_2"], NG, NE)):
                act.dma_start(router_w[:, :, a:a + n], src[0].rearrange("(p c) n -> p c n", c=KD)).then_inc(
                    row_landed, 16)
            drain_output("w_out_2", lambda tile: stream_squares(4, tile))

            act.wait_ge(logits_in_psum, 1)
            nc.scalar.copy(small[:, 0:144], proj_bank[0][:, 0:144]).then_inc(proj_in_sbuf, 1)
            act.wait_ge(mask_ready, 1)
            nc.scalar.activation(g_exp, g_diff, ACT.Exp).then_inc(gates_exp, 1)
            act.wait_ge(mask_ready, 2)
            nc.scalar.activation(ratio, top_diff, ACT.Exp).then_inc(gates_exp, 1)

            def expert_rounds(rounds, base):
                with act.Fori(0, rounds) as r:
                    for half in range(2):
                        act.wait_ge(picked_in_psum, 2 * (base + r) + (half + 1))
                        nc.scalar.copy(picked[:, 4 * half:4 * half + 4, :],
                                       bank[half][:].rearrange("p (c s) -> p c s", c=4)).then_inc(picked_ready, 1)
                    for i in range(GROUP):
                        act.wait_ge(hidden_in_psum, GROUP * (base + r) + (i + 1))
                        nc.scalar.activation(act_g, bank[2][:, 0:P], ACT.Silu).then_inc(silu_done, 1)
                        act.wait_ge(down_in_psum, GROUP * (base + r) + (i + 1))
                        nc.scalar.copy(expert_out[SLOTS * i:SLOTS * i + SLOTS, 0:256], bank[4][0:32, 0:256])
                        nc.scalar.copy(expert_out[SLOTS * i:SLOTS * i + SLOTS, 256:512],
                                       bank[4][32:64, 0:256]).then_inc(down_drained_act, 1)

            expert_rounds(ROUNDS, 0)
            act.wait_ge(routing_ready, 1)
            most = act.value_load(largest[0:1, 0:1], min_val=0, max_val=SEQ)
            with act.If(most > SLOTS):
                with act.Fori(1, PASSES) as p:
                    expert_rounds(ROUNDS, ROUNDS * p)

            for tile in range(TILES):
                stream_squares(6, tile)

        @block.vector
        def _(dve):
            chain = [0]

            def link(ins):
                chain[0] += 1
                ins.then_inc(dve_chain, 1)
                dve.wait_ge(dve_chain, chain[0])

            def rsqrt(name):
                n, a, w = RSQRT[name]
                dve.wait_ge(rsqrt_done, n + 1)
                return rstd[:, a:a + w]

            def ask(name, ins):
                ins.then_inc(rsqrt_asked, 1)

            def variances(name):
                n, a, w = RSQRT[name]
                return var[:, a:a + w]

            tr = [0]

            def drain(dst, gain=None, rows=P, width=512):
                n = tr[0]
                dve.wait_ge(tr_in_psum, n + 1)
                src = tr_bank[n % 2][0:rows, 0:width]
                src = src.rearrange("p (c s) -> p c s", s=P)
                if gain is None:
                    ins = nc.vector.tensor_copy(dst, src)
                else:
                    blocks = width // P
                    ins = nc.vector.tensor_tensor(dst, src, gain.rearrange("p (c a) -> p c a", a=1).to_broadcast(
                        [P, blocks, P]), ALU.mult)
                ins.then_inc(tr_in_sbuf, 1)
                tr[0] += 1

            def drain_split(tile):
                for half in range(2):
                    n = tr[0]
                    dve.wait_ge(tr_in_psum, n + 1)
                    src = tr_bank[n % 2][:].rearrange("p (c s) -> p c s", s=P)
                    at = (slice(None), slice(4 * half, 4 * half + 4), slice(tile * P, tile * P + P))
                    link(nc.vector.tensor_copy(xt_hi[at], src))
                    nc.vector.tensor_tensor(xt_lo[at], src, xt_hi[at].bitcast(F32), ALU.subtract).then_inc(
                        tr_in_sbuf, 1)
                    tr[0] += 1

            def split_lo(b, pieces=(0, 1)):
                for piece in pieces:
                    k, w, lo, hi = piece_of(b, piece)
                    dve.wait_ge(hi_ready, k + 1)
                    nc.vector.tensor_tensor(lo, w, hi.bitcast(F32), ALU.subtract).then_inc(split_ready, 1)

            def drain_xt(gains=None, tiles=range(TILES)):
                for tile in tiles:
                    for half in range(2):
                        g = None if gains is None else gain_cols[:, gains + 4 * half:gains + 4 * half + 4]
                        drain(xt[:, 4 * half:4 * half + 4, tile * P:tile * P + P], g)

            for tile in range(TILES):
                drain_split(tile)
            split_lo(0)
            split_lo(1)
            dve.wait_ge(tr_in_psum, TR["gains"] + 1)
            nc.vector.tensor_copy(gain_cols[:], tr_bank[0][:, 0:GAIN_ROWS]).then_inc(tr_in_sbuf, 1)
            tr[0] += 1
            dve.wait_ge(consts_landed, 16)
            nc.vector.tensor_copy(ident_b[:], ident)
            nc.vector.tensor_copy(causal_b[:], const("causal")).then_inc(masks_cast, 1)
            dve.wait_ge(small_landed, 64)
            for k in range(2):
                g = head_gain[:, HD * k:HD * k + HD]
                pairs = g.rearrange("p (d two) -> p d two", two=2)
                scale = HD ** -0.5 if k == 0 else 1.0
                for tile in range(TILES):
                    at = slice(HD * tile, HD * tile + HD)
                    cos, sin = const("cos_g")[:, at], const("sin_g")[:, at].rearrange("p (d two) -> p d two", two=2)
                    nc.vector.scalar_tensor_tensor(rope_g[:, 2 * k, at], cos, scale, g, ALU.mult, ALU.mult)
                    for x in range(2):
                        dst = rope_g[:, 2 * k + 1, at].rearrange("p (d two) -> p d two", two=2)[:, :, x]
                        last = nc.vector.scalar_tensor_tensor(dst, sin[:, :, x], scale, pairs[:, :, 1 - x],
                                                              ALU.mult, ALU.mult)
            link(last)

            split_lo(2)
            dve.wait_ge(sumsq_done, 2)
            dve.wait_ge(proj_in_sbuf, JOB["mla_w_in", 1, 1] + 1)
            v = variances("mla").rearrange("p (t n) -> p t n", n=2)
            ss = small[:, 0:6].rearrange("p (t n) -> p t n", n=3)
            link(nc.vector.tensor_tensor(small[:, 6:8], ss[:, :, 0], ss[:, :, 1], ALU.add))
            link(nc.vector.tensor_scalar(v[:, :, 0], small[:, 6:8], 1 / Q_LORA, RMS_EPS, ALU.mult, ALU.add))
            ask("mla", nc.vector.tensor_scalar(v[:, :, 1], ss[:, :, 2], 1 / KV_LORA, RMS_EPS, ALU.mult, ALU.add))
            r = rsqrt("mla")
            for tile in range(TILES):
                nc.vector.tensor_scalar(wide[:, tile, 0:Q_LORA], wide[:, tile, 0:Q_LORA],
                                        r[:, 2 * tile:2 * tile + 1], None, ALU.mult)
                nc.vector.tensor_scalar(wide[:, tile, Q_LORA:D], wide[:, tile, Q_LORA:D],
                                        r[:, 2 * tile + 1:2 * tile + 2], None, ALU.mult).then_inc(latents_normed, 1)
            split_lo(3)
            split_lo(4)
            dve.wait_ge(proj_in_sbuf, JOB["mla_w_in", 2, 1] + 1)

            def rope_a(x, heads, tile, out):
                half = ROPE // 2
                cos = const("cos_a")[:, ROPE * tile:ROPE * tile + ROPE]
                sin = const("sin_a")[:, ROPE * tile:ROPE * tile + ROPE]

                def over_heads(a):
                    return a.rearrange("p (h d) -> p h d", h=1).to_broadcast([P, heads, a.shape[-1]])

                c = tmp[:, 0, 0:heads * ROPE].rearrange("p (h d) -> p h d", h=heads)
                s = tmp[:, 1, 0:heads * ROPE].rearrange("p (h d) -> p h d", h=heads)
                nc.vector.tensor_tensor(c, x, over_heads(cos), ALU.mult)
                nc.vector.tensor_tensor(s[:, :, 0:half], x[:, :, half:ROPE], over_heads(sin[:, 0:half]), ALU.mult)
                link(nc.vector.tensor_tensor(s[:, :, half:ROPE], x[:, :, 0:half], over_heads(sin[:, half:ROPE]),
                                             ALU.mult))
                return nc.vector.tensor_tensor(out, c, s, ALU.add)

            key_rope = small[:, 64:64 + TILES * ROPE].rearrange("p (t d) -> p t d", t=TILES)
            for tile in range(TILES):
                x = z_in[:, tile, :].rearrange("p (h d) -> p h d", h=1)
                link(rope_a(x, 1, tile, key_rope[:, tile:tile + 1, :]))
            dve.wait_ge(tr_in_sbuf, TR["gains"] + 1)
            drain_xt(GAIN_Q)

            def q_a_rope(n):
                b, tile = n // TILES, n % TILES
                dve.wait_ge(proj_in_sbuf, JOB["mla_w_uq", b, tile] + 1)
                x = stage[:, n % 4, 0:4 * QKD].rearrange("p (h d) -> p h d", h=4)[:, :, NOPE:QKD]
                rope_a(x, 4, tile, x).then_inc(heads_roped, 1)
                dve.wait_ge(heads_roped, n + 1)

            def heads_out(dst, n, per, rows):
                b, tile = n // TILES, n % TILES
                drain(dst[0:rows, per * b:per * b + per, tile * P:tile * P + P], rows=rows, width=per * P)

            for n in range(8 + LAG):
                if n < 8:
                    q_a_rope(n)
                if n >= LAG:
                    heads_out(q_a, n - LAG, 4, QKD)
            for i in range(4):
                last = nc.vector.tensor_copy(
                    stage[:, i, 0:4 * QKD].rearrange("p (h d) -> p h d", h=4)[:, :, NOPE:QKD],
                    key_rope[:, i % 2:i % 2 + 1, :].to_broadcast([P, 4, ROPE]))
            last.then_inc(key_rope_placed, 1)
            for n in range(8):
                heads_out(k_a, n, 4, QKD)

            row_sum = small[:, 256:256 + 80]
            neg_max = small[:, 336:336 + 80]
            inverse = small[:, 416:416 + 80]

            def attention(kind, units, depth, out_of, tail, beside=()):
                for u in range(units + depth + 1):
                    if u < units:
                        n = UNIT0[kind] + u
                        dve.wait_ge(scores_in_psum, n + 1)
                        keys = keys_of(kind, unit_of(u)[1])
                        nc.vector.tensor_reduce(neg_max[:, n:n + 1], score_bank[u % 4][:, 0:keys],
                                                AX.X, ALU.max, negate=True).then_inc(max_done, 1)
                    if u in beside:
                        beside[u]()
                    m = u - depth
                    if 0 <= m < units:
                        keys = keys_of(kind, unit_of(m)[1])
                        drain(probs_t[:, m % 2, 0:keys].rearrange("p (c s) -> p c s", s=P), width=keys)
                    if m == units - 1:
                        tail()
                    m = u - depth - 1
                    if m >= 0 and m % 8 == 7:
                        group, tile = m // (8 * TILES), unit_of(m)[1]
                        sums = row_sum[:, UNIT0[kind] + m - 7:UNIT0[kind] + m + 1]
                        inv = inverse[:, 8 * tile:8 * tile + 8]
                        dve.wait_ge(probs_done, UNIT0[kind] + m + 1)
                        link(nc.vector.reciprocal(inv, sums))
                        dve.wait_ge(out_in_psum, OUT0[kind] + group * TILES + tile + 1)
                        dst = out_of(tile, group)
                        link_out = nc.vector.tensor_tensor(
                            dst.rearrange("p (h d) -> p h d", h=8),
                            out_bank[tile][:].rearrange("p (h d) -> p h d", h=8),
                            inv.rearrange("p (h a) -> p h a", a=1).to_broadcast([P, 8, HD]), ALU.mult)
                        link_out.then_inc(out_drained, 1)

            def half_of(tile, group):
                return wide[:, tile, 512 * group:512 * group + 512]

            attention("a", UNITS_A, 3, half_of, lambda: drain_xt(tiles=[0]))
            drain_xt(tiles=[1])
            split_lo(block_of(("moba_w_kv", 0, 0)))

            def rms_of_stream(name, first_ready, tile):
                rs, column = f"{name}t{tile}", 16 + first_ready + tile
                dve.wait_ge(sumsq_done, first_ready + tile + 1)
                ask(rs, nc.vector.tensor_scalar(variances(rs), small[:, column:column + 1], 1 / D, RMS_EPS,
                                                ALU.mult, ALU.add))
                return rsqrt(rs)

            def post_norm(layer, name):
                stats = small[:, 128:140].rearrange("p (c s) -> p c s", c=2)
                for tile in range(TILES):
                    for b in range(2):
                        half = slice(512 * b, 512 * b + 512)
                        dve.wait_ge(proj_in_sbuf, JOB[name, b, tile] + 1)
                        link(nc.vector.scalar_tensor_tensor(res[:, tile, half], res[:, tile, half], ALPHA,
                                                            wide[:, tile, half], ALU.mult, ALU.add))
                        last = nc.vector.bn_stats(stats[:, b, :], res[:, tile, half])
                    link(last)
                    link(nc.vector.bn_aggr(small[:, 140:142], small[:, 128:140]))
                    rs = f"ln{layer}t{tile}"
                    ask(rs, nc.vector.tensor_scalar(variances(rs), small[:, 141:142], LN_EPS, None, ALU.add))
                    r = rsqrt(rs)
                    link(nc.vector.tensor_scalar(res[:, tile, :], res[:, tile, :], small[:, 140:141], r,
                                                 ALU.subtract, ALU.mult))
                    if tile == 0:
                        dve.wait_ge(ln_landed, 32 * (layer + 1))
                    link(nc.vector.tensor_tensor(res[:, tile, :], res[:, tile, :], ln_row[:, 0, :], ALU.mult))
                    nc.vector.tensor_tensor(res[:, tile, :], res[:, tile, :], ln_row[:, 1, :], ALU.add).then_inc(
                        res_ready, 1)
                    dve.wait_ge(res_ready, 2 * layer + tile + 1)
                    if tile == 1:
                        nc.vector.memset(small[:, 142:143], 0.0).then_inc(ln_used, 1)
                        dve.wait_ge(ln_used, layer + 1)
                    if layer == 0:
                        drain_split(tile)
                    else:
                        r = rms_of_stream("norm1", 2, tile)
                        nc.vector.tensor_scalar(wide[:, tile, :], res[:, tile, :], r, None, ALU.mult).then_inc(
                            normed_ready, 1)
                        drain_xt(GAIN_N1, [tile])

            post_norm(0, "mla_w_o")

            def rope_b(x, tile, heads, cos, sin, swap, n):
                def over_heads(a):
                    return a.rearrange("p (h d) -> p h d", h=1).to_broadcast([P, heads, HD])

                def split(a):
                    a = a.rearrange("p (h d) -> p h d", h=heads)
                    if swap == "halves":
                        return a[:, :, 0:HD // 2], a[:, :, HD // 2:HD]
                    a = a.rearrange("p h (d two) -> p h d two", two=2)
                    return a[:, :, :, 0], a[:, :, :, 1]

                width = heads * HD
                c, s = tmp[:, 0, 0:width], tmp[:, 1, 0:width]
                x0, x1 = split(x)
                s0, s1 = split(s)
                nc.vector.tensor_tensor(c.rearrange("p (h d) -> p h d", h=heads),
                                        x.rearrange("p (h d) -> p h d", h=heads), over_heads(cos), ALU.mult)
                sin3 = over_heads(sin)
                if swap == "halves":
                    w0, w1 = sin3[:, :, 0:HD // 2], sin3[:, :, HD // 2:HD]
                else:
                    w = sin.rearrange("p (h d two) -> p h d two", h=1, two=2)
                    w0 = w[:, :, :, 0].to_broadcast([P, heads, HD // 2])
                    w1 = w[:, :, :, 1].to_broadcast([P, heads, HD // 2])
                nc.vector.tensor_tensor(s0, x1, w0, ALU.mult)
                link(nc.vector.tensor_tensor(s1, x0, w1, ALU.mult))
                return nc.vector.tensor_tensor(x, c, s, ALU.add)

            def heads_b(name, base, dst):
                for b in range(4):
                    following = after_block(block_of((name, b, 0)))
                    split_lo(following, (0, 1) if following != OUT_B else (0,))
                    for n in (2 * b - 2, 2 * b - 1) if b in (1, 2) else ():
                        heads_out(dst, n, 4, P)
                    for n in (2 * b, 2 * b + 1) if b < 2 else ():
                        tile = n % TILES
                        dve.wait_ge(proj_in_sbuf, JOB[name, b, tile] + 1)
                        rope_b(stage[:, n, :], tile, 8, const("cos_b")[:, HD * tile:HD * tile + HD],
                               const("sin_b")[:, HD * tile:HD * tile + HD], "halves", n).then_inc(heads_roped, 1)
                        dve.wait_ge(heads_roped, base + n + 1)

            heads_b("moba_w_kv", 8, k_b)
            heads_b("moba_w_in", 12, q_b)
            attention("b", UNITS_B, 3, half_of, lambda: drain_split(0))
            split_lo(OUT_B, (1,))
            split_lo(OUT_B + 1)
            drain_split(1)
            nc.vector.memset(up_w, 0.0).then_inc(up_zeroed, 1)
            post_norm(1, "moba_w_o")

            nc.vector.memset(masked, 0.0)
            nc.vector.memset(z_t[32:33, :], 1.0)
            for tile in range(TILES):
                drain(z_t[0:32, tile * P:tile * P + P].rearrange("p (c s) -> p c s", s=P), rows=32, width=P)
            for tile in range(TILES):
                dve.wait_ge(decay_log, tile + 1)
                nc.vector.scalar_tensor_tensor(decay[:, tile, :], out_bank[tile][:], 0.0,
                                               probs[:, 2 * tile:2 * tile + 2, :].rearrange("p a b -> p (a b)"),
                                               ALU.min, ALU.subtract).then_inc(decay_ready, 1)
            dve.wait_ge(proj_in_sbuf, JOB["w_in_2", 1, 1] + 1)
            v = variances("qk")
            for tile in range(TILES):
                q, k = att_q[:, tile, :], att_kv[:, tile, 0:128]
                nc.vector.tensor_tensor(tmp[:, tile, 0:512], q, q, ALU.mult)
                link(nc.vector.tensor_tensor(tmp[:, tile, 512:640], k, k, ALU.mult))
                link(nc.vector.tensor_reduce(v[:, 10 * tile:10 * tile + 10],
                                             tmp[:, tile, 0:640].rearrange("p (h d) -> p h d", h=10), AX.X, ALU.add))
            ask("qk", nc.vector.tensor_scalar(v, v, 1 / HD, RMS_EPS, ALU.mult, ALU.add))
            r = rsqrt("qk")
            for tile in range(TILES):
                at = slice(HD * tile, HD * tile + HD)
                for x, heads, first, k in ((att_q[:, tile, :], QH, 0, 0), (att_kv[:, tile, 0:128], KVH, QH, 2)):
                    x3 = x.rearrange("p (h d) -> p h d", h=heads)
                    link(nc.vector.tensor_tensor(x3, x3, r[:, 10 * tile + first:10 * tile + first + heads].rearrange(
                        "p (h a) -> p h a", a=1).to_broadcast([P, heads, HD]), ALU.mult))
                    link(rope_b(x, tile, heads, rope_g[:, k, at], rope_g[:, k + 1, at], "pairs", 0))
                for kv in range(KVH):
                    last = nc.vector.tensor_copy(
                        key2[:, tile, 128 * kv:128 * kv + 128].rearrange("p (c d) -> p c d", c=2),
                        att_kv[:, tile, HD * kv:HD * kv + HD].rearrange("p (c d) -> p c d", c=1).to_broadcast(
                            [P, 2, HD]))
                last.then_inc(gqa_ready, 1)
            for tile in range(TILES):
                drain(gla_t[:, :, tile * P:tile * P + P])
            dve.wait_ge(tr_in_sbuf, TR["gla"] + 2)
            for n, (tile, way) in enumerate([(i, j) for i in range(TILES) for j in range(2)]):
                at = slice(tile * P, tile * P + P)
                dve.wait_ge(cum_exp, n + 1)
                nc.vector.tensor_tensor(q_in[:, way, :, at], exp_b[:, way, :, at], gla_t[:, 0:2, at], ALU.mult)
                nc.vector.tensor_tensor(exp_q[:, way, :, at], exp_q[:, way, :, at], gla_t[:, 0:2, at], ALU.mult)
                nc.vector.tensor_tensor(exp_k[:, way, :, at], exp_k[:, way, :, at], gla_t[:, 2:4, at], ALU.mult)
                nc.vector.tensor_tensor(k_out[:, tile, way, :], k_out[:, tile, way, :], gla_qk[:, tile, GW:512],
                                        ALU.mult).then_inc(gla_operands, 1)
            for tile in range(TILES):
                drain(q_g[:, :, tile * P:tile * P + P])
            for tile in range(TILES):
                drain(k_g[:, :, tile * P:tile * P + P], width=2 * P)
            dve.wait_ge(gla_operands, 4)
            for n, (way, step) in enumerate(KV_ORDER):
                chunk = step if way == 0 else NCHUNK - 1 - step
                src = score_bank[chunk % 2][:].rearrange("p (a e) -> p a e", a=2)
                dst = state_of(way, step)
                dve.wait_ge(kv_in_psum, n + 1)
                if step == 0:
                    nc.vector.tensor_copy(dst, src).then_inc(state_ready, 1)
                else:
                    last_token = CHUNK * chunk + (CHUNK - 1 if way == 0 else 0)
                    dve.wait_ge(state_ready, n - 1)
                    for pair in range(2):
                        last = nc.vector.scalar_tensor_tensor(
                            dst[:, pair, :], state_of(way, step - 1)[:, pair, :],
                            exp_b[:, way, pair, last_token:last_token + 1], src[:, pair, :], ALU.mult, ALU.add)
                    last.then_inc(state_ready, 1)
            for tile in range(TILES):
                for way in range(2):
                    mask = const("cum_fwd" if way == 0 else "cum_bwd")[:, P:2 * P].bitcast(I32)
                    for odd in range(2):
                        dve.wait_ge(gla_scores, 4 * tile + 2 * way + odd + 1)
                        if tile:
                            dve.wait_ge(gla_intra, tile)
                        dst = masked[:, way, :].rearrange("p (a o s) -> p a o s", a=2, o=2)[:, :, odd, :]
                        src = intra_bank[2 * way + odd][:, 0:2 * P].rearrange("p (a s) -> p a s", a=2)
                        for pair in range(2):
                            last = nc.vector.copy_predicated(dst[:, pair, :], mask, src[:, pair, :])
                        last.then_inc(gla_masked, 1)
                dve.wait_ge(gla_copied, tile + 1)
                dve.wait_ge(gla_inter, tile + 1)
                for odd in range(2):
                    o = wide[:, tile, 0:512].rearrange("p (a o e) -> p a o e", a=2, o=2)[:, :, odd, :]
                    last = nc.vector.tensor_tensor(o, o, out_bank[odd][:, 0:256].rearrange("p (a e) -> p a e", a=2),
                                                   ALU.add)
                last.then_inc(gla_summed, 1)
            dve.wait_ge(gla_summed, 2)

            def gla_variance():
                v = variances("gla")
                dve.wait_ge(gla_squared, 4 * TILES)
                ask("gla", nc.vector.tensor_scalar(v, v, 1 / GDV, RMS_EPS, ALU.mult, ALU.add))

            def att_variance(tile):
                v = variances(f"att{tile}")
                dve.wait_ge(att_squared, tile + 1)
                ask(f"att{tile}", nc.vector.tensor_scalar(v, v, 1 / 512, RMS_EPS, ALU.mult, ALU.add))

            def att_scaled(tile):
                nc.vector.tensor_scalar(wide[:, tile, 512:1024], wide[:, tile, 512:1024], rsqrt(f"att{tile}"), None,
                                        ALU.mult).then_inc(mixed_ready, 1)

            attention("g", UNITS_G, 3, lambda tile, group: wide[:, tile, 512:1024],
                      lambda: drain_xt(GAIN_MIX, [0]),
                      {9: gla_variance, 15: lambda: att_variance(0), 17: lambda: att_scaled(0)})
            att_variance(1)
            att_scaled(1)
            drain_xt(GAIN_MIX, [1])
            for tile in range(TILES):
                for b in range(2):
                    half = slice(512 * b, 512 * b + 512)
                    dve.wait_ge(proj_in_sbuf, JOB["w_out_2", b, tile] + 1)
                    last = nc.vector.tensor_tensor(res[:, tile, half], res[:, tile, half], wide[:, tile, half], ALU.add)
                last.then_inc(res_ready, 1)
                r = rms_of_stream("norm2", 4, tile)
                if tile == 0:
                    dve.wait_ge(row_landed, 64)
                dst = routed[:, tile].rearrange("p c k -> p k c")
                nc.vector.scalar_tensor_tensor(dst, res[:, tile, :].rearrange("p (k c) -> p k c", c=KD), r,
                                               norm2_row.rearrange("p (k c) -> p k c", c=KD),
                                               ALU.mult, ALU.mult).then_inc(routed_ready, 1)
            drain_xt()

            dve.wait_ge(proj_in_sbuf, len(JOBS) + 1)
            logits = small[:, 0:144].rearrange("p (t n) -> p t n", t=TILES)

            def over_tiles(a):
                return a.rearrange("p (t n) -> p t n", t=1).to_broadcast([P, TILES, a.shape[-1]])

            def over(a, n):
                return a.rearrange("p (t n) -> p t n", n=1).to_broadcast([P, TILES, n])

            def view(a, n):
                return tmp[:, 0, a:a + TILES * n].rearrange("p (t n) -> p t n", t=TILES)

            link(nc.vector.tensor_tensor(logits, logits, over_tiles(router_b[:]), ALU.add))
            scal = small[:, 160:180]
            g_log, e_log = logits[:, :, 0:NG], logits[:, :, NG:]

            def first_max(x, n, top, is_top, work, best, out):
                link(nc.vector.tensor_reduce(top, x, AX.X, ALU.max))
                link(nc.vector.tensor_tensor(is_top, x, over(top, n), ALU.is_equal))
                link(nc.vector.tensor_tensor(work, is_top, over_tiles(const("desc")[:, NE - n:NE]), ALU.mult))
                link(nc.vector.tensor_reduce(best, work, AX.X, ALU.max))
                link(nc.vector.tensor_tensor(out, work, over(best, n), ALU.is_equal))

            g_top, g_best = scal[:, 0:2], scal[:, 2:4]
            g_is, g_work, g_hot = view(0, NG), view(16, NG), view(32, NG)
            first_max(g_log, NG, g_top, g_is, g_work, g_best, g_hot)
            nc.vector.tensor_tensor(view(48, NG), g_log, over(g_top, NG), ALU.subtract).then_inc(mask_ready, 1)
            g_low = view(64, NG)
            link(nc.vector.tensor_scalar(g_low, g_hot, -1.0, BIG, ALU.add, ALU.mult))
            for tile in range(TILES):
                e3 = e_log[:, tile, :].rearrange("p (g e) -> p g e", g=NG)
                last = nc.vector.tensor_tensor(e3, e3, g_low[:, tile, :].rearrange("p (g a) -> p g a", a=1).to_broadcast(
                    [P, NG, EPG]), ALU.add)
            link(last)
            e_is, e_work = view(128, NE), view(256, NE)
            hot1, hot2 = view(384, NE), view(512, NE)
            top1, top2, best1, best2 = (scal[:, 4 + 2 * i:6 + 2 * i] for i in range(4))
            first_max(e_log, NE, top1, e_is, e_work, best1, hot1)
            e2 = view(640, NE)
            link(nc.vector.scalar_tensor_tensor(e2, hot1, -2 * BIG, e_log, ALU.mult, ALU.add))
            first_max(e2, NE, top2, e_is, e_work, best2, hot2)
            nc.vector.tensor_tensor(top_diff, top2, top1, ALU.subtract).then_inc(mask_ready, 1)
            mask = view(768, NE)
            nc.vector.tensor_tensor(mask, hot1, hot2, ALU.add).then_inc(mask_ready, 1)
            dve.wait_ge(gates_exp, 2)
            g_sum = small[:, 180:182]
            link(nc.vector.tensor_reduce(g_sum, g_exp.rearrange("p (t n) -> p t n", t=TILES), AX.X, ALU.add))
            link(nc.vector.tensor_scalar(scal[:, 14:16], ratio, 1.0, None, ALU.add))
            link(nc.vector.tensor_tensor(scal[:, 16:18], scal[:, 14:16], g_sum, ALU.mult))
            link(nc.vector.reciprocal(scal[:, 16:18], scal[:, 16:18]))
            link(nc.vector.tensor_tensor(scal[:, 18:20], scal[:, 16:18], ratio, ALU.mult))
            nc.vector.tensor_tensor(hot1, hot1, over(scal[:, 16:18], NE), ALU.mult)
            link(nc.vector.tensor_tensor(hot2, hot2, over(scal[:, 18:20], NE), ALU.mult))
            link(nc.vector.tensor_tensor(gates[:], hot1, hot2, ALU.add))
            dve.wait_ge(ranks_in_psum, 1)
            dve.wait_ge(mask_ready, 3)
            link(nc.vector.tensor_tensor(rank[:], proj_bank[1][:, 0:2 * NE].rearrange("p (t n) -> p t n", t=TILES),
                                         mask, ALU.mult))
            link(nc.vector.tensor_scalar(rank[:], rank[:], -1.0, None, ALU.add))
            link(nc.vector.tensor_reduce(small[:, 182:183], proj_bank[1][:, 2 * NE:3 * NE], AX.X, ALU.max))
            nc.vector.tensor_copy(largest[:], small[:, 182:183]).then_inc(routing_ready, 1)

            def expert_rounds(rounds, base):
                with dve.Fori(0, rounds) as r:
                    n = base + r
                    for tile in range(TILES):
                        nc.vector.tensor_tensor(
                            onehot[:, tile, :].rearrange("p (e s) -> p e s", e=GROUP),
                            const("iota").rearrange("p (e s) -> p e s", e=1).to_broadcast([P, GROUP, SLOTS]),
                            rank[:, tile, bass.ds(GROUP * r, GROUP)].rearrange("p (e s) -> p e s", s=1).to_broadcast(
                                [P, GROUP, SLOTS]), ALU.is_equal).then_inc(onehot_ready, 1)
                    dve.wait_ge(onehot_ready, 3 * n + 2)
                    for tile in range(TILES):
                        last = nc.vector.tensor_tensor(
                            weighted[:, tile, :].rearrange("p (e s) -> p e s", e=GROUP),
                            onehot[:, tile, :].rearrange("p (e s) -> p e s", e=GROUP),
                            gates[:, tile, bass.ds(GROUP * r, GROUP)].rearrange("p (e s) -> p e s", s=1).to_broadcast(
                                [P, GROUP, SLOTS]), ALU.mult)
                    last.then_inc(onehot_ready, 1)
                    dve.wait_ge(back_in_psum, n + 1)
                    nc.vector.tensor_copy(back, bank[3][:, 0:256]).then_inc(back_ready, 1)
                    for i in range(GROUP):
                        x = GROUP * n + i
                        dve.wait_ge(silu_done, x + 1)
                        nc.vector.tensor_tensor(hidden, act_g, bank[2][:, P:2 * P], ALU.mult).then_inc(hidden_ready, 1)
                        dve.wait_ge(hidden_t_in_psum, x + 1)
                        nc.vector.tensor_copy(hidden_t, bank[3][:, 256:384]).then_inc(hidden_t_ready, 1)
                        dve.wait_ge(down_in_psum, x + 1)
                        nc.vector.tensor_copy(expert_out[SLOTS * i:SLOTS * i + SLOTS, 512:768], bank[4][64:96, 0:256])
                        nc.vector.tensor_copy(expert_out[SLOTS * i:SLOTS * i + SLOTS, 768:1024],
                                              bank[4][96:128, 0:256]).then_inc(down_drained_dve, 1)
                    for k in range(4):
                        tile, half = k // 2, k % 2
                        dve.wait_ge(sum_in_psum, 4 * n + (k + 1))
                        dst = res[:, tile, 512 * half:512 * half + 512]
                        nc.vector.tensor_tensor(dst, dst, bank[5 + k % 3][:], ALU.add).then_inc(sum_added, 1)

            expert_rounds(ROUNDS, 0)
            dve.wait_ge(sum_added, 4 * ROUNDS)
            most = dve.value_load(largest[0:1, 0:1], min_val=0, max_val=SEQ)
            with dve.If(most > SLOTS):
                with dve.Fori(1, PASSES) as p:
                    dve.wait_ge(onehot_ready, 3 * ROUNDS * p)
                    nc.vector.tensor_scalar(rank[:], rank[:], -float(SLOTS), None, ALU.add).then_inc(rank_moved, 1)
                    dve.wait_ge(rank_moved, p)
                    nc.vector.memset(small[:, 150:151], 0.0)
                    expert_rounds(ROUNDS, ROUNDS * p)
                dve.wait_ge(sum_added, 4 * ROUNDS * PASSES)

            for tile in range(TILES):
                nc.vector.memset(small[:, 150 + tile:151 + tile], 0.0).then_inc(res_ready, 1)
            for tile in range(TILES):
                r = rms_of_stream("final", 6, tile)
                nc.vector.scalar_tensor_tensor(wide[:, tile, :], res[:, tile, :], r, final_row, ALU.mult,
                                               ALU.mult).then_inc(out_ready, 1)

        @block.tensor
        def _(pe):
            tr = [0]

            def transposes(blocks):
                n = tr[0]
                if n >= 2:
                    pe.wait_ge(tr_in_sbuf, n - 1)
                for i, x in enumerate(blocks):
                    rows, cols = x.shape[0], x.shape[-1]
                    last = nc.tensor.transpose(tr_bank[n % 2][0:cols, P * i:P * i + rows], x, ident[0:rows, 0:rows])
                last.then_inc(tr_in_psum, 1)
                tr[0] += 1

            def transpose_rows(src, tile, half):
                transposes([src[:, tile, P * c:P * c + P] for c in range(4 * half, 4 * half + 4)])

            landed = set()

            def project(job, between=()):
                n = JOB[job]
                name, part, tile = job
                b = block_of(job)
                _, kc, _, width = BLOCKS[b]
                w = ring[:, b % RING, 0:kc * width].rearrange("p (c n) -> p c n", c=kc)
                if name == "mla_w_ukv":
                    w = w[:, :, 512 * part:512 * part + 512]
                    width = 512
                if b not in landed:
                    landed.add(b)
                    pe.wait_ge(block_landed[b % RING], 16 * (b // RING + 1))
                if n >= 2:
                    pe.wait_ge(proj_in_sbuf, n - 1)
                first = 6 if name == "mla_w_ukv" else 0
                for c in range(kc):
                    if c in between:
                        between[c]()
                    last = nc.tensor.matmul(proj_bank[n % 2][:, 0:width], xt[:, first + c, tile * P:tile * P + P],
                                            w[:, c, :], start=(c == 0), stop=(c == kc - 1))
                last.then_inc(proj_in_psum, 1)

            def project_piece(job, piece):
                n = JOB[job]
                tile, b = job[2], block_of(job)
                k, _, lo, hi = piece_of(b, piece)
                lo, hi = (a.rearrange("p (c n) -> p c n", c=4) for a in (lo, hi))
                dst = proj_bank[n % 2][:, 0:BLOCKS[b][3]]
                pe.wait_ge(split_ready, k + 1)
                if piece == 0 and n >= 2:
                    pe.wait_ge(proj_in_sbuf, n - 1)
                for c in range(4):
                    at = (slice(None), 4 * piece + c, slice(tile * P, tile * P + P))
                    for x, w in ((xt_hi, hi), (xt_hi, lo), (xt_lo, hi)):
                        last = nc.tensor.matmul(dst, x[at], w[:, c, :], start=(piece == 0 and c == 0 and w is hi and
                                                                               x is xt_hi),
                                                stop=(piece == 1 and c == 3 and x is xt_lo))
                if piece == 1:
                    last.then_inc(proj_in_psum, 1)
                elif tile == TILES - 1:
                    last.then_inc(hi_used, 1)

            def project_split(name, b):
                for piece in range(2):
                    for tile in range(TILES):
                        project_piece((name, b, tile), piece)

            def xt_ready():
                pe.wait_ge(tr_in_sbuf, tr[0])

            def attention(kind, units, depth, scores, values, tail):
                for u in range(units + depth + 1):
                    if u < units:
                        n = UNIT0[kind] + u
                        h, tile = unit_of(u)
                        keys = keys_of(kind, tile)
                        if u >= 4:
                            pe.wait_ge(probs_done, n - 3)
                        lhs, rhs = scores(h, tile, keys)
                        causal = kind != "g"
                        last = nc.tensor.matmul(score_bank[u % 4][:, 0:keys], lhs, rhs, start=True, stop=not causal)
                        if causal:
                            last = nc.tensor.matmul(score_bank[u % 4][:, keys - P:keys], ident_b[:], causal_b[:],
                                                    start=False, stop=True)
                        last.then_inc(scores_in_psum, 1)
                    m = u - depth
                    if 0 <= m < units:
                        pe.wait_ge(probs_done, UNIT0[kind] + m + 1)
                        transposes([probs[:, m % 4, P * k:P * k + P] for k in range(keys_of(kind, unit_of(m)[1]) // P)])
                    if m == units - 1:
                        tail()
                    m = u - depth - 1
                    if m >= 0:
                        h, tile = unit_of(m)
                        group = h // 8
                        pe.wait_ge(tr_in_sbuf, TR["att_" + kind] + m + 1)
                        if h % 8 == 0 and group:
                            pe.wait_ge(out_drained, OUT0[kind] + tile + 1)
                        blocks = keys_of(kind, tile) // P
                        for k in range(blocks):
                            last = nc.tensor.matmul(out_bank[tile][:, HD * (h % 8):HD * (h % 8) + HD],
                                                    probs_t[:, m % 2, P * k:P * k + P], values(h, k),
                                                    start=(k == 0), stop=(k == blocks - 1))
                        if h % 8 == 7:
                            last.then_inc(out_in_psum, 1)

            pe.wait_ge(ident_landed, 16)
            pe.wait_ge(x_landed, 16)
            for tile in range(TILES):
                for half in range(2):
                    transpose_rows(res, tile, half)
            xt_ready()
            project_split("mla_w_in", 0)
            pe.wait_ge(gains_landed, 128)
            transposes([gain_rows])
            for b in range(1, 5):
                project_split("mla_w_in", b)
            for tile in range(TILES):
                pe.wait_ge(latents_normed, tile + 1)
                for half in range(2):
                    transpose_rows(wide, tile, half)
            xt_ready()

            def staged_heads(n, width):
                return [stage[:, n % 4, width * i:width * i + width] for i in range(4)]

            for n in range(8 + LAG):
                if n < 8:
                    project(("mla_w_uq", n // TILES, n % TILES))
                if n >= LAG:
                    pe.wait_ge(heads_roped, n - LAG + 1)
                    transposes(staged_heads(n - LAG, QKD))
            for n in range(8 + LAG):
                if n < 8:
                    project(("mla_w_ukv", n // TILES, n % TILES))
                if n >= LAG:
                    m = n - LAG
                    pe.wait_ge(proj_in_sbuf, JOB["mla_w_ukv", m // TILES, m % TILES] + 1)
                    transposes(staged_heads(m, QKD))
            xt_ready()
            pe.wait_ge(proj_in_sbuf, JOB["mla_w_ukv", 3, 1] + 1)
            pe.wait_ge(masks_cast, 1)

            def scores_a(h, tile, keys):
                return q_a[0:QKD, h, tile * P:tile * P + P], k_a[0:QKD, h, 0:keys]

            def values_ab(h, k):
                return val[:, k, HD * h:HD * h + HD]

            def mixed_transposed(before, tile):
                for half in range(2):
                    pe.wait_ge(mixed_ready, before + 2 * half + tile + 1)
                    transpose_rows(wide, tile, half)

            def output_projection(name, transposed):
                def both_pieces(job):
                    for piece in range(2):
                        project_piece(job, piece)

                take = both_pieces if name == "moba_w_o" else project
                xt_ready()
                take((name, 0, 0))
                transposed(1)
                take((name, 1, 0))
                xt_ready()
                for b in range(2):
                    take((name, b, 1))

            attention("a", UNITS_A, 3, scores_a, values_ab, lambda: mixed_transposed(0, 0))
            output_projection("mla_w_o", lambda tile: mixed_transposed(0, tile))

            for tile in range(TILES):
                pe.wait_ge(res_ready, tile + 1)
                for half in range(2):
                    transpose_rows(res, tile, half)
                xt_ready()
                for piece in range(2):
                    project_piece(("moba_w_kv", 0, tile), piece)

            def heads_back(n, roped):
                pe.wait_ge(heads_roped, roped + n + 1)
                transposes(staged_heads(n, P))

            for name, roped in (("moba_w_kv", 8), ("moba_w_in", 12)):
                for b in range(1 if name == "moba_w_kv" else 0, 4):
                    project_split(name, b)
                    for n in (2 * b - 2, 2 * b - 1) if b in (1, 2) else ():
                        heads_back(n, roped)
            xt_ready()
            pe.wait_ge(proj_in_sbuf, JOB["moba_w_in", 3, 1] + 1)

            def scores_b(h, tile, keys):
                at = slice(HD * (h % 2), HD * (h % 2) + HD)
                return q_b[at, h // 2, tile * P:tile * P + P], k_b[at, h // 2, 0:keys]

            attention("b", UNITS_B, 3, scores_b, values_ab, lambda: mixed_transposed(4, 0))
            output_projection("moba_w_o", lambda tile: mixed_transposed(4, tile))

            for tile in range(TILES):
                pe.wait_ge(normed_ready, tile + 1)
                for half in range(2):
                    transpose_rows(wide, tile, half)
                xt_ready()
                for b in range(2):
                    project(("w_in_2", b, tile))
            for tile in range(TILES):
                pe.wait_ge(proj_in_sbuf, JOB["w_in_2", 0, tile] + 1)
                transposes([z_in[:, tile, :]])
            xt_ready()
            pe.wait_ge(up_landed, 64)
            for tile in range(TILES):
                nc.tensor.matmul(out_bank[tile][:], z_t[0:33, tile * P:tile * P + P], up_w, start=True,
                                 stop=True).then_inc(decay_in_psum, 1)
            project(("w_in_2", 2, 0))
            project(("w_in_2", 2, 1))

            def cumulate(n):
                tile, way = n // 2, n % 2
                if n < 2:
                    pe.wait_ge(decay_ready, n + 1)
                if n == 2:
                    pe.wait_ge(cum_exp, 2)
                name = "fwd" if way == 0 else "bwd"
                for pair in range(2):
                    nc.tensor.matmul(score_bank[n % 2][:, 256 * pair:256 * pair + 256],
                                     decay[:, tile, GW * way + P * pair:GW * way + P * pair + P],
                                     const("cum_" + name), start=True, stop=True)
                nc.tensor.matmul(out_bank[n % 2][:, 0:GW], const("rest_" + name),
                                 decay[:, tile, GW * way:GW * way + GW], start=True, stop=True).then_inc(
                    cum_in_psum, 1)

            cumulate(0)
            cumulate(1)
            for tile in range(TILES):
                pe.wait_ge(proj_in_sbuf, JOB["w_in_2", 2, tile] + 1)
                transposes([gla_qk[:, tile, P * c:P * c + P] for c in range(4)])
            project(("w_in_2", 3, 0))
            cumulate(2)
            cumulate(3)
            project(("w_in_2", 3, 1))
            for tile in range(TILES):
                pe.wait_ge(gqa_ready, tile + 1)
                transposes([att_q[:, tile, P * c:P * c + P] for c in range(4)])
            for tile in range(TILES):
                transposes([key2[:, tile, P * c:P * c + P] for c in range(KVH)])

            def chunk_sums(n):
                way, step = KV_ORDER[n]
                chunk = step if way == 0 else NCHUNK - 1 - step
                tile, rows = chunk // 2, slice(CHUNK * (chunk % 2), CHUNK * (chunk % 2) + CHUNK)
                if n == 0:
                    pe.wait_ge(gla_operands, 4)
                    pe.wait_ge(proj_in_sbuf, JOB["w_in_2", 3, 1] + 1)
                if n >= 2:
                    pe.wait_ge(state_ready, n)
                for pair in range(2):
                    last = nc.tensor.matmul(score_bank[chunk % 2][:, 256 * pair:256 * pair + 256],
                                            k_out[rows, tile, way, P * pair:P * pair + P],
                                            val[rows, tile, 256 * pair:256 * pair + 256], start=True, stop=True)
                last.then_inc(kv_in_psum, 1)

            def chunk_scores(j):
                tile, way, odd = j // 4, j // 2 % 2, j % 2
                at = slice(tile * P, tile * P + P)
                rows = slice(GDK * odd, GDK * odd + GDK)
                if j == 0:
                    pe.wait_ge(state_ready, len(KV_ORDER))
                    xt_ready()
                if j >= 4:
                    pe.wait_ge(gla_masked, j - 3)
                for pair in range(2):
                    last = nc.tensor.matmul(intra_bank[2 * way + odd][:, P * pair:P * pair + P], exp_k[rows, way, pair, at],
                                            exp_q[rows, way, pair, at], start=True, stop=True)
                last.then_inc(gla_scores, 1)

            project(("w_in_2", 4, 0), {c: (lambda n=n: (chunk_sums(n), chunk_sums(n + 1)))
                                       for c, n in ((1, 0), (4, 2), (7, 4))})
            project(("w_in_2", 4, 1), {c: (lambda j=j: (chunk_scores(j), chunk_scores(j + 1)))
                                       for c, j in ((3, 0), (6, 2))})
            for tile in range(TILES):
                if tile:
                    for j in range(4, 8):
                        chunk_scores(j)
                if tile:
                    pe.wait_ge(gla_summed, tile)
                for h in range(GH):
                    pair, odd = h // 2, h % 2
                    rows = slice(GDK * odd, GDK * odd + GDK)
                    for j in range(2):
                        chunk = 2 * tile + j
                        ways = [(0, chunk - 1)] * (chunk > 0) + [(1, NCHUNK - 2 - chunk)] * (chunk < NCHUNK - 1)
                        for k, (way, step) in enumerate(ways):
                            last = nc.tensor.matmul(
                                out_bank[odd][CHUNK * j:CHUNK * j + CHUNK, GDV * pair:GDV * pair + GDV],
                                q_in[rows, way, pair, CHUNK * chunk:CHUNK * chunk + CHUNK],
                                state_of(way, step)[rows, pair, GDV * odd:GDV * odd + GDV],
                                start=(k == 0), stop=(k == len(ways) - 1))
                last.then_inc(gla_inter, 1)
                pe.wait_ge(gla_masked, 4 * tile + 4)
                pe.wait_ge(proj_in_sbuf, JOB["w_in_2", 4, tile] + 1)
                for h in range(GH):
                    for way in range(2):
                        last = nc.tensor.matmul(proj_bank[tile][:, GDV * h:GDV * h + GDV],
                                                masked[:, way, P * h:P * h + P],
                                                val[:, tile, GDV * h:GDV * h + GDV],
                                                start=(way == 0), stop=(way == 1))
                last.then_inc(gla_intra, 1)

            def scores_g(h, tile, keys):
                if tile == 0 and h == 2:
                    pe.wait_ge(gla_copied, 2)
                if tile == 0 and h == 4:
                    pe.wait_ge(gla_summed, 2)
                at = slice(HD * (h % 2), HD * (h % 2) + HD)
                return q_g[at, h // 2, tile * P:tile * P + P], k_g[at, h // (QH // KVH), 0:keys]

            def mixed_g_transposed(tile):
                pe.wait_ge(mixed_ready, 8 + tile + 1)
                pe.wait_ge(gla_gated, tile + 1)
                for half in range(2):
                    transpose_rows(wide, tile, half)

            attention("g", UNITS_G, 3, scores_g,
                      lambda h, k: att_kv[:, k, 128 + HD * (h // (QH // KVH)):128 + HD * (h // (QH // KVH)) + HD],
                      lambda: mixed_g_transposed(0))
            output_projection("w_out_2", mixed_g_transposed)

            pe.wait_ge(row_landed, 64)
            for tile in range(TILES):
                pe.wait_ge(routed_ready, tile + 1)
                for half in range(2):
                    transpose_rows(wide, tile, half)
                xt_ready()
                for c in range(KD):
                    last = nc.tensor.matmul(proj_bank[0][:, 72 * tile:72 * tile + 72], xt[:, c, tile * P:tile * P + P],
                                            router_w[:, c, :], start=(c == 0), stop=(c == KD - 1))
            last.then_inc(logits_in_psum, 1)
            pe.wait_ge(mask_ready, 3)
            mask = tmp[:, 0, 768:768 + 2 * NE]
            for n, (first, second) in enumerate((("tri", None), ("ones", "tri"), ("ones", "ones"))):
                dst = proj_bank[1][:, NE * n:NE * n + NE]
                last = nc.tensor.matmul(dst, const(first), mask[:, 0:NE], start=True, stop=second is None)
                if second:
                    last = nc.tensor.matmul(dst, const(second), mask[:, NE:2 * NE], start=False, stop=True)
            last.then_inc(ranks_in_psum, 1)

            def expert_round(n, first=False):
                pe.wait_ge(onehot_ready, 3 * n + 2)
                for c in range(KD):
                    for tile in range(TILES):
                        last = nc.tensor.matmul(bank[c // 4][:, P * (c % 4):P * (c % 4) + P],
                                                routed[:, tile, c, :], onehot[:, tile, :], start=(tile == 0),
                                                stop=(tile == TILES - 1))
                    if c % 4 == 3:
                        last.then_inc(picked_in_psum, 1)
                pe.wait_ge(onehot_ready, 3 * n + 3)
                for tile in range(TILES):
                    last = nc.tensor.transpose(bank[3][:, P * tile:P * tile + P], weighted[:, tile, :], ident)
                last.then_inc(back_in_psum, 1)
                pe.wait_ge(picked_ready, 2 * n + 2)
                for i in range(GROUP):
                    x = GROUP * n + i
                    gate_up = ring[:, 3 - 3 * (i % 2):5 - 3 * (i % 2), :]
                    if first and i < 2:
                        gate_up = extra if i else ring[:, 0:2, :]
                    pe.wait_ge(gate_up_landed[i % 2], 64 * n + (32 * (i // 2) + 32))
                    both = gate_up.rearrange("p m (c f) -> p m c f", c=KD)
                    for c in range(KD):
                        for j in range(4):
                            last = nc.tensor.matmul(bank[2][SLOTS * j:SLOTS * j + SLOTS, 0:256],
                                                    picked[:, c, SLOTS * i:SLOTS * i + SLOTS],
                                                    both[:, :, c, P * j:P * j + P], start=(c == 0),
                                                    stop=(c == KD - 1))
                    last.then_inc(hidden_in_psum, 1)
                    pe.wait_ge(hidden_ready, x + 1)
                    nc.tensor.transpose(bank[3][:, 256:384], hidden, ident).then_inc(hidden_t_in_psum, 1)
                    pe.wait_ge(hidden_t_ready, x + 1)
                    pe.wait_ge(down_landed[i % 2], 32 * n + (16 * (i // 2) + 16))
                    if i:
                        pe.wait_ge(down_drained_act, x)
                        pe.wait_ge(down_drained_dve, x)
                    down = early_down if first and i == 2 else ring[:, 2 + 3 * (i % 2), :]
                    down = down.rearrange("p (k d) -> p k d", k=4)
                    for k in range(4):
                        for j in range(4):
                            last = nc.tensor.matmul(bank[4][SLOTS * j:SLOTS * j + SLOTS, 0:256],
                                                    hidden_t[:, SLOTS * k:SLOTS * k + SLOTS],
                                                    down[:, k, 256 * j:256 * j + 256], start=(k == 0),
                                                    stop=(k == 3))
                    last.then_inc(down_in_psum, 1)
                pe.wait_ge(back_ready, n + 1)
                pe.wait_ge(down_drained_act, GROUP * n + GROUP)
                pe.wait_ge(down_drained_dve, GROUP * n + GROUP)
                for k in range(4):
                    tile, half = k // 2, k % 2
                    if k == 3:
                        pe.wait_ge(sum_added, 4 * n + 1)
                    nc.tensor.matmul(bank[5 + k % 3][:], back[:, P * tile:P * tile + P],
                                     expert_out[:, 512 * half:512 * half + 512], start=True,
                                     stop=True).then_inc(sum_in_psum, 1)

            expert_round(0, first=True)
            with pe.Fori(1, ROUNDS) as r:
                expert_round(r)
            most = pe.value_load(largest[0:1, 0:1], min_val=0, max_val=SEQ)
            with pe.If(most > SLOTS):
                with pe.Fori(1, PASSES) as p:
                    with pe.Fori(0, ROUNDS) as r:
                        expert_round(ROUNDS * p + r)


def kernel(**inputs):
    import concourse.bacc as bacc
    from concourse.bass_utils import run_bass_kernel_spmd as run

    nc = bacc.Bacc("TRN2", target_bir_lowering=False, num_devices=1,
                   dynamic_dma_scratch_size=1024)
    arrays = {name: np.ascontiguousarray(a) for name, a in inputs.items()}
    arrays["consts"] = np.concatenate(list(shape_constants().values()), axis=1)
    t = {name: nc.dram_tensor(f"in_{name}", a.shape, F32, kind="ExternalInput").ap() for name, a in arrays.items()}
    t["out"] = nc.dram_tensor("out_0", inputs["x"].shape, F32, kind="ExternalOutput").ap()
    build(nc, t)
    r = run(nc, [{f"in_{name}": a for name, a in arrays.items()}], core_ids=[0])
    return r.results[0]["out_0"]
```
